# Optimizing a Trainium2 kernel written in Bass

```python
import jax
import jax.numpy as jnp
from jax import lax
import numpy as np

D_MODEL = 1024
BATCH = 1
SEQ = 512
DEPTH = 1

MIX_WIDTH = D_MODEL
MOBA_HEADS = 4
MOBA_WIDTH = MIX_WIDTH // 4
MOBA_DH = MOBA_WIDTH // MOBA_HEADS
MOBA_BLOCK = 256
MOBA_TOPK = 3
MOBA_Q_CHUNK = 16
MLSTM_HEADS = 4
MLSTM_WIDTH = MIX_WIDTH // 2
MLSTM_DV = MLSTM_WIDTH // MLSTM_HEADS
MLSTM_DQK = MLSTM_DV // 2
MLSTM_CHUNK = 64
MLSTM_CONV = 4
NSA_HEADS = 4
NSA_WIDTH = MIX_WIDTH - MOBA_WIDTH - MLSTM_WIDTH
NSA_DH = NSA_WIDTH // NSA_HEADS
NSA_CMP_LEN = 32
NSA_CMP_STRIDE = 16
NSA_CMP_HIDDEN = 256
NSA_SEL_BLOCK = 64
NSA_TOPN = 8
NSA_WINDOW = 512
NSA_Q_CHUNK = 64
D_FF = 4 * D_MODEL
NORM_EPS = 1e-6
NEG_INF = -1e30

IN_SPLITS = (
    MOBA_WIDTH, MOBA_WIDTH, MOBA_WIDTH,
    MLSTM_HEADS * MLSTM_DQK, MLSTM_HEADS * MLSTM_DQK,
    MLSTM_WIDTH, MLSTM_WIDTH,
    MLSTM_HEADS, MLSTM_HEADS,
    NSA_WIDTH,
    NSA_DH, NSA_DH, NSA_DH, NSA_DH, NSA_DH, NSA_DH,
    3 * NSA_HEADS,
)
D_IN = sum(IN_SPLITS)

kernel_name = 'hybrid_moba_mlstm_nsa_trunk'

def _rms_norm(x, g):
    xf = x.astype(jnp.float32)
    y = xf * lax.rsqrt(jnp.mean(xf * xf, axis=-1, keepdims=True) + NORM_EPS)
    return (y * g.astype(jnp.float32)).astype(x.dtype)

def _head_norm(y, g):
    b, s, h, dh = y.shape
    return _rms_norm(y, g.reshape(h, dh)).reshape(b, s, h * dh)

def _causal_conv(x, w, bias):
    k, c = w.shape
    y = lax.conv_general_dilated(x, w[:, None, :].astype(x.dtype), window_strides=(1,),
                                 padding=[(k - 1, 0)], dimension_numbers=('NWC', 'WIO', 'NWC'),
                                 feature_group_count=c)
    return y + bias.astype(x.dtype)

def _moba_attention(q, k, v):
    b, h, s, dh = q.shape
    n_blk = -(-s // MOBA_BLOCK)
    s_pad = n_blk * MOBA_BLOCK
    pad = ((0, 0), (0, 0), (0, s_pad - s), (0, 0))
    q, k, v = jnp.pad(q, pad), jnp.pad(k, pad), jnp.pad(v, pad)
    k_blk = k.reshape(b * h, n_blk, MOBA_BLOCK, dh)
    v_blk = v.reshape(b * h, n_blk, MOBA_BLOCK, dh)
    k_mean = jnp.mean(k_blk.astype(jnp.float32), axis=2).reshape(b, h, n_blk, dh)
    n_top = min(MOBA_TOPK, n_blk - 1)
    cq = MOBA_Q_CHUNK
    n_chunks = s_pad // cq
    q_chunks = jnp.moveaxis(q.reshape(b, h, n_chunks, cq, dh), 2, 0)
    scale = dh ** -0.5
    bh_ids = jnp.arange(b * h)[:, None]
    blk_ids = jnp.arange(n_blk)

    def one_chunk(args):
        c, qb = args
        q0 = c * cq
        q_pos = q0 + jnp.arange(cq)
        cur = q0 // MOBA_BLOCK
        k_own = lax.dynamic_slice_in_dim(k, cur * MOBA_BLOCK, MOBA_BLOCK, axis=2)
        v_own = lax.dynamic_slice_in_dim(v, cur * MOBA_BLOCK, MOBA_BLOCK, axis=2)
        k_pos = cur * MOBA_BLOCK + jnp.arange(MOBA_BLOCK)
        s_own = jnp.einsum('bhqd,bhkd->bhqk', qb, k_own).astype(jnp.float32) * scale
        s_own = jnp.where(k_pos[None, :] <= q_pos[:, None], s_own, NEG_INF)
        if n_top == 0:
            p_own = jax.nn.softmax(s_own, axis=-1).astype(v.dtype)
            return jnp.einsum('bhqk,bhkd->bhqd', p_own, v_own)
        gate = jnp.einsum('bhqd,bhnd->bhqn', qb.astype(jnp.float32), k_mean)
        gate = jnp.where(blk_ids < cur, gate, -jnp.inf)
        g_val, g_idx = lax.top_k(gate, n_top)
        flat_idx = g_idx.reshape(b * h, cq * n_top)
        k_sel = k_blk[bh_ids, flat_idx].reshape(b, h, cq, n_top, MOBA_BLOCK, dh)
        v_sel = v_blk[bh_ids, flat_idx].reshape(b, h, cq, n_top, MOBA_BLOCK, dh)
        s_sel = jnp.einsum('bhqd,bhqjkd->bhqjk', qb, k_sel).astype(jnp.float32) * scale
        s_sel = jnp.where((g_val > -jnp.inf)[..., None], s_sel, NEG_INF)
        scores = jnp.concatenate([s_sel.reshape(b, h, cq, n_top * MOBA_BLOCK), s_own], axis=-1)
        p = jax.nn.softmax(scores, axis=-1).astype(v.dtype)
        p_sel = p[..., : n_top * MOBA_BLOCK].reshape(b, h, cq, n_top, MOBA_BLOCK)
        p_own = p[..., n_top * MOBA_BLOCK:]
        return (jnp.einsum('bhqjk,bhqjkd->bhqd', p_sel, v_sel)
                + jnp.einsum('bhqk,bhkd->bhqd', p_own, v_own))

    out = lax.map(one_chunk, (jnp.arange(n_chunks), q_chunks))
    return jnp.moveaxis(out, 0, 2).reshape(b, h, s_pad, dh)[:, :, :s]

def _mlstm_chunkwise(q, k, v, i_pre, f_pre):
    b, s, h, dk = q.shape
    dv = v.shape[-1]
    L = MLSTM_CHUNK
    nc = s // L
    f32 = jnp.float32

    def chunks(t):
        t = jnp.moveaxis(t.astype(f32), 2, 1)
        return t.reshape((b, h, nc, L) + t.shape[3:])

    q = chunks(q)
    k = chunks(k) * (dk ** -0.5)
    v = chunks(v)
    ig = chunks(i_pre)
    logf = jax.nn.log_sigmoid(chunks(f_pre))
    bcum = jnp.cumsum(logf, axis=-1)
    b_end = bcum[..., -1]
    w_end = b_end[..., None] - bcum + ig
    a_end = jnp.max(w_end, axis=-1)
    e_end = jnp.exp(w_end - a_end[..., None])
    c_chunk = jnp.einsum('bhcs,bhcsv,bhcsk->bhcvk', e_end, v, k)
    n_chunk = jnp.einsum('bhcs,bhcsk->bhck', e_end, k)

    def step(carry, xs):
        c_st, n_st, m_st = carry
        be, ac, cc, nn = xs
        m_new = jnp.maximum(be + m_st, ac)
        decay = jnp.exp(be + m_st - m_new)
        inj = jnp.exp(ac - m_new)
        c_new = decay[..., None, None] * c_st + inj[..., None, None] * cc
        n_new = decay[..., None] * n_st + inj[..., None] * nn
        return (c_new, n_new, m_new), (c_st, n_st, m_st)

    init = (jnp.zeros((b, h, dv, dk), f32), jnp.zeros((b, h, dk), f32), jnp.zeros((b, h), f32))
    xs = (jnp.moveaxis(b_end, 2, 0), jnp.moveaxis(a_end, 2, 0),
          jnp.moveaxis(c_chunk, 2, 0), jnp.moveaxis(n_chunk, 2, 0))
    _, (c_prev, n_prev, m_prev) = lax.scan(step, init, xs)
    c_prev = jnp.moveaxis(c_prev, 0, 2)
    n_prev = jnp.moveaxis(n_prev, 0, 2)
    m_prev = jnp.moveaxis(m_prev, 0, 2)

    causal = jnp.tril(jnp.ones((L, L), dtype=bool))
    d_log = jnp.where(causal, bcum[..., :, None] - bcum[..., None, :] + ig[..., None, :], -jnp.inf)
    m_inter = bcum + m_prev[..., None]
    m_t = jnp.maximum(m_inter, jnp.max(d_log, axis=-1))
    s_intra = jnp.einsum('bhctd,bhcsd->bhcts', q, k) * jnp.exp(d_log - m_t[..., None])
    w_inter = jnp.exp(m_inter - m_t)
    num = (jnp.einsum('bhcts,bhcsv->bhctv', s_intra, v)
           + jnp.einsum('bhctd,bhcvd->bhctv', q, c_prev) * w_inter[..., None])
    den = s_intra.sum(axis=-1) + jnp.einsum('bhctd,bhcd->bhct', q, n_prev) * w_inter
    hid = num / jnp.maximum(jnp.abs(den), jnp.exp(-m_t))[..., None]
    return jnp.moveaxis(hid.reshape(b, h, s, dv), 1, 2)

def _nsa_attention(q, kc, vc, ksl, vsl, kwn, vwn, gate_pre, cmp_pe, cmp_w1, cmp_w2):
    b, h, s, dh = q.shape
    f32 = jnp.float32
    scale = dh ** -0.5
    t_pos = jnp.arange(s)

    n_cmp = (s - NSA_CMP_LEN) // NSA_CMP_STRIDE + 1
    cmp_idx = jnp.arange(n_cmp)[:, None] * NSA_CMP_STRIDE + jnp.arange(NSA_CMP_LEN)[None, :]

    def compress(t, j):
        blk = t[:, cmp_idx] + cmp_pe[j]
        blk = blk.reshape(b, n_cmp, NSA_CMP_LEN * dh)
        return jax.nn.gelu(blk @ cmp_w1[j]) @ cmp_w2[j]

    k_cmp = compress(kc, 0)
    v_cmp = compress(vc, 1)
    cmp_end = jnp.arange(n_cmp) * NSA_CMP_STRIDE + NSA_CMP_LEN - 1
    vis = cmp_end[None, :] <= t_pos[:, None]
    s_cmp = jnp.einsum('bhtd,bnd->bhtn', q, k_cmp).astype(f32) * scale
    p_cmp = jnp.where(vis, jax.nn.softmax(jnp.where(vis, s_cmp, NEG_INF), axis=-1), 0.0)
    o_cmp = jnp.einsum('bhtn,bnd->bhtd', p_cmp.astype(v_cmp.dtype), v_cmp)

    n_sel = s // NSA_SEL_BLOCK
    lo = np.arange(n_cmp)[:, None] * NSA_CMP_STRIDE
    sl = np.arange(n_sel)[None, :] * NSA_SEL_BLOCK
    overlap = np.maximum(np.minimum(lo + NSA_CMP_LEN, sl + NSA_SEL_BLOCK) - np.maximum(lo, sl), 0) / NSA_CMP_LEN
    p_slc = jnp.einsum('btn,nj->btj', p_cmp.sum(axis=1), jnp.asarray(overlap, dtype=f32))
    blk_ids = jnp.arange(n_sel)[None, :]
    cur = (t_pos // NSA_SEL_BLOCK)[:, None]
    forced = (blk_ids == 0) | (blk_ids == cur) | (blk_ids == cur - 1)
    score = jnp.where(blk_ids > cur, -jnp.inf, jnp.where(forced, jnp.inf, p_slc))
    top = min(NSA_TOPN, n_sel)
    s_val, s_idx = lax.top_k(score, top)
    s_valid = s_val > -jnp.inf

    cq = NSA_Q_CHUNK
    n_ch = s // cq
    k_sel_blk = ksl.reshape(b, n_sel, NSA_SEL_BLOCK, dh)
    v_sel_blk = vsl.reshape(b, n_sel, NSA_SEL_BLOCK, dh)
    win_pad = ((0, 0), (NSA_WINDOW, 0), (0, 0))
    k_win_pad = jnp.pad(kwn, win_pad)
    v_win_pad = jnp.pad(vwn, win_pad)
    b_ids = jnp.arange(b)[:, None]
    q_c = jnp.moveaxis(q.reshape(b, h, n_ch, cq, dh), 2, 0)
    idx_c = jnp.moveaxis(s_idx.reshape(b, n_ch, cq, top), 1, 0)
    val_c = jnp.moveaxis(s_valid.reshape(b, n_ch, cq, top), 1, 0)

    def one_chunk(args):
        c, qb, idx, valid = args
        q0 = c * cq
        q_pos = q0 + jnp.arange(cq)
        flat_idx = idx.reshape(b, cq * top)
        k_sel = k_sel_blk[b_ids, flat_idx].reshape(b, cq, top, NSA_SEL_BLOCK, dh)
        v_sel = v_sel_blk[b_ids, flat_idx].reshape(b, cq, top, NSA_SEL_BLOCK, dh)
        k_pos = idx[..., None] * NSA_SEL_BLOCK + jnp.arange(NSA_SEL_BLOCK)
        m_sel = valid[..., None] & (k_pos <= q_pos[None, :, None, None])
        s_sel = jnp.einsum('bhqd,bqjkd->bhqjk', qb, k_sel).astype(f32) * scale
        s_sel = jnp.where(m_sel[:, None], s_sel, NEG_INF).reshape(b, h, cq, top * NSA_SEL_BLOCK)
        p_sel = jax.nn.softmax(s_sel, axis=-1).astype(v_sel.dtype).reshape(b, h, cq, top, NSA_SEL_BLOCK)
        o_sel = jnp.einsum('bhqjk,bqjkd->bhqd', p_sel, v_sel)
        k_win = lax.dynamic_slice_in_dim(k_win_pad, q0, NSA_WINDOW + cq, axis=1)
        v_win = lax.dynamic_slice_in_dim(v_win_pad, q0, NSA_WINDOW + cq, axis=1)
        w_pos = q0 - NSA_WINDOW + jnp.arange(NSA_WINDOW + cq)
        rel = q_pos[:, None] - w_pos[None, :]
        m_win = (w_pos[None, :] >= 0) & (rel >= 0) & (rel < NSA_WINDOW)
        s_win = jnp.einsum('bhqd,bkd->bhqk', qb, k_win).astype(f32) * scale
        p_win = jax.nn.softmax(jnp.where(m_win, s_win, NEG_INF), axis=-1).astype(v_win.dtype)
        o_win = jnp.einsum('bhqk,bkd->bhqd', p_win, v_win)
        return o_sel, o_win

    o_sel, o_win = lax.map(one_chunk, (jnp.arange(n_ch), q_c, idx_c, val_c))
    o_sel = jnp.moveaxis(o_sel, 0, 2).reshape(b, h, s, dh)
    o_win = jnp.moveaxis(o_win, 0, 2).reshape(b, h, s, dh)
    g = jax.nn.sigmoid(gate_pre.astype(f32)).transpose(0, 2, 1, 3)
    out = g[..., 0:1] * o_cmp + g[..., 1:2] * o_sel + g[..., 2:3] * o_win
    return out.astype(q.dtype).transpose(0, 2, 1, 3)

def _hybrid_layer(x, norm_g, w_in, conv_w, conv_b, gate_b, cmp_pe, cmp_w1, cmp_w2, head_g, w_out, w1, w2):
    b, s, _ = x.shape
    hin = _rms_norm(x, norm_g[0])
    z = hin @ w_in
    split_points = [int(p) for p in np.cumsum(IN_SPLITS)[:-1]]
    (mq, mk, mv, lq, lk, lv, lo, li, lf,
     nq, kc, vc, ksl, vsl, kwn, vwn, ng) = jnp.split(z, split_points, axis=-1)

    def heads(t, n):
        return t.reshape(b, s, n, -1).transpose(0, 2, 1, 3)

    y_moba = _moba_attention(heads(mq, MOBA_HEADS), heads(mk, MOBA_HEADS), heads(mv, MOBA_HEADS))
    y_moba = y_moba.transpose(0, 2, 1, 3)
    qk = jax.nn.silu(_causal_conv(jnp.concatenate([lq, lk], axis=-1), conv_w, conv_b))
    lq, lk = jnp.split(qk, 2, axis=-1)
    y_ml = _mlstm_chunkwise(lq.reshape(b, s, MLSTM_HEADS, MLSTM_DQK), lk.reshape(b, s, MLSTM_HEADS, MLSTM_DQK),
                            lv.reshape(b, s, MLSTM_HEADS, MLSTM_DV), li + gate_b[0], lf + gate_b[1]).astype(x.dtype)
    y_nsa = _nsa_attention(heads(nq, NSA_HEADS), kc, vc, ksl, vsl, kwn, vwn,
                           ng.reshape(b, s, NSA_HEADS, 3), cmp_pe, cmp_w1, cmp_w2)
    g_moba, g_ml, g_nsa = jnp.split(head_g, [MOBA_WIDTH, MOBA_WIDTH + MLSTM_WIDTH])
    y = jnp.concatenate([_head_norm(y_moba, g_moba),
                         _head_norm(y_ml, g_ml) * jax.nn.sigmoid(lo),
                         _head_norm(y_nsa, g_nsa)], axis=-1)
    x = x + _rms_norm(y @ w_out, norm_g[1])
    hm = _rms_norm(x, norm_g[2])
    y = jnp.square(jax.nn.relu(hm @ w1)) @ w2
    return x + _rms_norm(y, norm_g[3])

def setup_inputs(seed: int = 0) -> dict:
    key = jax.random.key(seed)
    ks = jax.random.split(key, 14)
    f32 = jnp.float32

    def normal(k, shape, scale):
        return jax.random.normal(k, shape, f32) * scale

    qk_width = 2 * MLSTM_HEADS * MLSTM_DQK
    i_bias = normal(ks[5], (DEPTH, MLSTM_HEADS), 0.1)
    f_bias = jnp.linspace(3.0, 6.0, MLSTM_HEADS, dtype=f32)[None, :] + normal(ks[6], (DEPTH, MLSTM_HEADS), 0.1)
    return {
        'x': normal(ks[0], (BATCH, SEQ, D_MODEL), 1.0),
        'norm_g': 1.0 + normal(ks[1], (DEPTH, 4, D_MODEL), 0.02),
        'w_in': normal(ks[2], (DEPTH, D_MODEL, D_IN), D_MODEL ** -0.5),
        'mlstm_conv_w': normal(ks[3], (DEPTH, MLSTM_CONV, qk_width), MLSTM_CONV ** -0.5),
        'mlstm_conv_b': normal(ks[4], (DEPTH, qk_width), 0.02),
        'mlstm_gate_b': jnp.stack([i_bias, f_bias], axis=1),
        'nsa_cmp_pe': normal(ks[7], (DEPTH, 2, NSA_CMP_LEN, NSA_DH), 0.02),
        'nsa_cmp_w1': normal(ks[8], (DEPTH, 2, NSA_CMP_LEN * NSA_DH, NSA_CMP_HIDDEN), (NSA_CMP_LEN * NSA_DH) ** -0.5),
        'nsa_cmp_w2': normal(ks[9], (DEPTH, 2, NSA_CMP_HIDDEN, NSA_DH), NSA_CMP_HIDDEN ** -0.5),
        'head_g': 1.0 + normal(ks[10], (DEPTH, MIX_WIDTH), 0.02),
        'w_out': normal(ks[11], (DEPTH, MIX_WIDTH, D_MODEL), MIX_WIDTH ** -0.5),
        'w_mlp1': normal(ks[12], (DEPTH, D_MODEL, D_FF), D_MODEL ** -0.5),
        'w_mlp2': normal(ks[13], (DEPTH, D_FF, D_MODEL), D_FF ** -0.5),
    }

def reference(x, norm_g, w_in, mlstm_conv_w, mlstm_conv_b, mlstm_gate_b, nsa_cmp_pe, nsa_cmp_w1,
              nsa_cmp_w2, head_g, w_out, w_mlp1, w_mlp2):
    for layer in range(DEPTH):
        x = _hybrid_layer(x, norm_g[layer], w_in[layer], mlstm_conv_w[layer], mlstm_conv_b[layer],
                          mlstm_gate_b[layer], nsa_cmp_pe[layer], nsa_cmp_w1[layer], nsa_cmp_w2[layer],
                          head_g[layer], w_out[layer], w_mlp1[layer], w_mlp2[layer])
    return x


_drawn_inputs = setup_inputs


def setup_inputs(seed=0):
    import zlib

    import numpy as np

    out = dict(_drawn_inputs(seed))
    spreads = {}
    factors = {'mlstm_conv_b': 7.032, 'nsa_cmp_pe': 5.116, 'head_g': 3.844}
    for name, (base, spread) in spreads.items():
        noise = np.random.default_rng([zlib.crc32(name.encode()), seed]).standard_normal(out[name].shape)
        drawn = base * np.exp(spread * noise) if base else spread * noise
        out[name] = jnp.asarray(drawn.astype(out[name].dtype))
    for name, factor in factors.items():
        out[name] = (out[name] * factor).astype(out[name].dtype)
    return out
```

```python
from contextlib import ExitStack

import concourse.bass as bass
from concourse import mybir

ALU = mybir.AluOpType
ACT = mybir.ActivationFunctionType
AX = mybir.AxisListType
F32 = mybir.dt.float32
F32R = mybir.dt.float32r
BF16 = mybir.dt.bfloat16
I32 = mybir.dt.int32

P = 128
SEQ = 512
D = 1024
NT = SEQ // P
NC = D // P
DH = 64
DV = 128
HEADS = 4
FF = 4 * D
EPS = 1e-6
NEG = -1e30
CMP_STRIDE, CMP_LEN, CMP_HID = 16, 32, 256
NCMP = (SEQ - CMP_LEN) // CMP_STRIDE + 1
NP_ = NCMP + 1

MQ, MK, MV, LQ, LK, LV, LO, LI, LF, NQ, KC, VC, KSL, VSL, KWN, VWN, NG, DIN = (
    0, 256, 512, 768, 1024, 1280, 1792, 2304, 2308, 2312, 2568, 2632, 2696, 2760, 2824, 2888, 2952, 2964)
BV, BS, BW, BG, BI, BF, BN = 0, 256, 320, 384, 396, 400, 404

CHUNK = 2048
RAW = 2

C_B, C_LQ, C_LK, C_LO, C_KVS, C_NQ, C_LV, C_MQ, C_MK, C_CMP, C_WO, C_MLP = 0, 2, 3, 4, 6, 7, 8, 10, 11, 12, 16, 20
FB = 8
NB = FF // P // FB
PER_BLOCK = FB // 2 + FB // 2
NCHUNK = C_MLP + NB * PER_BLOCK

J_B, J_CONV, J_LO, J_LI, J_LF, J_KV, J_KS, J_NQ, J_GC, J_LV, J_MQ, J_MK, J_MB, J_H = (
    0, 4, 8, 12, 13, 14, 15, 16, 18, 19, 23, 25, 27, 31)
NJOB = 33
READER = "vvvv" "vvvv" "aaaa" "v" "v" "v" "a" "aa" "a" "vvvv" "aa" "vv" "aaaa" "vv"

K_ORDER = [2, 3, 4, 5, 6, 7, 0, 1]
UNITS = [(br, p, i) for br in ("sel", "win") for p in range(2) for i in range(NT)] + \
        [("moba", p, i) for i in reversed(range(NT)) for p in range(2)]
N_NSA = 16
ML_UNITS = [(p, i) for p in range(2) for i in range(NT)]
WO_BANK = [0, 6, 2, 4]
YT_BANK = [4, 5, 6, 7, 2, 3, 4, 5]
SETS = [(0, 1, 6, 7), (2, 3, 4, 5)]


def ring_slot(c):
    return c % 3 if c < C_WO + 3 else [1, 2, 0, 3][(c - C_WO) % 4]


def ring_previous(c):
    return c - 3 if c < C_WO + 3 else c - 4


def build(nc, x, norm_g, w_in, conv_w, conv_b, gate_b, cmp_pe, cmp_w1, cmp_w2, head_g, w_out, w1, w2, out):
    ctx = ExitStack()
    with ctx:
        base = (nc.sbuf_base + 63) // 64 * 64
        cursor = [base]

        def at(name, shape, dt, offset):
            return nc.alloc_sbuf_tensor_at(name, shape, dt, offset=offset)

        def put(name, shape, dt):
            size = 2 if dt == BF16 else 4
            for d in shape[1:]:
                size *= d
            size = (size + 63) // 64 * 64
            cursor[0] += size
            return at(name, shape, dt, cursor[0] - size)

        raw = [put(f"raw{r}", [P, CHUNK], F32) for r in range(RAW)]
        ring_h = [put(f"ring_h{r}", [P, CHUNK], F32R) for r in range(3)]
        ring_l = [put(f"ring_l{r}", [P, CHUNK], F32R) for r in range(3)]
        o_xt = cursor[0]
        xT_h = put("xT_h", [P, NC, SEQ], F32R)
        xT_l = put("xT_l", [P, NC, SEQ], F32R)
        W = at("W", [P, HEADS, NT, NT, P], F32, o_xt)
        xres = put("xres", [P, NT, D], F32)
        gain_a = put("gain_a", [P, D], F32)
        ident = put("ident", [P, P], F32)
        identb = put("identb", [P, P], BF16)
        mask_s = put("mask_s", [P, P], BF16)
        mask_c = put("mask_c", [P, NT, 2, NP_], BF16)
        vis = put("vis", [P, NT, NP_], F32)
        rows = put("rows", [28, P], F32)
        cols = put("cols", [P, 28], F32)
        pe_rows = put("pe_rows", [CMP_LEN, P], F32)
        gb = put("gb", [HEADS, 2], F32)
        w2k = put("w2k", [P, 2, 2, DH], F32)
        w2v = put("w2v", [P, 2, DH], F32)
        peT = put("peT", [P, CMP_LEN], F32)
        junkb = put("junkb", [P, DV], F32)
        wide = put("wide", [P, 48], F32)
        zero1 = put("zero1", [P, 1], F32)
        stat = put("stat", [P, 256], F32)
        gt = put("gt", [P, NT, 12], F32)
        gcol = put("gcol", [P, NT, HEADS], F32)
        emc = put("emc", [P, NT, HEADS], F32)
        kcT = put("kcT", [P, NP_], F32)
        gel = put("gel", [P, 2, 2 * NP_], F32)
        gelr = put("gelr", [P, 2, HEADS, NP_], F32)
        o_cg = cursor[0]
        cg = put("cg", [P, 4, 2, 2 * NP_], F32)
        sel = at("sel", [HEADS, HEADS, P], F32, o_cg)

        o_a = cursor[0]
        lv1 = at("lv1", [P, NT, HEADS, DV + 1], F32, o_a)
        qkT = at("qkT", [P, 4, SEQ], F32, o_a + 8320)
        ring_h.append(at("ring_h3", [P, CHUNK], F32R, o_a))
        ring_l.append(at("ring_l3", [P, CHUNK], F32R, o_a + 8320))
        y = at("y", [P, NT, D], F32, o_a + 16512)
        o_m = o_a + 32896
        mqT = at("mqT", [P, 2, SEQ], F32, o_m)
        mkT = at("mkT", [P, 2, SEQ], F32, o_m + 4096)
        nqT = at("nqT", [P, 2, SEQ], F32, o_m + 8192)
        gain_b = at("gain_b", [P, D], F32, o_m + 8192)
        kselT = at("kselT", [P, SEQ], F32, o_m + 12288)
        kwinT = at("kwinT", [P, SEQ], F32, o_m + 14336)
        zB = at("zB", [P, NT, BN], F32, o_m + 16384)
        hid = at("hid", [P, NT, HEADS, DV], F32, o_m + 22848)
        blk_h = at("blk_h", [P, CMP_LEN, 2, NP_], F32R, o_m + 22848)
        o_p = o_m + 31040
        probs = at("probs", [P, 3, SEQ], F32, o_p)
        probsT = at("probsT", [P, 3, SEQ], F32, o_p + 6144)
        blk_l = at("blk_l", [P, CMP_LEN, 2, NP_], F32R, o_p)
        sig = at("sig", [P, 2, SEQ], F32, o_p)
        junk = at("junk", [P, D], F32, o_p + 8192)
        o_r = o_p + 12288
        g_row = at("g_row", [HEADS, 3, SEQ], F32, o_r)
        junk_w = at("junk_w", [P, D], F32, o_m)
        cexp = at("cexp", [P, NT, 4, NP_], F32, o_r)
        cexpT = at("cexpT", [P, NT, P], F32, o_r + 2048)
        vbd = at("vbd", [P, HEADS * DH], F32, o_r + 4096)
        hT_h = at("hT_h", [P, FB, SEQ], F32R, o_m)
        hT_l = at("hT_l", [P, FB, SEQ], F32R, o_m + 16384)
        ow = at("ow", [P, 2, D], F32, o_m + 32768)
        relu = at("relu", [P, 2, SEQ], F32, o_m + 40960)
        sq = at("sq", [P, 2, SEQ], F32, o_m + 45056)
        assert o_r + 6144 <= nc.sbuf_usable_end and o_m + 49152 <= nc.sbuf_usable_end, (o_r + 6144, nc.sbuf_usable_end)

        ps = ctx.enter_context(nc.psum_tensor("ps", [P, 8, 512], F32))

        SS_X, SS_ML, SS_NSA, SS_MB, SS_O, SS_X1, SS_Y = 0, 4, 20, 36, 52, 56, 60
        R_X, R_ML, R_NSA, R_MB, R_O, R_X1, R_Y = 68, 72, 88, 104, 120, 124, 128
        NMAX, RSUM, WK = 132, 180, 228
        head_norm = {"ml": (SS_ML, R_ML), "nsa": (SS_NSA, R_NSA), "moba": (SS_MB, R_MB)}

        def sem(name):
            return ctx.enter_context(nc.semaphore(name))

        x_in = [sem(f"x_in{t}") for t in range(NT)]
        small_in = sem("small_in")
        gain0_in = sem("gain0_in")
        gain1_in, gain2_in, gain3_in = sem("gain1_in"), sem("gain2_in"), sem("gain3_in")
        raw_in = [sem(f"raw_in{r}") for r in range(RAW)]
        dup_in = sem("dup_in")
        stored = sem("stored")
        consts = sem("consts")
        hi_done, lo_done = sem("hi_done"), sem("lo_done")
        part_used = sem("part_used")
        x_sq, hn_ready, xt_done, xh_ready, xl_ready = (sem(n) for n in
                                                      ("x_sq", "hn_ready", "xt_done", "xh_ready", "xl_ready"))
        params_t = sem("params_t")
        params_ready = sem("params_ready")
        job_done = sem("job_done")
        read_v, read_a = sem("read_v"), sem("read_a")
        chain = sem("chain")
        conv_lin, conv_acc, conv_sig = sem("conv_lin"), sem("conv_acc"), sem("conv_sig")
        silu_done, w_step = sem("silu_done"), sem("w_step")
        blkh_ready = sem("blkh_ready")
        ks_ready = sem("ks_ready")
        gates_ready = sem("gates_ready")
        lf_step, lf_ready = sem("lf_step"), sem("lf_ready")
        rows_ready = sem("rows_ready")
        gcol_ready = sem("gcol_ready")
        w_exp, w_ready = sem("w_exp"), sem("w_ready")
        gelu_arg, gelu_exp, gelu_ready = sem("gelu_arg"), sem("gelu_exp"), sem("gelu_ready")
        kv_cmp, kc_ready, vc_ready = sem("kv_cmp"), sem("kc_ready"), sem("vc_ready")
        cs_done, cs_sub, cs_exp, cs_ready = sem("cs_done"), sem("cs_sub"), sem("cs_exp"), sem("cs_ready")
        ct_done, ct_ready, co_done, co_used = sem("ct_done"), sem("ct_ready"), sem("co_done"), sem("co_used")
        ml_s, ml_p, ml_o, ml_used, ml_ss = sem("ml_s"), sem("ml_p"), sem("ml_o"), sem("ml_used"), sem("ml_ss")
        ml_rn, nsa_rn, ml_y, nsa_y, moba_y = (sem(n) for n in ("ml_rn", "nsa_rn", "ml_y", "nsa_y", "moba_y"))
        s_done, mx_done, p_ready = sem("s_done"), sem("mx_done"), sem("p_ready")
        t_done, pt_v, pt_a = sem("t_done"), sem("pt_v"), sem("pt_a")
        o_done, o_used, y_ss = sem("o_done"), sem("o_used"), sem("y_ss")
        yt_done, yh_ready, yl_ready = sem("yt_done"), sem("yh_ready"), sem("yl_ready")
        wo_done, o_sq, x1_ready, x1_sq, hm_ready = (sem(n) for n in ("wo_done", "o_sq", "x1_ready", "x1_sq", "hm_ready"))
        hmt_done, hmh_ready, hml_ready = sem("hmt_done"), sem("hmh_ready"), sem("hml_ready")
        up_done, relu_ready, sq_ready, hh_ready, hl_ready = (sem(n) for n in (
            "up_done", "relu_ready", "sq_ready", "hh_ready", "hl_ready"))
        down_done, acc_ready, y_sq, res_ready = sem("down_done"), sem("acc_ready"), sem("y_sq"), sem("res_ready")

        def reads(n):
            return (read_v if READER[n] == "v" else read_a), READER[:n + 1].count(READER[n])

        def released(c):
            inside = [C_B, C_LO, C_LV, C_CMP, C_CMP + 1, C_CMP + 2, C_WO, C_WO + 1]
            if c in inside:
                return part_used, inside.index(c) + 1
            if c < C_WO:
                return job_done, {C_B + 1: J_B + 4, C_LQ: J_CONV + 2, C_LK: J_CONV + 4, C_LO + 1: J_LO + 4,
                                  C_KVS: J_KS + 1, C_NQ: J_NQ + 2, C_LV + 1: J_LV + 4, C_MQ: J_MQ + 2,
                                  C_MK: J_MK + 2, C_CMP + 3: NJOB}[c]
            if c < C_MLP:
                return wo_done, {C_WO + 2: 7, C_WO + 3: 8}[c]
            b, k = divmod(c - C_MLP, PER_BLOCK)
            if k < FB // 2:
                return up_done, FB * b + 2 * (k + 1)
            half, q = divmod(k - FB // 2, 2)
            if q == 0:
                return part_used, len(inside) + 2 * b + half + 1
            return down_done, 8 * b + 4 * (half + 1)

        def chunk_parts(c):
            def kn(lo, n, k0=0, kn_=NC):
                return w_in[0, k0 * P:(k0 + kn_) * P, lo:lo + n].rearrange("(k p) n -> p k n", p=P)
            if c in (C_B, C_B + 1):
                k0 = 4 * (c - C_B)
                return BN, [((0, 256), kn(MV, 256, k0, 4)), ((BS, 64), kn(VSL, 64, k0, 4)),
                            ((BW, 76), kn(VWN, 76, k0, 4)), ((BI, 8), kn(LI, 8, k0, 4))]
            if c in (C_LO, C_LO + 1):
                return 512, [((0, 512), kn(LO, 512, 4 * (c - C_LO), 4))]
            if c in (C_LV, C_LV + 1):
                return 512, [((0, 512), kn(LV, 512, 4 * (c - C_LV), 4))]
            if c == C_KVS:
                return 256, [((0, 192), kn(KC, 192)), ((192, 64), kn(KWN, 64))]
            if c < C_CMP:
                return 256, [((0, 256), kn({C_LQ: LQ, C_LK: LK, C_NQ: NQ, C_MQ: MQ, C_MK: MK}[c], 256))]
            if c < C_WO:
                l0 = 8 * (c - C_CMP)
                return 256, [((0, 256), cmp_w1[0, j, l0 * DH:(l0 + 8) * DH, :].rearrange("(l d) h -> d l h", d=DH))
                             for j in range(2)]
            if c < C_MLP:
                kset, half = divmod(c - C_WO, 2)
                ks = K_ORDER[4 * kset:4 * kset + 4]
                runs = [(ks[0], 4)] if kset == 0 else [(ks[0], 2), (ks[2], 2)]
                return 512, [((0, 512), w_out[0, k0 * P:(k0 + n) * P, 512 * half:512 * half + 512]
                              .rearrange("(k p) n -> p k n", p=P)) for k0, n in runs]
            b, k = divmod(c - C_MLP, PER_BLOCK)
            if k < FB // 2:
                f0 = (FB * b + 2 * k) * P
                return 256, [((0, 256), w1[0, :, f0:f0 + 256].rearrange("(k p) n -> p k n", p=P))]
            half, q = divmod(k - FB // 2, 2)
            f0 = (FB * b + 4 * q) * P
            return 512, [((0, 512), w2[0, f0:f0 + 512, 512 * half:512 * half + 512]
                          .rearrange("(k p) n -> p k n", p=P))]

        def size(c):
            n = chunk_parts(c)[0]
            return n * (4 if n > 256 else 8)

        def grid(t, c):
            n = chunk_parts(c)[0]
            return t[:, 0:size(c)].rearrange("p (k n) -> p k n", n=n)

        block = ctx.enter_context(nc.Block())

        @block.sync
        def _(sp):
            def load_chunk(c):
                if c >= RAW:
                    sp.wait_ge(lo_done, c - RAW + 1)
                view = grid(raw[c % RAW], c)
                parts = chunk_parts(c)[1]
                k0 = 0
                for j, ((n0, n), src) in enumerate(parts):
                    if C_CMP <= c < C_WO:
                        dst = view[DH * j:DH * j + DH, :, :]
                    elif C_WO <= c < C_MLP:
                        kk = src.shape[1]
                        dst = view[:, k0:k0 + kk, :]
                        k0 += kk
                    else:
                        dst = view[:, :, n0:n0 + n]
                    sp.dma_start(dst, src).then_inc(raw_in[c % RAW], 16)

            for t in range(NT):
                sp.dma_start(xres[:, t, :], x[0, t * P:(t + 1) * P, :]).then_inc(x_in[t], 16)
                if t == 1:
                    load_chunk(0)
            for c in range(1, NCHUNK):
                if c == C_WO:
                    sp.wait_ge(hn_ready, NT)
                    sp.dma_start(gain_a[:], norm_g[0, 1:2, :].to_broadcast([P, D])).then_inc(gain1_in, 16)
                if c == C_MLP:
                    sp.wait_ge(s_done, 2 * N_NSA)
                    sp.dma_start(gain_b[:], norm_g[0, 2:3, :].to_broadcast([P, D])).then_inc(gain2_in, 16)
                if c == C_MLP + PER_BLOCK:
                    sp.wait_ge(x1_ready, NT)
                    sp.dma_start(gain_a[:], norm_g[0, 3:4, :].to_broadcast([P, D])).then_inc(gain3_in, 16)
                load_chunk(c)
            for t in range(NT):
                sp.wait_ge(res_ready, t + 1)
                sp.dma_start(out[0, t * P:(t + 1) * P, :], xres[:, t, :]).then_inc(stored, 16)
            sp.wait_ge(stored, 16 * NT)

        def raw_full(c):
            return 16 * sum(len(chunk_parts(k)[1]) for k in range(c % RAW, c + 1, RAW))

        @block.gpsimd
        def _(pool):
            nc.gpsimd.memset(ident[:], 0.0).then_inc(consts, 1)
            nc.gpsimd.memset(identb[:], 0.0).then_inc(consts, 1)
            nc.gpsimd.memset(mask_s[:], 0.0).then_inc(consts, 1)
            nc.gpsimd.memset(mask_c[:], 0.0).then_inc(consts, 1)
            nc.gpsimd.memset(vis[:], 1.0).then_inc(consts, 1)
            nc.gpsimd.memset(sel[:], 0.0).then_inc(consts, 1)
            nc.gpsimd.memset(zero1[:], 0.0).then_inc(consts, 1)
            pool.wait_ge(consts, 7)
            nc.gpsimd.affine_select(out=ident[:], in_=ident[:], compare_op=ALU.not_equal, fill=1.0, base=0,
                                    pattern=[[-1, P]], channel_multiplier=1).then_inc(consts, 1)
            nc.gpsimd.affine_select(out=identb[:], in_=identb[:], compare_op=ALU.not_equal, fill=1.0, base=0,
                                    pattern=[[-1, P]], channel_multiplier=1).then_inc(consts, 1)
            nc.gpsimd.affine_select(out=mask_s[:], in_=mask_s[:], compare_op=ALU.is_ge, fill=NEG, base=0,
                                    pattern=[[-1, P]], channel_multiplier=1).then_inc(consts, 1)
            nc.gpsimd.affine_select(out=mask_c[:], in_=mask_c[:], compare_op=ALU.is_ge, fill=NEG,
                                    base=1 - CMP_LEN, pattern=[[P, NT], [0, 2], [-CMP_STRIDE, NP_]],
                                    channel_multiplier=1).then_inc(consts, 1)
            nc.gpsimd.affine_select(out=vis[:], in_=vis[:], compare_op=ALU.is_ge, fill=0.0,
                                    base=1 - CMP_LEN, pattern=[[P, NT], [-CMP_STRIDE, NP_]],
                                    channel_multiplier=1).then_inc(consts, 1)
            nc.gpsimd.affine_select(out=sel[:], in_=sel[:], compare_op=ALU.not_equal, fill=1.0, base=0,
                                    pattern=[[-1, HEADS], [0, P]], channel_multiplier=1).then_inc(consts, 1)

            def low_half(c):
                pool.wait_ge(hi_done, c + 1)
                n, r = size(c), ring_slot(c)
                nc.gpsimd.tensor_tensor(ring_l[r][:, 0:n], raw[c % RAW][:, 0:n], ring_h[r][:, 0:n].bitcast(F32),
                                        ALU.subtract).then_inc(lo_done, 1)

            for c in range(C_WO):
                low_half(c)
            for h in range(HEADS):
                pool.wait_ge(w_exp, h + 1)
                for i in range(NT):
                    last = nc.gpsimd.affine_select(out=W[:, h, i, i, :], in_=W[:, h, i, i, :], compare_op=ALU.is_ge,
                                                   fill=0.0, base=0, pattern=[[1, P]], channel_multiplier=-1)
                last.then_inc(w_ready, 1)
            low_half(C_WO)
            low_half(C_WO + 1)
            pool.wait_ge(ml_rn, 1)
            rn = stat[:, R_ML:R_ML + 16].rearrange("p (t h o) -> p t h o", h=HEADS, o=1).to_broadcast([P, NT, HEADS, DV])
            nc.gpsimd.tensor_tensor(hid[:], hid[:], rn, ALU.mult).then_inc(ml_y, 1)
            pool.wait_ge(ml_y, 1)
            yml = y[:, :, 256:768].rearrange("p t (h d) -> p t h d", h=HEADS)
            nc.gpsimd.tensor_tensor(yml, yml, hid[:], ALU.mult).then_inc(ml_y, 1)
            low_half(C_WO + 2)
            low_half(C_WO + 3)
            pool.wait_ge(nsa_rn, 1)
            rn = stat[:, R_NSA:R_NSA + 16].rearrange("p (t h o) -> p t h o", h=HEADS, o=1).to_broadcast([P, NT, HEADS, DH])
            yn = y[:, :, 768:1024].rearrange("p t (h d) -> p t h d", h=HEADS)
            nc.gpsimd.tensor_tensor(yn, yn, rn, ALU.mult).then_inc(nsa_y, 1)
            for c in range(C_MLP, NCHUNK):
                low_half(c)

        @block.scalar
        def _(act):
            act.dma_start(rows[0:16, :], conv_w[0].rearrange("k (c p) -> (k c) p", p=P)).then_inc(small_in, 16)
            act.dma_start(rows[16:20, :], conv_b[0].rearrange("(c p) -> c p", p=P)).then_inc(small_in, 16)
            act.dma_start(rows[20:28, :], head_g[0].rearrange("(c p) -> c p", p=P)).then_inc(small_in, 16)
            act.dma_start(gain_a[:], norm_g[0, 0:1, :].to_broadcast([P, D])).then_inc(gain0_in, 16)
            act.dma_start(pe_rows[:].rearrange("l (j d) -> l j d", j=2), cmp_pe[0].rearrange("j l d -> l j d")).then_inc(small_in, 16)
            with nc.allow_non_contiguous_dma(reason="eight gate biases"):
                act.dma_start(gb[:], gate_b[0].rearrange("j h -> h j")).then_inc(small_in, 16)
            for s in range(2):
                act.dma_start(w2k[:, :, s, :], cmp_w2[0, 0].rearrange("(t p) d -> p t d", p=P)).then_inc(small_in, 16)
            act.dma_start(w2v[:], cmp_w2[0, 1].rearrange("(t p) d -> p t d", p=P)).then_inc(small_in, 16)
            N_SMALL = 16 * 8

            def high_half(c):
                act.wait_ge(raw_in[c % RAW], raw_full(c))
                if c == C_WO + 3:
                    act.wait_ge(ml_o, len(ML_UNITS))
                elif c >= 3:
                    act.wait_ge(*released(ring_previous(c)))
                n, r = size(c), ring_slot(c)
                nc.scalar.activation(ring_h[r][:, 0:n], raw[c % RAW][:, 0:n], ACT.Copy).then_inc(hi_done, 1)

            for t in range(NT):
                act.wait_ge(x_in[t], 16)
                if t:
                    act.wait_ge(x_sq, t)
                nc.scalar.activation(junk[:], xres[:, t, :], ACT.Square,
                                     accum_out=stat[:, SS_X + t:SS_X + t + 1]).then_inc(x_sq, 1)
            high_half(0)
            for t in range(NT):
                act.wait_ge(xt_done, t + 1)
                for b in range(2):
                    nc.scalar.activation(xT_h[:, 4 * b:4 * b + 4, t * P:(t + 1) * P],
                                         ps[:, 2 * t + b, :].rearrange("p (c q) -> p c q", c=4),
                                         ACT.Copy).then_inc(xh_ready, 1)
                if t % 2 == 1:
                    high_half(1 + t // 2)
            high_half(3)

            def conv_linear(n):
                act.wait_ge(job_done, J_CONV + n + 1)
                if n == 0:
                    act.wait_ge(params_ready, 1)
                nc.scalar.activation(qkT[:, n, :], ps[:, (J_CONV + n) % 8, :], ACT.Identity,
                                     scale=cols[:, 12 + n:13 + n], bias=cols[:, 16 + n:17 + n]).then_inc(conv_lin, 1)

            def conv_sigmoid(n):
                act.wait_ge(conv_acc, n + 1)
                nc.scalar.activation(sig[:, n % 2, :], qkT[:, n, :], ACT.Sigmoid).then_inc(conv_sig, 1)

            for n in range(4):
                conv_linear(n)
                if n >= 1:
                    conv_sigmoid(n - 1)
                if n == 1:
                    high_half(4)
            conv_sigmoid(3)
            high_half(5)
            act.wait_ge(read_v, J_B + NT)
            nc.scalar.activation(gt[:], zB[:, :, BG:BG + 12], ACT.Sigmoid).then_inc(gates_ready, 1)
            for t in range(NT):
                act.wait_ge(job_done, J_LO + t + 1)
                nc.scalar.activation(y[:, t, 256:768], ps[:, (J_LO + t) % 8, :], ACT.Sigmoid).then_inc(read_a, 1)
                if t == 1:
                    high_half(6)
            high_half(7)
            act.wait_ge(job_done, J_LF + 1)
            nc.scalar.activation(g_row[:, 0, :], ps[0:HEADS, J_LF % 8, :], ACT.Abs, bias=gb[:, 1:2]).then_inc(lf_step, 1)
            act.wait_ge(lf_step, 1)
            nc.scalar.activation(g_row[:, 0, :], g_row[:, 0, :], ACT.Exp, scale=-1.0).then_inc(lf_step, 1)
            act.wait_ge(lf_step, 2)
            nc.scalar.activation(g_row[:, 0, :], g_row[:, 0, :], ACT.Ln, bias=1.0).then_inc(lf_ready, 1)
            act.wait_ge(job_done, J_KV + 1)
            for j in range(2):
                for a in range(2):
                    src = ps[DH * j:DH * j + DH, J_KV % 8, :].rearrange("p (n b) -> p b n", b=16)[:, :, a:a + NCMP]
                    nc.scalar.activation(blk_h[DH * j:DH * j + DH, 16 * a:16 * a + 16, j, 0:NCMP], src,
                                         ACT.Copy).then_inc(blkh_ready, 1)
                act.wait_ge(params_ready, 2)
                nc.scalar.activation(blk_h[DH * j:DH * j + DH, :, j, NCMP], peT[DH * j:DH * j + DH, :],
                                     ACT.Copy).then_inc(blkh_ready, 1)
            act.wait_ge(job_done, J_KS + 1)
            nc.scalar.activation(kselT[0:DH, :], ps[0:DH, J_KS % 8, :], ACT.Copy).then_inc(ks_ready, 1)
            nc.scalar.activation(kwinT[DH:P, :], ps[DH:P, J_KS % 8, :], ACT.Copy).then_inc(read_a, 1)
            act.wait_ge(ks_ready, 1)
            act.dma_start(kselT[DH:P, :], kselT[0:DH, :]).then_inc(dup_in, 16)
            act.wait_ge(read_a, reads(J_KS)[1])
            act.dma_start(kwinT[0:DH, :], kwinT[DH:P, :]).then_inc(dup_in, 16)
            high_half(8)
            high_half(9)
            for p in range(2):
                act.wait_ge(job_done, J_NQ + p + 1)
                nc.scalar.activation(nqT[:, p, :], ps[:, (J_NQ + p) % 8, :], ACT.Copy, scale=DH ** -0.5).then_inc(read_a, 1)
            act.wait_ge(job_done, J_GC + 1)
            nc.scalar.activation(gcol[:].rearrange("p t h -> p (t h)"), ps[:, J_GC % 8, 0:16], ACT.Copy).then_inc(gcol_ready, 1)
            nc.scalar.activation(emc[:].rearrange("p t h -> p (t h)"), ps[:, J_GC % 8, 16:32], ACT.Exp,
                                 scale=-1.0).then_inc(read_a, 1)
            high_half(10)
            high_half(11)
            high_half(12)
            for p in range(2):
                act.wait_ge(job_done, J_MQ + p + 1)
                nc.scalar.activation(mqT[:, p, :], ps[:, (J_MQ + p) % 8, :], ACT.Copy, scale=DH ** -0.5).then_inc(read_a, 1)
            high_half(13)
            high_half(14)
            act.wait_ge(gcol_ready, 1)
            for h in range(HEADS):
                act.wait_ge(job_done, J_MB + h + 1)
                for j in range(NT):
                    last = nc.scalar.activation(W[:, h, j:NT, j, :],
                                                ps[:, (J_MB + h) % 8, j * P:SEQ].rearrange("p (i t) -> p i t", t=P),
                                                ACT.Exp, scale=-1.0, bias=gcol[:, j, h:h + 1])
                    if j < NT - 1:
                        last.then_inc(w_step, 1)
                    else:
                        last.then_inc(read_a, 1)
                act.wait_ge(read_a, reads(J_MB + h)[1])
                nc.scalar.activation(zero1[:], zero1[:], ACT.Copy).then_inc(w_exp, 1)
                if h == 1:
                    high_half(15)
            high_half(C_WO)
            high_half(C_WO + 1)

            def ml_squares(u):
                p, i = ML_UNITS[u]
                act.wait_ge(ml_used, u + 1)
                for m in range(2):
                    h = 2 * p + m
                    c = SS_ML + HEADS * i + h
                    if 2 * u + m:
                        act.wait_ge(ml_ss, 2 * u + m)
                    nc.scalar.activation(junkb[:, 0:DV], hid[:, i, h, :], ACT.Square,
                                         accum_out=stat[:, c:c + 1]).then_inc(ml_ss, 1)

            for u in range(len(ML_UNITS)):
                if u == 1:
                    act.wait_ge(gelu_arg, 1)
                    nc.scalar.activation(cg[:, 3], cg[:, 2], ACT.Exp, scale=-1.5957691216057308).then_inc(gelu_exp, 1)
                if u == 2:
                    act.wait_ge(kv_cmp, 1)
                    nc.scalar.activation(kcT[:], ps[:, 4, 0:NP_], ACT.Copy).then_inc(kc_ready, 1)
                if u == 4:
                    act.wait_ge(cs_sub, 1)
                    nc.scalar.activation(cexp[:], cexp[:], ACT.Exp).then_inc(cs_exp, 1)
                if u == 7:
                    act.wait_ge(ct_done, 1)
                    nc.scalar.activation(cexpT[:].rearrange("p t q -> p (t q)"), ps[:, 4, :], ACT.Copy).then_inc(ct_ready, 1)
                if u >= 1:
                    ml_squares(u - 1)
            ml_squares(len(ML_UNITS) - 1)
            high_half(C_WO + 2)
            high_half(C_WO + 3)

            def exps(u):
                for m in range(2):
                    s = 2 * u + m
                    w = (UNITS[u][2] + 1) * P
                    act.wait_ge(mx_done, s + 1)
                    if s >= 3:
                        act.wait_ge(t_done, s - 2)
                    nc.scalar.activation(probs[:, s % 3, 0:w], ps[:, 2 * (u % 2) + m, 0:w], ACT.Exp,
                                         bias=stat[:, NMAX + s:NMAX + s + 1],
                                         accum_out=stat[:, RSUM + s:RSUM + s + 1]).then_inc(p_ready, 1)

            def copy_t(u):
                s = 2 * u + 1
                w = (UNITS[u][2] + 1) * P
                act.wait_ge(t_done, s + 1)
                if s >= 3:
                    act.wait_ge(o_done, (s - 3) // 2 + 1)
                nc.scalar.activation(probsT[:, s % 3, 0:w], ps[:, 5, 0:w], ACT.Copy).then_inc(pt_a, 1)

            squared = [0]

            def y_squares(u):
                br, p, i = UNITS[u]
                if br == "sel":
                    return
                act.wait_ge(o_used, u + 1)
                for m in range(2):
                    h = 2 * p + m
                    y0 = (0 if br == "moba" else 768) + DH * h
                    c = (SS_MB if br == "moba" else SS_NSA) + HEADS * i + h
                    if squared[0]:
                        act.wait_ge(y_ss, squared[0])
                    else:
                        act.wait_ge(ml_ss, 16)
                    squared[0] += 1
                    nc.scalar.activation(junkb[:, 0:DH], y[:, i, y0:y0 + DH], ACT.Square,
                                         accum_out=stat[:, c:c + 1]).then_inc(y_ss, 1)

            def y_high(k):
                c = K_ORDER[k]
                act.wait_ge(yt_done, k + 1)
                nc.scalar.activation(xT_h[:, c, :], ps[:, YT_BANK[k], :], ACT.Copy,
                                     scale=cols[:, 20 + c:21 + c]).then_inc(yh_ready, 1)

            NU = len(UNITS)
            exps(0)
            for u in range(NU):
                if u == N_NSA:
                    for k in range(4):
                        y_high(k)
                copy_t(u)
                if u + 1 < NU:
                    exps(u + 1)
                if u >= 2:
                    y_squares(u - 2)
            y_squares(NU - 2)
            y_squares(NU - 1)
            for k in range(4, 8):
                y_high(k)

            def hm_high(t):
                act.wait_ge(hmt_done, t + 1)
                for b in range(2):
                    nc.scalar.activation(xT_h[:, 4 * b:4 * b + 4, t * P:(t + 1) * P],
                                         ps[:, WO_BANK[t] + b, :].rearrange("p (c q) -> p c q", c=4),
                                         ACT.Copy).then_inc(hmh_ready, 1)

            for t in range(NT):
                act.wait_ge(wo_done, 2 * t + 2)
                if t:
                    act.wait_ge(x1_sq, t)
                nc.scalar.activation(junk_w[:], ps[:, WO_BANK[t]:WO_BANK[t] + 2, :].rearrange("p b n -> p (b n)"), ACT.Square,
                                     accum_out=stat[:, SS_O + t:SS_O + t + 1]).then_inc(o_sq, 1)
                act.wait_ge(x1_ready, t + 1)
                nc.scalar.activation(junk_w[:], xres[:, t, :], ACT.Square,
                                     accum_out=stat[:, SS_X1 + t:SS_X1 + t + 1]).then_inc(x1_sq, 1)
                if t == NT - 1:
                    high_half(C_MLP)
            for t in range(NT):
                hm_high(t)
            high_half(C_MLP + 1)
            high_half(C_MLP + 2)

            c = C_MLP + 3
            for b in range(NB):
                for f in range(FB):
                    n = FB * b + f
                    act.wait_ge(up_done, n + 1)
                    if n >= 2:
                        act.wait_ge(sq_ready, n - 1)
                    nc.scalar.activation(relu[:, n % 2, :], ps[:, SETS[b % 2][f % 4], :], ACT.Relu).then_inc(relu_ready, 1)
                    act.wait_ge(relu_ready, n + 1)
                    nc.scalar.activation(hT_h[:, f, :], relu[:, n % 2, :], ACT.Square).then_inc(hh_ready, 1)
                    if f % 2 == 1 and c < NCHUNK:
                        high_half(c)
                        c += 1
                for q in range(FB // 2):
                    if c < NCHUNK:
                        high_half(c)
                        c += 1
                    if b == NB - 1 and q % 2 == 1:
                        half = q // 2
                        for t in range(NT):
                            act.wait_ge(acc_ready, 8 * b + 4 * half + t + 1)
                            if 4 * half + t:
                                act.wait_ge(y_sq, 4 * half + t)
                            cc = SS_Y + 2 * t + half
                            nc.scalar.activation(relu[:, 0, :], y[:, t, 512 * half:512 * half + 512], ACT.Square,
                                                 accum_out=stat[:, cc:cc + 1]).then_inc(y_sq, 1)

        @block.vector
        def _(dve):
            steps = [0]

            def link(ins):
                steps[0] += 1
                ins.then_inc(chain, 1)
                dve.wait_ge(chain, steps[0])

            def rsqrt(ss, r, n, width):
                v, a, yv = stat[:, WK:WK + n], stat[:, WK + 8:WK + 8 + n], stat[:, r:r + n]
                if n > 8:
                    v, a = wide[:, 0:n], wide[:, 16:16 + n]
                link(nc.vector.tensor_scalar(v, stat[:, ss:ss + n], 1.0 / width, EPS, ALU.mult, ALU.add))
                link(nc.vector.tensor_scalar(yv.bitcast(I32), v.bitcast(I32), -0.5, float(0x5f3759df), ALU.mult, ALU.add))
                link(nc.vector.tensor_scalar(v, v, -0.5, None, ALU.mult))
                for k in range(3):
                    if n == 1:
                        link(nc.vector.scalar_tensor_tensor(a, yv, v, yv, ALU.mult, ALU.mult))
                    else:
                        link(nc.vector.tensor_tensor(a, yv, yv, ALU.mult))
                        link(nc.vector.tensor_tensor(a, a, v, ALU.mult))
                    if k < 2:
                        link(nc.vector.scalar_tensor_tensor(yv, a, 1.5, yv, ALU.add, ALU.mult))
                return nc.vector.scalar_tensor_tensor(yv, a, 1.5, yv, ALU.add, ALU.mult)

            link(nc.vector.memset(blk_h[DH:P, :, 0, :].bitcast(F32), 0.0))
            link(nc.vector.memset(blk_h[0:DH, :, 1, :].bitcast(F32), 0.0))
            link(nc.vector.memset(lv1[:, :, :, DV:DV + 1], 1.0))

            for t in range(NT):
                dve.wait_ge(x_sq, t + 1)
                link(rsqrt(SS_X + t, R_X + t, 1, D))
                if t == 0:
                    dve.wait_ge(gain0_in, 16)
                nc.vector.scalar_tensor_tensor(y[:, t, :], xres[:, t, :], stat[:, R_X + t:R_X + t + 1], gain_a[:],
                                               ALU.mult, ALU.mult).then_inc(hn_ready, 1)
                if t == 1:
                    dve.wait_ge(params_t, 1)
                    nc.vector.tensor_copy(cols[:], ps[:, 7, 0:28]).then_inc(params_ready, 1)
                    nc.vector.tensor_copy(peT[:], ps[:, 7, 64:96]).then_inc(params_ready, 1)
            for t in range(NT):
                for b in range(2):
                    dve.wait_ge(xh_ready, 2 * t + b + 1)
                    nc.vector.tensor_tensor(xT_l[:, 4 * b:4 * b + 4, t * P:(t + 1) * P],
                                            ps[:, 2 * t + b, :].rearrange("p (c q) -> p c q", c=4),
                                            xT_h[:, 4 * b:4 * b + 4, t * P:(t + 1) * P].bitcast(F32),
                                            ALU.subtract).then_inc(xl_ready, 1)

            for t in range(NT):
                dve.wait_ge(job_done, J_B + t + 1)
                nc.vector.tensor_copy(zB[:, t, :], ps[:, (J_B + t) % 8, 0:BN]).then_inc(read_v, 1)

            def silu(n):
                dve.wait_ge(conv_sig, n + 1)
                nc.vector.scalar_tensor_tensor(qkT[:, n, :], qkT[:, n, :], 1.0 if n < 2 else DH ** -0.5,
                                               sig[:, n % 2, :], ALU.mult, ALU.mult).then_inc(silu_done, 1)

            for n in range(4):
                dve.wait_ge(conv_lin, n + 1)
                for back in (1, 2, 3):
                    ins = nc.vector.scalar_tensor_tensor(
                        qkT[:, n, back:SEQ], ps[:, (J_CONV + n) % 8, 0:SEQ - back],
                        cols[:, 4 * (3 - back) + n:4 * (3 - back) + n + 1], qkT[:, n, back:SEQ], ALU.mult, ALU.add)
                    if back < 3:
                        link(ins)
                    else:
                        ins.then_inc(read_v, 1)
                dve.wait_ge(read_v, reads(J_CONV + n)[1])
                nc.vector.tensor_copy(stat[:, WK:WK + 1], stat[:, WK:WK + 1]).then_inc(conv_acc, 1)
                if n >= 1:
                    silu(n - 1)
            silu(3)
            dve.wait_ge(lf_ready, 1)
            link(nc.vector.tensor_scalar(g_row[:, 1, :], ps[0:HEADS, J_LF % 8, :], gb[:, 1:2], 0.0, ALU.add, ALU.min))
            link(nc.vector.tensor_tensor(g_row[:, 1, :], g_row[:, 1, :], g_row[:, 0, :], ALU.subtract))
            link(nc.vector.tensor_tensor_scan(g_row[:, 0, :], g_row[:, 1, :], zero1[0:HEADS, :].to_broadcast([HEADS, SEQ]),
                                              0.0, ALU.add, ALU.add))
            dve.wait_ge(job_done, J_LI + 1)
            nc.vector.scalar_tensor_tensor(g_row[:, 1, :], ps[0:HEADS, J_LI % 8, :], gb[:, 0:1], g_row[:, 0, :],
                                           ALU.add, ALU.subtract).then_inc(read_v, 1)
            dve.wait_ge(read_v, reads(J_LI)[1])
            link(nc.vector.tensor_tensor_scan(g_row[:, 2, :], g_row[:, 1, :], g_row[:, 1, :], 0.0, ALU.max, ALU.max))
            nc.vector.tensor_tensor(g_row[:, 0, :], g_row[:, 0, :], g_row[:, 2, :], ALU.add).then_inc(read_v, 1)
            dve.wait_ge(silu_done, 4)
            link(nc.vector.memset(blk_l[DH:P, :, 0, :].bitcast(F32), 0.0))
            link(nc.vector.memset(blk_l[0:DH, :, 1, :].bitcast(F32), 0.0))
            dve.wait_ge(blkh_ready, 6)
            for j in range(2):
                rs_ = slice(DH * j, DH * j + DH)
                for a in range(2):
                    src = ps[rs_, J_KV % 8, :].rearrange("p (n b) -> p b n", b=16)[:, :, a:a + NCMP]
                    nc.vector.tensor_tensor(blk_l[rs_, 16 * a:16 * a + 16, j, 0:NCMP], src,
                                            blk_h[rs_, 16 * a:16 * a + 16, j, 0:NCMP].bitcast(F32), ALU.subtract)
                last = nc.vector.tensor_tensor(blk_l[rs_, :, j, NCMP], peT[rs_, :], blk_h[rs_, :, j, NCMP].bitcast(F32),
                                               ALU.subtract)
            last.then_inc(read_v, 1)
            for t in range(NT):
                dve.wait_ge(job_done, J_LV + t + 1)
                nc.vector.tensor_copy(lv1[:, t, :, 0:DV], ps[:, (J_LV + t) % 8, :].rearrange("p (h d) -> p h d", h=HEADS)
                                      ).then_inc(read_v, 1)
            for p in range(2):
                dve.wait_ge(job_done, J_MK + p + 1)
                nc.vector.tensor_copy(mkT[:, p, :], ps[:, (J_MK + p) % 8, :]).then_inc(read_v, 1)
            for t in range(2):
                dve.wait_ge(job_done, J_H + t + 1)
                nc.vector.tensor_copy(cg[:, 0, t, :], ps[:, (J_H + t) % 8, 0:2 * NP_]).then_inc(read_v, 1)

            def gelu():
                dve.wait_ge(read_v, READER.count("v"))
                hv = cg[:, 0].rearrange("p t (j n) -> p (t j) n", n=NP_)
                xv = cg[:, 1].rearrange("p t (j n) -> p (t j) n", n=NP_)
                link(nc.vector.tensor_tensor(xv, hv, hv[:, :, NCMP:NP_].to_broadcast([P, 4, NP_]), ALU.add))
                link(nc.vector.tensor_tensor(cg[:, 2], cg[:, 1], cg[:, 1], ALU.mult))
                link(nc.vector.tensor_scalar(cg[:, 2], cg[:, 2], 0.044715, 1.0, ALU.mult, ALU.add))
                nc.vector.tensor_tensor(cg[:, 2], cg[:, 2], cg[:, 1], ALU.mult).then_inc(gelu_arg, 1)
                dve.wait_ge(gelu_exp, 1)
                link(nc.vector.tensor_scalar(cg[:, 3], cg[:, 3], 1.0, None, ALU.add))
                link(nc.vector.reciprocal(cg[:, 3], cg[:, 3]))
                link(nc.vector.tensor_tensor(gel[:], cg[:, 1], cg[:, 3], ALU.mult))
                gv = gel[:].rearrange("p t (j n) -> p t j n", n=NP_)
                link(nc.vector.memset(gv[:, :, :, NCMP:NP_], 0.0))
                for t in range(2):
                    last = nc.vector.tensor_copy(gelr[:, t], gv[:, t, 1:2, :].to_broadcast([P, HEADS, NP_]))
                last.then_inc(gelu_ready, 1)

            def cmp_values():
                link(nc.vector.memset(vbd[:], 0.0))
                dve.wait_ge(kv_cmp, 2)
                for m in range(2):
                    for p in range(2):
                        r, h = 2 * m + p, 2 * p + m
                        last = nc.vector.tensor_copy(vbd[32 * r:32 * r + 32, DH * h:DH * h + DH],
                                                     ps[32 * r:32 * r + 32, 5, 0:DH])
                last.then_inc(vc_ready, 1)

            def cmp_max():
                dve.wait_ge(cs_done, 1)
                for m in range(2):
                    link(nc.vector.tensor_reduce(wide[:, 32 + 8 * m:40 + 8 * m],
                                                 ps[:, 4 + m, 0:8 * NP_].rearrange("p (a n) -> p a n", n=NP_), AX.X, ALU.max))
                for m in range(2):
                    last = nc.vector.tensor_tensor(
                        cexp[:, :, 2 * m:2 * m + 2, :],
                        ps[:, 4 + m, 0:8 * NP_].rearrange("p (i a n) -> p i a n", i=NT, n=NP_),
                        wide[:, 32 + 8 * m:40 + 8 * m].rearrange("p (i a o) -> p i a o", i=NT, o=1).to_broadcast([P, NT, 2, NP_]),
                        ALU.subtract)
                    if m == 0:
                        link(last)
                last.then_inc(cs_sub, 1)

            def cmp_probs():
                dve.wait_ge(cs_exp, 1)
                link(nc.vector.tensor_reduce(wide[:, 32:48], cexp[:].rearrange("p i a n -> p (i a) n"), AX.X, ALU.add))
                link(nc.vector.reciprocal(wide[:, 32:48], wide[:, 32:48]))
                link(nc.vector.tensor_tensor(cexp[:], cexp[:], vis[:].rearrange("p i (o n) -> p i o n", o=1)
                                             .to_broadcast([P, NT, 4, NP_]), ALU.mult))
                cv = cexp[:].rearrange("p i a n -> p (i a) n")
                nc.vector.tensor_tensor(cv, cv, wide[:, 32:48].rearrange("p (a o) -> p a o", o=1).to_broadcast([P, 16, NP_]),
                                        ALU.mult).then_inc(cs_ready, 1)

            def ml_out(u):
                p, i = ML_UNITS[u]
                dve.wait_ge(ml_o, u + 1)
                if u:
                    dve.wait_ge(ml_used, u)
                ob = ps[:, 6 + u % 2, :].rearrange("p (m d) -> p m d", m=2)
                d = stat[:, WK:WK + 2].rearrange("p (m o) -> p m o", o=1)
                den = ob[:, :, DV:DV + 1]
                link(nc.vector.scalar_tensor_tensor(d, den, -1.0, emc[:, i, 2 * p:2 * p + 2].rearrange("p (m o) -> p m o", o=1),
                                                    ALU.mult, ALU.max))
                link(nc.vector.tensor_tensor(d, den, d, ALU.max))
                link(nc.vector.reciprocal(d, d))
                nc.vector.tensor_tensor(hid[:, i, 2 * p:2 * p + 2, :], ob[:, :, 0:DV], d.to_broadcast([P, 2, DV]),
                                        ALU.mult).then_inc(ml_used, 1)

            for u, (p, i) in enumerate(ML_UNITS):
                w = (i + 1) * P
                for m in range(2):
                    s, h = 2 * u + m, 2 * p + m
                    dve.wait_ge(ml_s, u + 1)
                    dve.wait_ge(w_ready, h + 1)
                    if s >= 3:
                        dve.wait_ge(ml_o, (s - 3) // 2 + 1)
                    nc.vector.tensor_tensor(probsT[:, s % 3, 0:w], ps[:, 2 * (u % 2) + m, 0:w],
                                            W[:, h, i, 0:i + 1, :].rearrange("p j t -> p (j t)"), ALU.mult).then_inc(ml_p, 1)
                if u == 1:
                    gelu()
                if u == 2:
                    cmp_values()
                if u == 4:
                    cmp_max()
                if u == 5:
                    cmp_probs()
                if u >= 1:
                    ml_out(u - 1)
            ml_out(len(ML_UNITS) - 1)
            dve.wait_ge(ml_used, len(ML_UNITS))
            for i in range(NT):
                dve.wait_ge(co_done, i // 2 + 1)
                last = nc.vector.tensor_tensor(
                    y[:, i, 768:1024].rearrange("p (h d) -> p h d", h=HEADS),
                    ps[:, 5 - i // 2, 256 * (i % 2):256 * (i % 2) + 256].rearrange("p (h d) -> p h d", h=HEADS),
                    gt[:, i, :].rearrange("p (h b) -> p h b", b=3)[:, :, 0:1].to_broadcast([P, HEADS, DH]), ALU.mult)
            last.then_inc(co_used, 1)

            def maxes(u, m):
                s = 2 * u + m
                w = (UNITS[u][2] + 1) * P
                dve.wait_ge(s_done, s + 1)
                nc.vector.tensor_reduce(stat[:, NMAX + s:NMAX + s + 1], ps[:, 2 * (u % 2) + m, 0:w], AX.X, ALU.max,
                                        negate=True).then_inc(mx_done, 1)

            def copy_t(u):
                s = 2 * u
                w = (UNITS[u][2] + 1) * P
                dve.wait_ge(t_done, s + 1)
                if s >= 3:
                    dve.wait_ge(o_done, (s - 3) // 2 + 1)
                nc.vector.tensor_copy(probsT[:, s % 3, 0:w], ps[:, 4, 0:w]).then_inc(pt_v, 1)

            def attn_out(u):
                br, p, i = UNITS[u]
                dve.wait_ge(p_ready, 2 * u + 2)
                rv = stat[:, WK:WK + 2]
                if u:
                    dve.wait_ge(o_used, u)
                link(nc.vector.reciprocal(rv, stat[:, RSUM + 2 * u:RSUM + 2 * u + 2]))
                ob = ps[:, 6 + u % 2, 0:2 * DH].rearrange("p (m d) -> p m d", m=2)
                if br == "moba":
                    dve.wait_ge(o_done, u + 1)
                    nc.vector.tensor_tensor(y[:, i, P * p:P * p + P].rearrange("p (m d) -> p m d", m=2), ob,
                                            rv.rearrange("p (m o) -> p m o", o=1).to_broadcast([P, 2, DH]),
                                            ALU.mult).then_inc(o_used, 1)
                    return
                g = gt[:, i, :].rearrange("p (h b) -> p h b", b=3)[:, 2 * p:2 * p + 2, 1 if br == "sel" else 2]
                link(nc.vector.tensor_tensor(rv, rv, g, ALU.mult))
                dve.wait_ge(o_done, u + 1)
                for m in range(2):
                    ya = y[:, i, 768 + DH * (2 * p + m):768 + DH * (2 * p + m) + DH]
                    last = nc.vector.scalar_tensor_tensor(ya, ob[:, m, :], rv[:, m:m + 1], ya, ALU.mult, ALU.add)
                last.then_inc(o_used, 1)

            def y_low(k):
                c = K_ORDER[k]
                dve.wait_ge(yh_ready, k + 1)
                nc.vector.scalar_tensor_tensor(xT_l[:, c, :], ps[:, YT_BANK[k], :], cols[:, 20 + c:21 + c],
                                               xT_h[:, c, :].bitcast(F32), ALU.mult, ALU.subtract).then_inc(yl_ready, 1)

            NU = len(UNITS)
            maxes(0, 0)
            maxes(0, 1)
            for u in range(NU):
                if u == N_NSA:
                    attn_out(u - 1)
                    for k in range(4):
                        y_low(k)
                if u + 1 < NU:
                    maxes(u + 1, 0)
                copy_t(u)
                if u + 1 < NU:
                    maxes(u + 1, 1)
                if u >= 1 and u != N_NSA:
                    attn_out(u - 1)
                if u == 2:
                    dve.wait_ge(ml_ss, 16)
                    rsqrt(SS_ML, R_ML, 16, DV).then_inc(ml_rn, 1)
                    dve.wait_ge(ml_rn, 1)
                if u == N_NSA + 2:
                    dve.wait_ge(y_ss, 16)
                    rsqrt(SS_NSA, R_NSA, 16, DH).then_inc(nsa_rn, 1)
                    dve.wait_ge(nsa_rn, 1)
            attn_out(NU - 1)
            dve.wait_ge(y_ss, 32)
            link(rsqrt(SS_MB, R_MB, 16, DH))
            ym = y[:, :, 0:256].rearrange("p t (h d) -> p t h d", h=HEADS)
            nc.vector.tensor_tensor(ym, ym, stat[:, R_MB:R_MB + 16].rearrange("p (t h o) -> p t h o", h=HEADS, o=1)
                                    .to_broadcast([P, NT, HEADS, DH]), ALU.mult).then_inc(moba_y, 1)
            for k in range(4, 8):
                y_low(k)

            def hm_low(t):
                for b in range(2):
                    dve.wait_ge(hmh_ready, 2 * t + b + 1)
                    nc.vector.tensor_tensor(xT_l[:, 4 * b:4 * b + 4, t * P:(t + 1) * P],
                                            ps[:, WO_BANK[t] + b, :].rearrange("p (c q) -> p c q", c=4),
                                            xT_h[:, 4 * b:4 * b + 4, t * P:(t + 1) * P].bitcast(F32),
                                            ALU.subtract).then_inc(hml_ready, 1)

            for t in range(NT):
                dve.wait_ge(o_sq, t + 1)
                link(rsqrt(SS_O + t, R_O + t, 1, D))
                if t == 0:
                    dve.wait_ge(gain1_in, 16)
                    dve.wait_ge(gain2_in, 16)
                if t >= 2:
                    dve.wait_ge(hmt_done, t - 1)
                link(nc.vector.scalar_tensor_tensor(ow[:, t % 2, :], ps[:, WO_BANK[t]:WO_BANK[t] + 2, :].rearrange("p b n -> p (b n)"),
                                                    stat[:, R_O + t:R_O + t + 1], gain_a[:], ALU.mult, ALU.mult))
                nc.vector.tensor_tensor(xres[:, t, :], xres[:, t, :], ow[:, t % 2, :], ALU.add).then_inc(x1_ready, 1)
                dve.wait_ge(x1_sq, t + 1)
                link(rsqrt(SS_X1 + t, R_X1 + t, 1, D))
                nc.vector.scalar_tensor_tensor(ow[:, t % 2, :], xres[:, t, :], stat[:, R_X1 + t:R_X1 + t + 1], gain_b[:],
                                               ALU.mult, ALU.mult).then_inc(hm_ready, 1)
            for t in range(NT):
                hm_low(t)

            for b in range(NB):
                for f in range(FB):
                    n = FB * b + f
                    dve.wait_ge(relu_ready, n + 1)
                    nc.vector.tensor_tensor(sq[:, n % 2, :], relu[:, n % 2, :], relu[:, n % 2, :], ALU.mult).then_inc(sq_ready, 1)
                    dve.wait_ge(sq_ready, n + 1)
                    dve.wait_ge(hh_ready, n + 1)
                    nc.vector.tensor_tensor(hT_l[:, f, :], sq[:, n % 2, :], hT_h[:, f, :].bitcast(F32),
                                            ALU.subtract).then_inc(hl_ready, 1)
                for half in range(2):
                    banks = SETS[(b + 1 + half) % 2]
                    for t in range(NT):
                        n = 8 * b + 4 * half + t
                        dve.wait_ge(down_done, n + 1)
                        ya = y[:, t, 512 * half:512 * half + 512]
                        if b == 0:
                            nc.vector.tensor_copy(ya, ps[:, banks[t], :]).then_inc(acc_ready, 1)
                        else:
                            dve.wait_ge(acc_ready, n - 7)
                            nc.vector.tensor_tensor(ya, ps[:, banks[t], :], ya, ALU.add).then_inc(acc_ready, 1)
            dve.wait_ge(gain3_in, 16)
            for t in range(NT):
                dve.wait_ge(y_sq, 4 + t + 1)
                link(nc.vector.tensor_tensor(stat[:, SS_O + t:SS_O + t + 1], stat[:, SS_Y + 2 * t:SS_Y + 2 * t + 1],
                                             stat[:, SS_Y + 2 * t + 1:SS_Y + 2 * t + 2], ALU.add))
                link(rsqrt(SS_O + t, R_Y + t, 1, D))
                link(nc.vector.scalar_tensor_tensor(ow[:, t % 2, :], y[:, t, :], stat[:, R_Y + t:R_Y + t + 1], gain_a[:],
                                                    ALU.mult, ALU.mult))
                nc.vector.tensor_tensor(xres[:, t, :], xres[:, t, :], ow[:, t % 2, :], ALU.add).then_inc(res_ready, 1)

        @block.tensor
        def _(pe):
            def mm3(o, sh, sl, mh, ml, start, stop):
                nc.tensor.matmul(o, sh, mh, start=start, stop=False)
                nc.tensor.matmul(o, sh, ml, start=False, stop=False)
                return nc.tensor.matmul(o, sl, mh, start=False, stop=stop)

            def bank_free(n):
                if n >= 8:
                    pe.wait_ge(*reads(n - 8))

            def chunk(c):
                pe.wait_ge(lo_done, c + 1)
                r = ring_slot(c)
                return grid(ring_h[r], c), grid(ring_l[r], c)

            pe.wait_ge(consts, 13)
            pe.wait_ge(small_in, 16 * 8)
            nc.tensor.transpose(ps[:, 7, 0:28], rows[:], ident[0:28, 0:28])
            nc.tensor.transpose(ps[:, 7, 64:96], pe_rows[:], ident[0:32, 0:32]).then_inc(params_t, 1)
            for t in range(NT):
                pe.wait_ge(hn_ready, t + 1)
                if t == 3:
                    pe.wait_ge(params_ready, 2)
                for c in range(NC):
                    last = nc.tensor.transpose(ps[:, 2 * t + c // 4, (c % 4) * P:(c % 4) * P + P], y[:, t, c * P:(c + 1) * P], ident[:])
                last.then_inc(xt_done, 1)

            def token_group(j0, c0, n, first):
                for q in range(2):
                    wh, wl = chunk(c0 + q)
                    for t in range(NT):
                        if q == 0:
                            if first:
                                pe.wait_ge(xl_ready, 2 * t + 2)
                            else:
                                bank_free(j0 + t)
                        for k in range(4):
                            kk = 4 * q + k
                            last = mm3(ps[:, (j0 + t) % 8, 0:n], xT_h[:, kk, t * P:(t + 1) * P], xT_l[:, kk, t * P:(t + 1) * P],
                                       wh[:, k, :], wl[:, k, :], kk == 0, kk == NC - 1)
                        if q == 1:
                            last.then_inc(job_done, 1)
                        elif t == NT - 1:
                            last.then_inc(part_used, 1)

            def feature_group(j0, c):
                wh, wl = chunk(c)
                for j in range(2):
                    bank_free(j0 + j)
                    for k in range(NC):
                        last = mm3(ps[:, (j0 + j) % 8, :], wh[:, k, j * P:(j + 1) * P], wl[:, k, j * P:(j + 1) * P],
                                   xT_h[:, k, :], xT_l[:, k, :], k == 0, k == NC - 1)
                    last.then_inc(job_done, 1)

            token_group(J_B, C_B, BN, True)
            feature_group(J_CONV, C_LQ)
            feature_group(J_CONV + 2, C_LK)
            token_group(J_LO, C_LO, 512, False)
            pe.wait_ge(read_v, J_B + NT)
            for job, b0 in ((J_LI, BI), (J_LF, BF)):
                bank_free(job)
                for t in range(NT):
                    last = nc.tensor.transpose(ps[0:HEADS, job % 8, t * P:(t + 1) * P], zB[:, t, b0:b0 + HEADS], ident[:])
                last.then_inc(job_done, 1)
            feature_group(J_KV, C_KVS)
            feature_group(J_NQ, C_NQ)
            bank_free(J_GC)
            pe.wait_ge(read_v, reads(J_LF)[1])
            for k, r in enumerate((1, 0)):
                for t in range(NT):
                    c = 16 * k + HEADS * t
                    last = nc.tensor.transpose(ps[:, J_GC % 8, c:c + HEADS], g_row[:, r, t * P:(t + 1) * P], ident[0:HEADS, 0:HEADS])
            last.then_inc(job_done, 1)
            token_group(J_LV, C_LV, 512, False)
            feature_group(J_MQ, C_MQ)
            feature_group(J_MK, C_MK)
            for h in range(HEADS):
                bank_free(J_MB + h)
                nc.tensor.matmul(ps[:, (J_MB + h) % 8, :], sel[:, h, :], g_row[:, 2, :], start=True, stop=True).then_inc(job_done, 1)
            bank_free(J_H)
            bank_free(J_H + 1)
            for q in range(4):
                wh, wl = chunk(C_CMP + q)
                for k in range(8):
                    l = 8 * q + k
                    for t in range(2):
                        last = mm3(ps[:, (J_H + t) % 8, 0:2 * NP_], wh[:, k, t * P:(t + 1) * P], wl[:, k, t * P:(t + 1) * P],
                                   blk_h[:, l].rearrange("p j n -> p (j n)"), blk_l[:, l].rearrange("p j n -> p (j n)"),
                                   l == 0, l == CMP_LEN - 1)
                        if q == 3 and k == 7:
                            last.then_inc(job_done, 1)
                if q < 3:
                    last.then_inc(part_used, 1)

            def ml_scores(u):
                p, i = ML_UNITS[u]
                if u >= 2:
                    pe.wait_ge(ml_p, 2 * u - 2)
                for j in range(i + 1):
                    for m in range(2):
                        r = slice(DH * m, DH * m + DH)
                        last = nc.tensor.matmul(ps[:, 2 * (u % 2) + m, j * P:(j + 1) * P], qkT[r, 2 + p, j * P:(j + 1) * P],
                                                qkT[r, p, i * P:(i + 1) * P], start=True, stop=True)
                last.then_inc(ml_s, 1)

            def ml_values(u):
                p, i = ML_UNITS[u]
                pe.wait_ge(ml_p, 2 * u + 2)
                if u >= 2:
                    pe.wait_ge(ml_used, u - 1)
                for m in range(2):
                    for j in range(i + 1):
                        last = nc.tensor.matmul(ps[:, 6 + u % 2, 256 * m:256 * m + DV + 1],
                                                probsT[:, (2 * u + m) % 3, j * P:(j + 1) * P],
                                                lv1[:, j, 2 * p + m, :], start=(j == 0), stop=(j == i))
                last.then_inc(ml_o, 1)

            pe.wait_ge(read_v, READER.count("v"))
            pe.wait_ge(read_a, READER.count("a"))
            pe.wait_ge(silu_done, 4)
            ml_scores(0)
            for u in range(len(ML_UNITS)):
                if u + 1 < len(ML_UNITS):
                    ml_scores(u + 1)
                ml_values(u)
                if u == 2:
                    pe.wait_ge(gelu_ready, 1)
                    for t in range(2):
                        last = nc.tensor.matmul(ps[:, 4, 0:NP_], w2k[:, t].rearrange("p s d -> p (s d)"), gel[:, t, 0:NP_],
                                                start=(t == 0), stop=(t == 1))
                    last.then_inc(kv_cmp, 1)
                    for t in range(2):
                        last = nc.tensor.matmul(ps[:, 5, 0:DH], gelr[:, t].rearrange("p h n -> p (h n)"), w2v[:, t, :],
                                                start=(t == 0), stop=(t == 1))
                    last.then_inc(kv_cmp, 1)
                if u == 3:
                    pe.wait_ge(kc_ready, 1)
                    pe.wait_ge(vc_ready, 1)
                    for m in range(2):
                        nc.tensor.matmul(ps[:, 4 + m, 0:8 * NP_], identb[:], mask_c[:].rearrange("p i a n -> p (i a n)"),
                                         start=True, stop=True)
                    for i in range(NT):
                        for p in range(2):
                            for m in range(2):
                                r = slice(DH * m, DH * m + DH)
                                c = (2 * i + p) * NP_
                                last = nc.tensor.matmul(ps[:, 4 + m, c:c + NP_], nqT[r, p, i * P:(i + 1) * P], kcT[r, :],
                                                        start=False, stop=True, skip_group_check=True)
                    last.then_inc(cs_done, 1)
                if u == 6:
                    pe.wait_ge(cs_ready, 1)
                    for i in range(NT):
                        last = nc.tensor.transpose(ps[:, 4, i * P:(i + 1) * P], cexp[:, i].rearrange("p a n -> p (a n)"), ident[:])
                    last.then_inc(ct_done, 1)
            pe.wait_ge(ct_ready, 1)
            for i in range(NT):
                last = nc.tensor.matmul(ps[:, 5 - i // 2, 256 * (i % 2):256 * (i % 2) + 256], cexpT[:, i, :], vbd[:],
                                        start=True, stop=True)
                if i % 2 == 1:
                    last.then_inc(co_done, 1)

            keys = {"sel": kselT, "win": kwinT}

            def scores(u):
                br, p, i = UNITS[u]
                if u >= 2:
                    pe.wait_ge(p_ready, 2 * u - 2)
                w = (i + 1) * P
                for m in range(2):
                    r = slice(DH * m, DH * m + DH)
                    q = (mqT if br == "moba" else nqT)[r, p, i * P:(i + 1) * P]
                    k = mkT[r, p, 0:w] if br == "moba" else keys[br][r, 0:w]
                    nc.tensor.matmul(ps[:, 2 * (u % 2) + m, 0:w], q, k, start=True, stop=True)
                for m in range(2):
                    nc.tensor.matmul(ps[:, 2 * (u % 2) + m, w - P:w], identb[:], mask_s[:], start=False,
                                     stop=True, skip_group_check=True).then_inc(s_done, 1)

            def transposes(u):
                i = UNITS[u][2]
                for m in range(2):
                    s = 2 * u + m
                    pe.wait_ge(p_ready, s + 1)
                    if u >= 1:
                        pe.wait_ge(pt_a if m else pt_v, u)
                    for j in range(i + 1):
                        last = nc.tensor.transpose(ps[:, 4 + m, j * P:(j + 1) * P], probs[:, s % 3, j * P:(j + 1) * P], ident[:])
                    last.then_inc(t_done, 1)

            def values(u):
                br, p, i = UNITS[u]
                if u >= 2:
                    pe.wait_ge(o_used, u - 1)
                for m in range(2):
                    pe.wait_ge(pt_a if m else pt_v, u + 1)
                    v0 = {"sel": BS, "win": BW, "moba": BV + DH * (2 * p + m)}[br]
                    for j in range(i + 1):
                        last = nc.tensor.matmul(ps[:, 6 + u % 2, DH * m:DH * m + DH], probsT[:, (2 * u + m) % 3, j * P:(j + 1) * P],
                                                zB[:, j, v0:v0 + DH], start=(j == 0), stop=(j == i))
                last.then_inc(o_done, 1)

            def y_transposes(k):
                c = K_ORDER[k]
                for t in range(NT):
                    last = nc.tensor.transpose(ps[:, YT_BANK[k], t * P:(t + 1) * P], y[:, t, c * P:(c + 1) * P], ident[:])
                last.then_inc(yt_done, 1)

            NU = len(UNITS)
            pe.wait_ge(dup_in, 32)
            pe.wait_ge(ml_p, 2 * len(ML_UNITS))
            scores(0)
            pe.wait_ge(co_used, 1)
            pe.wait_ge(ml_used, len(ML_UNITS))
            for u in range(NU):
                if u + 1 < NU:
                    scores(u + 1)
                transposes(u)
                if u >= 1 and u != N_NSA:
                    values(u - 1)
                if u == N_NSA - 1:
                    values(u)
                    pe.wait_ge(ml_y, 2)
                    pe.wait_ge(pt_v, N_NSA)
                    pe.wait_ge(pt_a, N_NSA)
                    pe.wait_ge(o_used, N_NSA)
                    for k in range(4):
                        y_transposes(k)
                    pe.wait_ge(yl_ready, 4)
            values(NU - 1)

            def project(t, half, k_lo, k_hi):
                for k in range(k_lo, k_hi):
                    kset, kk = divmod(k, 4)
                    wh, wl = grid(ring_h[ring_slot(C_WO + 2 * kset + half)], C_WO), grid(ring_l[ring_slot(C_WO + 2 * kset + half)], C_WO)
                    c = K_ORDER[k]
                    last = mm3(ps[:, WO_BANK[t] + half, :], xT_h[:, c, t * P:(t + 1) * P], xT_l[:, c, t * P:(t + 1) * P],
                               wh[:, kk, :], wl[:, kk, :], k == 0, k == NC - 1)
                    if t == NT - 1 and k == 3:
                        last.then_inc(part_used, 1)
                if k_hi == NC:
                    last.then_inc(wo_done, 1)

            def hm_transposes(t):
                pe.wait_ge(hm_ready, t + 1)
                for c in range(NC):
                    last = nc.tensor.transpose(ps[:, WO_BANK[t] + c // 4, (c % 4) * P:(c % 4) * P + P],
                                               ow[:, t % 2, c * P:(c + 1) * P], ident[:])
                last.then_inc(hmt_done, 1)

            pe.wait_ge(lo_done, C_WO + 4)
            pe.wait_ge(p_ready, 2 * NU)
            pe.wait_ge(nsa_y, 1)
            y_transposes(4)
            y_transposes(5)
            project(0, 0, 0, 4)
            project(0, 1, 0, 4)
            pe.wait_ge(yl_ready, 6)
            project(0, 0, 4, 6)
            project(0, 1, 4, 6)
            pe.wait_ge(moba_y, 1)
            y_transposes(6)
            y_transposes(7)
            pe.wait_ge(yl_ready, 8)
            project(0, 0, 6, 8)
            project(0, 1, 6, 8)
            pe.wait_ge(o_used, NU)
            for t in range(1, NT):
                project(t, 0, 0, NC)
                project(t, 1, 0, NC)
                if t >= 2:
                    hm_transposes(t - 2)
            hm_transposes(NT - 2)
            hm_transposes(NT - 1)
            pe.wait_ge(hml_ready, 2 * NT)

            for b in range(NB):
                c0 = C_MLP + PER_BLOCK * b
                for f in range(FB):
                    n = FB * b + f
                    wh, wl = chunk(c0 + f // 2)
                    if f >= 4:
                        pe.wait_ge(relu_ready, n - 3)
                    elif b >= 1:
                        pe.wait_ge(acc_ready, 8 * (b - 1) + f + 1)
                    for k in range(NC):
                        last = mm3(ps[:, SETS[b % 2][f % 4], :], wh[:, k, (f % 2) * P:(f % 2) * P + P], wl[:, k, (f % 2) * P:(f % 2) * P + P],
                                   xT_h[:, k, :], xT_l[:, k, :], k == 0, k == NC - 1)
                    last.then_inc(up_done, 1)
                for half in range(2):
                    banks = SETS[(b + 1 + half) % 2]
                    for q in range(2):
                        wh, wl = chunk(c0 + FB // 2 + 2 * half + q)
                        for t in range(NT):
                            if q == 0 and half == 0 and b >= 1:
                                pe.wait_ge(acc_ready, 8 * (b - 1) + 4 + t + 1)
                            if q == 0 and half == 1:
                                pe.wait_ge(relu_ready, FB * b + FB)
                            for k in range(4):
                                f = 4 * q + k
                                if t == 0 and half == 0:
                                    pe.wait_ge(hl_ready, FB * b + f + 1)
                                last = mm3(ps[:, banks[t], :], hT_h[:, f, t * P:(t + 1) * P], hT_l[:, f, t * P:(t + 1) * P],
                                           wh[:, k, :], wl[:, k, :], f == 0, f == FB - 1)
                            if q == 1:
                                last.then_inc(down_done, 1)
                            elif t == NT - 1:
                                last.then_inc(part_used, 1)


_INS = ["x", "norm_g", "w_in", "mlstm_conv_w", "mlstm_conv_b", "mlstm_gate_b", "nsa_cmp_pe", "nsa_cmp_w1",
        "nsa_cmp_w2", "head_g", "w_out", "w_mlp1", "w_mlp2"]


def kernel(**inputs):
    import numpy as np
    import concourse.bacc as bacc
    from concourse.bass_utils import run_bass_kernel_spmd

    nc = bacc.Bacc("TRN2", target_bir_lowering=False, num_devices=1)
    arrays, args = {}, []
    for name in _INS:
        a = np.ascontiguousarray(inputs[name])
        arrays[f"in_{name}"] = a
        args.append(nc.dram_tensor(f"in_{name}", a.shape, mybir.dt.from_np(a.dtype), kind="ExternalInput").ap())
    o = nc.dram_tensor("out_0", (1, SEQ, D), F32, kind="ExternalOutput").ap()
    build(nc, *args, o)
    r = run_bass_kernel_spmd(nc, [arrays], core_ids=[0])
    return r.results[0]["out_0"]
```

```python
from contextlib import ExitStack

import concourse.bass as bass
from concourse import mybir

ALU = mybir.AluOpType
ACT = mybir.ActivationFunctionType
AX = mybir.AxisListType
F32 = mybir.dt.float32
F32R = mybir.dt.float32r
BF16 = mybir.dt.bfloat16
I32 = mybir.dt.int32

P = 128
SEQ = 512
D = 1024
NT = SEQ // P
NC = D // P
DH = 64
DV = 128
HEADS = 4
FF = 4 * D
EPS = 1e-6
NEG = -1e30
CMP_STRIDE, CMP_LEN, CMP_HID = 16, 32, 256
NCMP = (SEQ - CMP_LEN) // CMP_STRIDE + 1
NP_ = NCMP + 1

MQ, MK, MV, LQ, LK, LV, LO, LI, LF, NQ, KC, VC, KSL, VSL, KWN, VWN, NG, DIN = (
    0, 256, 512, 768, 1024, 1280, 1792, 2304, 2308, 2312, 2568, 2632, 2696, 2760, 2824, 2888, 2952, 2964)
BV, BS, BW, BG, BI, BF, BN = 0, 256, 320, 384, 396, 400, 404

CHUNK = 2048
RAW = 2

C_B, C_LQ, C_LK, C_LO, C_KVS, C_NQ, C_LV, C_MQ, C_MK, C_CMP, C_WO, C_MLP = 0, 2, 3, 4, 6, 7, 8, 10, 11, 12, 16, 20
FB = 8
NB = FF // P // FB
PER_BLOCK = FB // 2 + FB // 2
NCHUNK = C_MLP + NB * PER_BLOCK

J_B, J_CONV, J_LO, J_LI, J_LF, J_KV, J_KS, J_NQ, J_GC, J_LV, J_MQ, J_MK, J_MB, J_H = (
    0, 4, 8, 12, 13, 14, 15, 16, 18, 19, 23, 25, 27, 31)
NJOB = 33
PARAM_BANK = 7
READER = "vvvv" "vvvv" "aaaa" "v" "v" "v" "a" "aa" "a" "vvvv" "aa" "vv" "aaaa" "vv"

K_ORDER = [2, 3, 4, 5, 6, 7, 0, 1]
PAIRS = [("sel", 0), ("sel", 1), ("win", 0), ("win", 1), ("moba", 0), ("moba", 1)]
SHARED = (0, 1, C_CMP + 3, C_MLP)
N_NSA = 4
NU = NT * len(PAIRS)
ML_UNITS = [(p, i) for p in range(2) for i in range(NT)]
WO_BANK = [0, 6, 2, 4]
YT_BANK = [4, 5, 2, 3, 4, 5, 2, 3]
EARLY_F, EARLY_T = 2, 2
SETS = [(0, 1, 6, 7), (2, 3, 4, 5)]


def ring_slot(c):
    return c % 3 if c < C_WO + 3 else [1, 2, 0, 3][(c - C_WO) % 4]


def ring_previous(c):
    return c - 3 if c < C_WO + 3 else c - 4


def build(nc, x, norm_g, w_in, conv_w, conv_b, gate_b, cmp_pe, cmp_w1, cmp_w2, head_g, w_out, w1, w2, out):
    ctx = ExitStack()
    with ctx:
        base = (nc.sbuf_base + 63) // 64 * 64
        cursor = [base]

        def at(name, shape, dt, offset):
            return nc.alloc_sbuf_tensor_at(name, shape, dt, offset=offset)

        def put(name, shape, dt):
            size = 2 if dt == BF16 else 4
            for d in shape[1:]:
                size *= d
            size = (size + 63) // 64 * 64
            cursor[0] += size
            return at(name, shape, dt, cursor[0] - size)

        raw = [put(f"raw{r}", [P, CHUNK], F32) for r in range(RAW)]
        ring_h = [put(f"ring_h{r}", [P, CHUNK], F32R) for r in range(3)]
        ring_l = [put(f"ring_l{r}", [P, CHUNK], F32R) for r in range(3)]
        o_xt = cursor[0]
        xT_h = put("xT_h", [P, NC, SEQ], F32R)
        xT_l = put("xT_l", [P, NC, SEQ], F32R)
        W = at("W", [P, HEADS, NT, NT, P], F32, o_xt)
        pT = at("pT", [P, 2, 2, NT, SEQ], F32, o_xt)
        xres = put("xres", [P, NT, D], F32)
        gain_a = put("gain_a", [P, D], F32)
        ident = put("ident", [P, P], F32)
        identb = put("identb", [P, P], BF16)
        mask_s = put("mask_s", [P, P], BF16)
        mask_c = put("mask_c", [P, NT, 2, NP_], BF16)
        vis = put("vis", [P, NT, NP_], F32)
        rows = put("rows", [28, P], F32)
        cols = put("cols", [P, 28], F32)
        pe_rows = put("pe_rows", [CMP_LEN, P], F32)
        gb = put("gb", [HEADS, 2], F32)
        w2k = put("w2k", [P, 2, 2, DH], F32)
        w2v = put("w2v", [P, 2, DH], F32)
        peT = put("peT", [P, CMP_LEN], F32)
        junkb = put("junkb", [P, DV], F32)
        wide = put("wide", [P, 48], F32)
        zero1 = put("zero1", [P, 1], F32)
        eps1 = put("eps1", [P, 1], F32)
        stat = put("stat", [P, 256], F32)
        gt = put("gt", [P, NT, 12], F32)
        gcol = put("gcol", [P, NT, HEADS], F32)
        emc = put("emc", [P, NT, HEADS], F32)
        kcT = put("kcT", [P, NP_], F32)
        gel = put("gel", [P, 2, 2 * NP_], F32)
        gelr = put("gelr", [P, 2, HEADS, NP_], F32)
        o_cg = cursor[0]
        cg = put("cg", [P, 4, 2, 2 * NP_], F32)
        hsb = at("hsb", [2 * NP_, CMP_HID], F32, o_cg + 1024)
        sel = at("sel", [HEADS, HEADS, P], F32, o_cg)

        o_a = cursor[0]
        lv1 = at("lv1", [P, NT, HEADS, DV + 1], F32, o_a)
        qkT = at("qkT", [P, 4, SEQ], F32, o_a + 8320)
        ring_h.append(at("ring_h3", [P, CHUNK], F32R, o_a))
        ring_l.append(at("ring_l3", [P, CHUNK], F32R, o_a + 8320))
        y = at("y", [P, NT, D], F32, o_a + 16512)
        o_m = o_a + 32896
        mqT = at("mqT", [P, 2, SEQ], F32, o_m)
        mkT = at("mkT", [P, 2, SEQ], F32, o_m + 4096)
        nqT = at("nqT", [P, 2, SEQ], F32, o_m + 8192)
        gain_b = at("gain_b", [P, D], F32, o_m + 8192)
        kselT = at("kselT", [P, SEQ], F32, o_m + 12288)
        kwinT = at("kwinT", [P, SEQ], F32, o_m + 14336)
        zB = at("zB", [P, NT, BN], F32, o_m + 16384)
        hid = at("hid", [P, NT, HEADS, DV], F32, o_m + 22848)
        blk_h = at("blk_h", [P, CMP_LEN, 2, NP_], F32R, o_m + 22848)
        o_p = o_m + 31040
        probs = at("probs", [P, 3, SEQ], F32, o_p)
        probsT = at("probsT", [P, 3, SEQ], F32, o_p + 6144)
        blk_l = at("blk_l", [P, CMP_LEN, 2, NP_], F32R, o_p)
        sig = at("sig", [P, 2, SEQ], F32, o_p)
        oT = at("oT", [P, SEQ], F32, o_p + 6144)
        work = at("work", [P, SEQ], F32, o_p + 8192)
        ysq = at("ysq", [P, SEQ], F32, o_p + 10240)
        junk = at("junk", [P, D], F32, o_p + 8192)
        o_r = o_p + 12288
        g_row = at("g_row", [HEADS, 3, SEQ], F32, o_r)
        junk_w = at("junk_w", [P, D], F32, o_m)
        cexp = at("cexp", [P, NT, 4, NP_], F32, o_r)
        cexpT = at("cexpT", [P, NT, P], F32, o_r + 2048)
        vbd = at("vbd", [P, HEADS * DH], F32, o_r + 4096)
        hT_h = at("hT_h", [P, FB, SEQ], F32R, o_m)
        hT_l = at("hT_l", [P, FB, SEQ], F32R, o_m + 16384)
        ow = at("ow", [P, 2, D], F32, o_m + 32768)
        relu = at("relu", [P, 2, SEQ], F32, o_m + 40960)
        sq = at("sq", [P, 2, SEQ], F32, o_m + 45056)
        yg = at("yg", [P, NT, D // 2], F32, o_m + 32768)
        assert o_r + 6144 <= nc.sbuf_usable_end and o_m + 49152 <= nc.sbuf_usable_end, (o_r + 6144, nc.sbuf_usable_end)

        ps = ctx.enter_context(nc.psum_tensor("ps", [P, 8, 512], F32))

        SS_X, SS_ML, SS_NSA, SS_MB, SS_O, SS_X1, SS_Y = 0, 4, 20, 36, 52, 56, 60
        R_X, R_ML, R_NSA, R_MB, R_O, R_X1, R_Y = 68, 72, 88, 104, 120, 124, 128
        NMAX, RSUM, WK, ROOT = 132, 180, 228, 244
        BASE = 4

        def rsum(u, m):
            return RSUM + 2 * u + m

        def sem(name):
            return ctx.enter_context(nc.semaphore(name))

        x_in = [sem(f"x_in{t}") for t in range(NT)]
        small_in = sem("small_in")
        gain0_in = sem("gain0_in")
        gain1_in, gain2_in, gain3_in = sem("gain1_in"), sem("gain2_in"), sem("gain3_in")
        raw_in = [sem(f"raw_in{r}") for r in range(RAW)]
        dup_in = sem("dup_in")
        stored = sem("stored")
        consts = sem("consts")
        hi_done, lo_done = sem("hi_done"), sem("lo_done")
        part_used = sem("part_used")
        x_sq, hn_ready, xt_done, xh_ready, xl_ready = (sem(n) for n in
                                                      ("x_sq", "hn_ready", "xt_done", "xh_ready", "xl_ready"))
        lo_first = sem("lo_first")
        eps_set, root_done = sem("eps_set"), sem("root_done")
        params_t = sem("params_t")
        params_ready = sem("params_ready")
        job_done = sem("job_done")
        read_v, read_a = sem("read_v"), sem("read_a")
        chain = sem("chain")
        conv_lin, conv_acc, conv_sig = sem("conv_lin"), sem("conv_acc"), sem("conv_sig")
        silu_done, w_step = sem("silu_done"), sem("w_step")
        blkh_ready = sem("blkh_ready")
        ks_ready = sem("ks_ready")
        gates_ready = sem("gates_ready")
        lf_step, lf_ready = sem("lf_step"), sem("lf_ready")
        rows_ready = sem("rows_ready")
        gcol_ready = sem("gcol_ready")
        w_exp, w_ready = sem("w_exp"), sem("w_ready")
        gelu_arg, gelu_exp, gelu_ready = sem("gelu_arg"), sem("gelu_exp"), sem("gelu_ready")
        kv_cmp, kc_ready, vc_ready = sem("kv_cmp"), sem("kc_ready"), sem("vc_ready")
        cs_done, cs_sub, cs_exp, cs_ready = sem("cs_done"), sem("cs_sub"), sem("cs_exp"), sem("cs_ready")
        ct_done, ct_ready, co_done, co_used = sem("ct_done"), sem("ct_ready"), sem("co_done"), sem("co_used")
        ml_s, ml_p, ml_o, ml_used, ml_ss = sem("ml_s"), sem("ml_p"), sem("ml_o"), sem("ml_used"), sem("ml_ss")
        ml_rn, nsa_rn, ml_y, nsa_y, moba_y = (sem(n) for n in ("ml_rn", "nsa_rn", "ml_y", "nsa_y", "moba_y"))
        s_done, mx_done, p_ready = sem("s_done"), sem("mx_done"), sem("p_ready")
        t_done, pt_v, pt_a = sem("t_done"), sem("pt_v"), sem("pt_a")
        o_done, ot_ready, bt_done = sem("o_done"), sem("ot_ready"), sem("bt_done")
        bt_used, y_sq_ready, y_ss = sem("bt_used"), sem("y_sq_ready"), sem("y_ss")
        yt_done, yh_ready, yl_ready = sem("yt_done"), sem("yh_ready"), sem("yl_ready")
        wo_done, o_sq, x1_ready, x1_sq, hm_ready = (sem(n) for n in ("wo_done", "o_sq", "x1_ready", "x1_sq", "hm_ready"))
        hmt_done, hmh_ready, hml_ready = sem("hmt_done"), sem("hmh_ready"), sem("hml_ready")
        up_done, relu_ready, sq_ready, hh_ready, hl_ready = (sem(n) for n in (
            "up_done", "relu_ready", "sq_ready", "hh_ready", "hl_ready"))
        down_done, acc_ready, y_sq, res_ready = sem("down_done"), sem("acc_ready"), sem("y_sq"), sem("res_ready")
        base_ready = sem("base_ready")
        yg_ready, ss0_ready = sem("yg_ready"), sem("ss0_ready")

        def reads(n):
            return (read_v if READER[n] == "v" else read_a), READER[:n + 1].count(READER[n])

        def released(c):
            inside = [C_B, C_LO, C_LV, C_CMP, C_CMP + 1, C_CMP + 2, C_WO, C_WO + 1]
            if c in inside:
                return part_used, inside.index(c) + 1
            if c < C_WO:
                return job_done, {C_B + 1: J_B + 4, C_LQ: J_CONV + 2, C_LK: J_CONV + 4, C_LO + 1: J_LO + 4,
                                  C_KVS: J_KS + 1, C_NQ: J_NQ + 2, C_LV + 1: J_LV + 4, C_MQ: J_MQ + 2,
                                  C_MK: J_MK + 2, C_CMP + 3: J_H + 1}[c]
            if c < C_MLP:
                return wo_done, {C_WO + 2: 7, C_WO + 3: 8}[c]
            b, k = divmod(c - C_MLP, PER_BLOCK)
            if k < FB // 2:
                return up_done, FB * b + 2 * (k + 1)
            half, q = divmod(k - FB // 2, 2)
            if q == 0:
                return part_used, len(inside) + 2 * b + half + 1
            return down_done, 8 * b + 4 * (half + 1)

        def chunk_parts(c):
            def kn(lo, n, k0=0, kn_=NC):
                return w_in[0, k0 * P:(k0 + kn_) * P, lo:lo + n].rearrange("(k p) n -> p k n", p=P)
            if c in (C_B, C_B + 1):
                k0 = 4 * (c - C_B)
                return BN, [((0, 256), kn(MV, 256, k0, 4)), ((BS, 64), kn(VSL, 64, k0, 4)),
                            ((BW, 76), kn(VWN, 76, k0, 4)), ((BI, 8), kn(LI, 8, k0, 4))]
            if c in (C_LO, C_LO + 1):
                return 512, [((0, 512), kn(LO, 512, 4 * (c - C_LO), 4))]
            if c in (C_LV, C_LV + 1):
                return 512, [((0, 512), kn(LV, 512, 4 * (c - C_LV), 4))]
            if c == C_KVS:
                return 256, [((0, 192), kn(KC, 192)), ((192, 64), kn(KWN, 64))]
            if c < C_CMP:
                return 256, [((0, 256), kn({C_LQ: LQ, C_LK: LK, C_NQ: NQ, C_MQ: MQ, C_MK: MK}[c], 256))]
            if c < C_WO:
                l0 = 8 * (c - C_CMP)
                return 256, [((0, 256), cmp_w1[0, j, l0 * DH:(l0 + 8) * DH, :].rearrange("(l d) h -> d l h", d=DH))
                             for j in range(2)]
            if c < C_MLP:
                kset, half = divmod(c - C_WO, 2)
                ks = K_ORDER[4 * kset:4 * kset + 4]
                runs = [(ks[0], 4)] if kset == 0 else [(ks[0], 2), (ks[2], 2)]
                return 512, [((0, 512), w_out[0, k0 * P:(k0 + n) * P, 512 * half:512 * half + 512]
                              .rearrange("(k p) n -> p k n", p=P)) for k0, n in runs]
            b, k = divmod(c - C_MLP, PER_BLOCK)
            if k < FB // 2:
                f0 = (FB * b + 2 * k) * P
                return 256, [((0, 256), w1[0, :, f0:f0 + 256].rearrange("(k p) n -> p k n", p=P))]
            half, q = divmod(k - FB // 2, 2)
            f0 = (FB * b + 4 * q) * P
            return 512, [((0, 512), w2[0, f0:f0 + 512, 512 * half:512 * half + 512]
                          .rearrange("(k p) n -> p k n", p=P))]

        def size(c):
            n = chunk_parts(c)[0]
            return n * (4 if n > 256 else 8)

        def grid(t, c):
            n = chunk_parts(c)[0]
            return t[:, 0:size(c)].rearrange("p (k n) -> p k n", n=n)

        block = ctx.enter_context(nc.Block())

        @block.sync
        def _(sp):
            def load_chunk(c):
                if c >= RAW:
                    sp.wait_ge(lo_done, c - RAW + 1)
                    if c - RAW in SHARED:
                        sp.wait_ge(lo_first, SHARED.index(c - RAW) + 1)
                view = grid(raw[c % RAW], c)
                parts = chunk_parts(c)[1]
                k0 = 0
                for j, ((n0, n), src) in enumerate(parts):
                    if C_CMP <= c < C_WO:
                        dst = view[DH * j:DH * j + DH, :, :]
                    elif C_WO <= c < C_MLP:
                        kk = src.shape[1]
                        dst = view[:, k0:k0 + kk, :]
                        k0 += kk
                    else:
                        dst = view[:, :, n0:n0 + n]
                    sp.dma_start(dst, src).then_inc(raw_in[c % RAW], 16)

            def load_x(t):
                sp.dma_start(xres[:, t, :], x[0, t * P:(t + 1) * P, :]).then_inc(x_in[t], 16)

            load_x(0)
            sp.dma_start(gain_a[:], norm_g[0, 0:1, :].to_broadcast([P, D])).then_inc(gain0_in, 16)
            load_chunk(0)
            load_x(1)
            load_chunk(1)
            load_x(2)
            load_x(3)
            sp.dma_start(rows[0:16, :], conv_w[0].rearrange("k (c p) -> (k c) p", p=P)).then_inc(small_in, 16)
            sp.dma_start(rows[16:20, :], conv_b[0].rearrange("(c p) -> c p", p=P)).then_inc(small_in, 16)
            sp.dma_start(rows[20:28, :], head_g[0].rearrange("(c p) -> c p", p=P)).then_inc(small_in, 16)
            sp.dma_start(pe_rows[:].rearrange("l (j d) -> l j d", j=2), cmp_pe[0].rearrange("j l d -> l j d")).then_inc(small_in, 16)
            with nc.allow_non_contiguous_dma(reason="eight gate biases"):
                sp.dma_start(gb[:], gate_b[0].rearrange("j h -> h j")).then_inc(small_in, 16)
            load_chunk(2)
            for s in range(2):
                sp.dma_start(w2k[:, :, s, :], cmp_w2[0, 0].rearrange("(t p) d -> p t d", p=P)).then_inc(small_in, 16)
            sp.dma_start(w2v[:], cmp_w2[0, 1].rearrange("(t p) d -> p t d", p=P)).then_inc(small_in, 16)
            for c in range(3, NCHUNK):
                if c == C_WO:
                    sp.wait_ge(hn_ready, NT)
                    sp.dma_start(gain_a[:], norm_g[0, 1:2, :].to_broadcast([P, D])).then_inc(gain1_in, 16)
                if c == C_MLP:
                    sp.wait_ge(s_done, 2 * NT * N_NSA)
                    sp.dma_start(gain_b[:], norm_g[0, 2:3, :].to_broadcast([P, D])).then_inc(gain2_in, 16)
                if c == C_MLP + PER_BLOCK:
                    sp.wait_ge(x1_ready, 2 * NT)
                    sp.dma_start(gain_a[:], norm_g[0, 3:4, :].to_broadcast([P, D])).then_inc(gain3_in, 16)
                load_chunk(c)
            for t in range(NT):
                for k, half in enumerate((1, 0)):
                    sp.wait_ge(res_ready, 2 * t + k + 1)
                    h0 = 512 * half
                    sp.dma_start(out[0, t * P:(t + 1) * P, h0:h0 + 512], xres[:, t, h0:h0 + 512]).then_inc(stored, 16)
            sp.wait_ge(stored, 16 * 2 * NT)

        def raw_full(c):
            return 16 * sum(len(chunk_parts(k)[1]) for k in range(c % RAW, c + 1, RAW))

        @block.gpsimd
        def _(pool):
            nc.gpsimd.memset(ident[:], 0.0).then_inc(consts, 1)
            pool.wait_ge(consts, 1)
            nc.gpsimd.affine_select(out=ident[:], in_=ident[:], compare_op=ALU.not_equal, fill=1.0, base=0,
                                    pattern=[[-1, P]], channel_multiplier=1).then_inc(consts, 1)
            nc.gpsimd.memset(identb[:], 0.0).then_inc(consts, 1)
            nc.gpsimd.memset(mask_s[:], 0.0).then_inc(consts, 1)
            nc.gpsimd.memset(mask_c[:], 0.0).then_inc(consts, 1)
            nc.gpsimd.memset(vis[:], 1.0).then_inc(consts, 1)
            nc.gpsimd.memset(sel[:], 0.0).then_inc(consts, 1)
            nc.gpsimd.memset(zero1[:], 0.0).then_inc(consts, 1)
            pool.wait_ge(consts, 8)
            nc.gpsimd.affine_select(out=identb[:], in_=identb[:], compare_op=ALU.not_equal, fill=1.0, base=0,
                                    pattern=[[-1, P]], channel_multiplier=1).then_inc(consts, 1)
            nc.gpsimd.affine_select(out=mask_s[:], in_=mask_s[:], compare_op=ALU.is_ge, fill=NEG, base=0,
                                    pattern=[[-1, P]], channel_multiplier=1).then_inc(consts, 1)
            nc.gpsimd.affine_select(out=mask_c[:], in_=mask_c[:], compare_op=ALU.is_ge, fill=NEG,
                                    base=1 - CMP_LEN, pattern=[[P, NT], [0, 2], [-CMP_STRIDE, NP_]],
                                    channel_multiplier=1).then_inc(consts, 1)
            nc.gpsimd.affine_select(out=vis[:], in_=vis[:], compare_op=ALU.is_ge, fill=0.0,
                                    base=1 - CMP_LEN, pattern=[[P, NT], [-CMP_STRIDE, NP_]],
                                    channel_multiplier=1).then_inc(consts, 1)
            nc.gpsimd.affine_select(out=sel[:], in_=sel[:], compare_op=ALU.not_equal, fill=1.0, base=0,
                                    pattern=[[-1, HEADS], [0, P]], channel_multiplier=1).then_inc(consts, 1)

            def low_half(c):
                pool.wait_ge(hi_done, c + 1)
                n, r = size(c), ring_slot(c)
                n0 = n // 2 if c in SHARED else 0
                nc.gpsimd.tensor_tensor(ring_l[r][:, n0:n], raw[c % RAW][:, n0:n], ring_h[r][:, n0:n].bitcast(F32),
                                        ALU.subtract).then_inc(lo_done, 1)

            for c in range(C_WO):
                low_half(c)
            for h in range(HEADS):
                pool.wait_ge(w_exp, h + 1)
                for i in range(NT):
                    last = nc.gpsimd.affine_select(out=W[:, h, i, i, :], in_=W[:, h, i, i, :], compare_op=ALU.is_ge,
                                                   fill=0.0, base=0, pattern=[[1, P]], channel_multiplier=-1)
                last.then_inc(w_ready, 1)
            low_half(C_WO)
            low_half(C_WO + 1)
            pool.wait_ge(ml_rn, 1)
            rn = stat[:, R_ML:R_ML + 16].rearrange("p (t h o) -> p t h o", h=HEADS, o=1).to_broadcast([P, NT, HEADS, DV])
            nc.gpsimd.tensor_tensor(hid[:], hid[:], rn, ALU.mult).then_inc(ml_y, 1)
            pool.wait_ge(ml_y, 1)
            yml = y[:, :, 256:768].rearrange("p t (h d) -> p t h d", h=HEADS)
            nc.gpsimd.tensor_tensor(yml, yml, hid[:], ALU.mult).then_inc(ml_y, 1)
            low_half(C_WO + 2)
            low_half(C_WO + 3)
            pool.wait_ge(nsa_rn, 1)
            rn = stat[:, R_NSA:R_NSA + 16].rearrange("p (t h o) -> p t h o", h=HEADS, o=1).to_broadcast([P, NT, HEADS, DH])
            yn = y[:, :, 768:1024].rearrange("p t (h d) -> p t h d", h=HEADS)
            nc.gpsimd.tensor_tensor(yn, yn, rn, ALU.mult).then_inc(nsa_y, 1)
            for c in range(C_MLP, NCHUNK):
                low_half(c)
            pool.wait_ge(gain3_in, 16)
            for t in range(NT):
                pool.wait_ge(acc_ready, 8 * (NB - 1) + t + 1)
                nc.gpsimd.tensor_tensor(yg[:, t, :], y[:, t, 0:512], gain_a[:, 0:512], ALU.mult).then_inc(yg_ready, 1)

        @block.scalar
        def _(act):
            def high_half(c):
                act.wait_ge(raw_in[c % RAW], raw_full(c))
                if c == C_WO + 3:
                    act.wait_ge(ml_o, len(ML_UNITS))
                elif c >= 3:
                    act.wait_ge(*released(ring_previous(c)))
                n, r = size(c), ring_slot(c)
                nc.scalar.activation(ring_h[r][:, 0:n], raw[c % RAW][:, 0:n], ACT.Copy).then_inc(hi_done, 1)

            act.wait_ge(eps_set, 1)
            nc.scalar.activation(stat[:, ROOT + 8:ROOT + 9], eps1[:], ACT.Sqrt)

            def root(ss, r, beside=eps1[:]):
                nc.scalar.activation(stat[:, r:r + 1], stat[:, ss:ss + 1], ACT.Sqrt, scale=1.0 / D,
                                     bias=beside).then_inc(root_done, 1)

            def x_root(t):
                act.wait_ge(x_in[t], 16)
                nc.scalar.activation(junk[:], xres[:, t, :], ACT.Square,
                                     accum_out=stat[:, SS_X + t:SS_X + t + 1]).then_inc(x_sq, 1)
                act.wait_ge(x_sq, t + 1)
                root(SS_X + t, ROOT + t)

            def x_high(t):
                act.wait_ge(xt_done, t + 1)
                for b in range(2):
                    nc.scalar.activation(xT_h[:, 4 * b:4 * b + 4, t * P:(t + 1) * P],
                                         ps[:, 2 * t + b, :].rearrange("p (c q) -> p c q", c=4),
                                         ACT.Copy).then_inc(xh_ready, 1)

            x_root(0)
            high_half(0)
            x_high(0)
            x_root(1)
            high_half(1)
            x_root(2)
            x_high(1)
            x_root(3)
            x_high(2)
            high_half(2)
            x_high(3)
            high_half(3)

            def conv_linear(n):
                act.wait_ge(job_done, J_CONV + n + 1)
                if n == 0:
                    act.wait_ge(params_ready, 1)
                nc.scalar.activation(qkT[:, n, :], ps[:, (J_CONV + n) % 8, :], ACT.Identity,
                                     scale=cols[:, 12 + n:13 + n], bias=cols[:, 16 + n:17 + n]).then_inc(conv_lin, 1)

            def conv_sigmoid(n):
                act.wait_ge(conv_acc, n + 1)
                nc.scalar.activation(sig[:, n % 2, :], qkT[:, n, :], ACT.Sigmoid).then_inc(conv_sig, 1)

            for n in range(4):
                conv_linear(n)
                if n >= 1:
                    conv_sigmoid(n - 1)
                if n == 1:
                    high_half(4)
            conv_sigmoid(3)
            high_half(5)
            act.wait_ge(read_v, J_B + NT)
            nc.scalar.activation(gt[:], zB[:, :, BG:BG + 12], ACT.Sigmoid).then_inc(gates_ready, 1)
            high_half(6)
            for t in range(NT):
                act.wait_ge(job_done, J_LO + t + 1)
                nc.scalar.activation(y[:, t, 256:768], ps[:, (J_LO + t) % 8, :], ACT.Sigmoid).then_inc(read_a, 1)
            high_half(7)
            act.wait_ge(job_done, J_LF + 1)
            nc.scalar.activation(g_row[:, 0, :], ps[0:HEADS, J_LF % 8, :], ACT.Abs, bias=gb[:, 1:2]).then_inc(lf_step, 1)
            act.wait_ge(lf_step, 1)
            nc.scalar.activation(g_row[:, 0, :], g_row[:, 0, :], ACT.Exp, scale=-1.0).then_inc(lf_step, 1)
            act.wait_ge(lf_step, 2)
            nc.scalar.activation(g_row[:, 0, :], g_row[:, 0, :], ACT.Ln, bias=1.0).then_inc(lf_ready, 1)
            act.wait_ge(job_done, J_KV + 1)
            for j in range(2):
                for a in range(2):
                    src = ps[DH * j:DH * j + DH, J_KV % 8, :].rearrange("p (n b) -> p b n", b=16)[:, :, a:a + NCMP]
                    nc.scalar.activation(blk_h[DH * j:DH * j + DH, 16 * a:16 * a + 16, j, 0:NCMP], src,
                                         ACT.Copy).then_inc(blkh_ready, 1)
                act.wait_ge(params_ready, 2)
                nc.scalar.activation(blk_h[DH * j:DH * j + DH, :, j, NCMP], peT[DH * j:DH * j + DH, :],
                                     ACT.Copy).then_inc(blkh_ready, 1)
            act.wait_ge(job_done, J_KS + 1)
            nc.scalar.activation(kselT[0:DH, :], ps[0:DH, J_KS % 8, :], ACT.Copy).then_inc(ks_ready, 1)
            nc.scalar.activation(kwinT[DH:P, :], ps[DH:P, J_KS % 8, :], ACT.Copy).then_inc(read_a, 1)
            act.wait_ge(ks_ready, 1)
            act.dma_start(kselT[DH:P, :], kselT[0:DH, :]).then_inc(dup_in, 16)
            act.wait_ge(read_a, reads(J_KS)[1])
            act.dma_start(kwinT[0:DH, :], kwinT[DH:P, :]).then_inc(dup_in, 16)
            high_half(8)
            high_half(9)
            for p in range(2):
                act.wait_ge(job_done, J_NQ + p + 1)
                nc.scalar.activation(nqT[:, p, :], ps[:, (J_NQ + p) % 8, :], ACT.Copy, scale=DH ** -0.5).then_inc(read_a, 1)
            act.wait_ge(job_done, J_GC + 1)
            nc.scalar.activation(gcol[:].rearrange("p t h -> p (t h)"), ps[:, J_GC % 8, 0:16], ACT.Copy).then_inc(gcol_ready, 1)
            nc.scalar.activation(emc[:].rearrange("p t h -> p (t h)"), ps[:, J_GC % 8, 16:32], ACT.Exp,
                                 scale=-1.0).then_inc(read_a, 1)
            high_half(10)
            high_half(11)
            high_half(12)
            for p in range(2):
                act.wait_ge(job_done, J_MQ + p + 1)
                nc.scalar.activation(mqT[:, p, :], ps[:, (J_MQ + p) % 8, :], ACT.Copy, scale=DH ** -0.5).then_inc(read_a, 1)
            high_half(13)
            high_half(14)
            act.wait_ge(gcol_ready, 1)
            for h in range(HEADS):
                act.wait_ge(job_done, J_MB + h + 1)
                for j in range(NT):
                    last = nc.scalar.activation(W[:, h, j:NT, j, :],
                                                ps[:, (J_MB + h) % 8, j * P:SEQ].rearrange("p (i t) -> p i t", t=P),
                                                ACT.Exp, scale=-1.0, bias=gcol[:, j, h:h + 1])
                    if j < NT - 1:
                        last.then_inc(w_step, 1)
                    else:
                        last.then_inc(read_a, 1)
                act.wait_ge(read_a, reads(J_MB + h)[1])
                nc.scalar.activation(zero1[:], zero1[:], ACT.Copy).then_inc(w_exp, 1)
                if h == 1:
                    high_half(15)
            high_half(C_WO)
            high_half(C_WO + 1)

            def ml_squares(u):
                p, i = ML_UNITS[u]
                act.wait_ge(ml_used, u + 1)
                for m in range(2):
                    h = 2 * p + m
                    c = SS_ML + HEADS * i + h
                    if 2 * u + m:
                        act.wait_ge(ml_ss, 2 * u + m)
                    nc.scalar.activation(junkb[:, 0:DV], hid[:, i, h, :], ACT.Square,
                                         accum_out=stat[:, c:c + 1]).then_inc(ml_ss, 1)

            for u in range(len(ML_UNITS)):
                if u == 1:
                    act.wait_ge(gelu_arg, 1)
                    nc.scalar.activation(cg[:, 3], cg[:, 2], ACT.Exp, scale=-1.5957691216057308).then_inc(gelu_exp, 1)
                if u == 3:
                    act.wait_ge(kv_cmp, 1)
                    nc.scalar.activation(kcT[:], ps[:, 4, 0:NP_], ACT.Copy).then_inc(kc_ready, 1)
                if u == 5:
                    act.wait_ge(cs_sub, 1)
                    nc.scalar.activation(cexp[:], cexp[:], ACT.Exp).then_inc(cs_exp, 1)
                if u >= 1:
                    ml_squares(u - 1)

            def exps(u):
                for m in range(2):
                    s = 2 * u + m
                    w = (u % NT + 1) * P
                    act.wait_ge(mx_done, s + 1)
                    if s >= 3:
                        act.wait_ge(t_done, s - 2)
                    nc.scalar.activation(probs[:, s % 3, 0:w], ps[:, 2 * (u % 2) + m, 0:w], ACT.Exp,
                                         bias=stat[:, NMAX + s:NMAX + s + 1],
                                         accum_out=stat[:, rsum(u, m):rsum(u, m) + 1]).then_inc(p_ready, 1)

            def copy_t(u):
                g, i = divmod(u, NT)
                act.wait_ge(t_done, 2 * u + 2)
                if i == 0 and g >= 2:
                    act.wait_ge(o_done, g - 1)
                nc.scalar.activation(pT[:, g % 2, 1, 0:i + 1, i * P:(i + 1) * P],
                                     ps[:, 5, 0:(i + 1) * P].rearrange("p (j q) -> p j q", q=P), ACT.Copy).then_inc(pt_a, 1)

            def copy_o(g):
                act.wait_ge(o_done, g + 1)
                if g:
                    act.wait_ge(bt_done, g)
                nc.scalar.activation(oT[:], ps[:, 6, :], ACT.Copy).then_inc(ot_ready, 1)

            def squares(g):
                br, p = PAIRS[g]
                if br == "sel":
                    return
                act.wait_ge(bt_used, g + 1)
                if g > 2:
                    act.wait_ge(y_ss, g - 2)
                y0 = (0 if br == "moba" else 768) + P * p
                nc.scalar.activation(ysq[:].rearrange("p (i d) -> p i d", i=NT), y[:, :, y0:y0 + P],
                                     ACT.Square).then_inc(y_sq_ready, 1)

            def y_high(k):
                c = K_ORDER[k]
                act.wait_ge(yt_done, k + 1)
                nc.scalar.activation(xT_h[:, c, :], ps[:, YT_BANK[k], :], ACT.Copy,
                                     scale=cols[:, 20 + c:21 + c]).then_inc(yh_ready, 1)

            exps(0)
            act.wait_ge(ct_done, 1)
            nc.scalar.activation(cexpT[:].rearrange("p t q -> p (t q)"), ps[:, 4, :], ACT.Copy).then_inc(ct_ready, 1)
            ml_squares(len(ML_UNITS) - 1)
            for u in range(NU):
                g, i = divmod(u, NT)
                if g and i == 3:
                    copy_o(g - 1)
                copy_t(u)
                if u + 1 < NU:
                    exps(u + 1)
                if g >= 2 and i == 1:
                    squares(g - 2)
                if u in (2, 4):
                    high_half(C_WO + 1 + u // 2)
            copy_o(len(PAIRS) - 1)
            squares(len(PAIRS) - 2)
            for k in range(2):
                y_high(k)
            squares(len(PAIRS) - 1)
            for k in range(2, 8):
                y_high(k)

            def hm_high(t):
                for b in range(2):
                    act.wait_ge(hmt_done, 2 * t + b + 1)
                    nc.scalar.activation(xT_h[:, 4 * b:4 * b + 4, t * P:(t + 1) * P],
                                         ps[:, WO_BANK[t] + b, :].rearrange("p (c q) -> p c q", c=4),
                                         ACT.Copy).then_inc(hmh_ready, 1)

            for t in range(NT):
                for half in range(2):
                    act.wait_ge(wo_done, 2 * t + half + 1)
                    if t:
                        act.wait_ge(x1_sq, 2 * t)
                    c = SS_Y + 2 * t + half
                    nc.scalar.activation(junk_w[:, 512 * half:512 * half + 512], ps[:, WO_BANK[t] + half, :], ACT.Square,
                                         accum_out=stat[:, c:c + 1]).then_inc(o_sq, 1)
                act.wait_ge(o_sq, 2 * t + 2)
                act.wait_ge(base_ready, 2 * t + 1)
                root(SS_Y + 2 * t + 1, ROOT + t, stat[:, BASE + 4 * t:BASE + 4 * t + 1])
                if t >= 1:
                    hm_high(t - 1)
                for half in range(2):
                    act.wait_ge(x1_ready, 2 * t + half + 1)
                    c = SS_O + 2 * t + half
                    nc.scalar.activation(junk_w[:, 512 * half:512 * half + 512], xres[:, t, 512 * half:512 * half + 512], ACT.Square,
                                         accum_out=stat[:, c:c + 1]).then_inc(x1_sq, 1)
                act.wait_ge(x1_sq, 2 * t + 2)
                act.wait_ge(base_ready, 2 * t + 2)
                root(SS_O + 2 * t + 1, ROOT + NT + t, stat[:, BASE + 4 * t + 2:BASE + 4 * t + 3])
                if t == NT - 2:
                    high_half(C_MLP)
            hm_high(NT - 1)
            high_half(C_MLP + 1)
            high_half(C_MLP + 2)

            c = C_MLP + 3
            for b in range(NB):
                for f in range(FB):
                    n = FB * b + f
                    act.wait_ge(up_done, n + 1)
                    if n >= 2:
                        act.wait_ge(sq_ready, n - 1)
                    nc.scalar.activation(relu[:, n % 2, :], ps[:, SETS[b % 2][f % 4], :], ACT.Relu).then_inc(relu_ready, 1)
                    act.wait_ge(relu_ready, n + 1)
                    nc.scalar.activation(hT_h[:, f, :], relu[:, n % 2, :], ACT.Square).then_inc(hh_ready, 1)
                    if f % 2 == 1 and c < NCHUNK:
                        high_half(c)
                        c += 1
                for q in range(FB // 2):
                    if c < NCHUNK:
                        high_half(c)
                        c += 1
            for half in range(2):
                for t in range(NT):
                    act.wait_ge(acc_ready, 8 * (NB - 1) + 4 * half + t + 1)
                    if 4 * half + t:
                        act.wait_ge(y_sq, 4 * half + t)
                    cc = SS_Y + 2 * t + half
                    nc.scalar.activation(relu[:, 0, :], y[:, t, 512 * half:512 * half + 512], ACT.Square,
                                         accum_out=stat[:, cc:cc + 1]).then_inc(y_sq, 1)
                    if half:
                        act.wait_ge(y_sq, 4 + t + 1)
                        act.wait_ge(ss0_ready, 1)
                        nc.scalar.activation(stat[:, ROOT + t:ROOT + t + 1], stat[:, cc:cc + 1], ACT.Sqrt, scale=1.0 / D,
                                             bias=stat[:, SS_O + t:SS_O + t + 1]).then_inc(root_done, 1)

        @block.vector
        def _(dve):
            steps = [0]

            def link(ins):
                steps[0] += 1
                ins.then_inc(chain, 1)
                dve.wait_ge(chain, steps[0])

            def rsqrt(ss, r, n, width):
                v, a, yv = stat[:, WK:WK + n], stat[:, WK + 8:WK + 8 + n], stat[:, r:r + n]
                if n > 8:
                    v, a = wide[:, 0:n], wide[:, 16:16 + n]
                link(nc.vector.tensor_scalar(v, stat[:, ss:ss + n], 1.0 / width, EPS, ALU.mult, ALU.add))
                link(nc.vector.tensor_scalar(yv.bitcast(I32), v.bitcast(I32), -0.5, float(0x5f3759df), ALU.mult, ALU.add))
                link(nc.vector.tensor_scalar(v, v, -0.5, None, ALU.mult))
                for k in range(3):
                    if n == 1:
                        link(nc.vector.scalar_tensor_tensor(a, yv, v, yv, ALU.mult, ALU.mult))
                    else:
                        link(nc.vector.tensor_tensor(a, yv, yv, ALU.mult))
                        link(nc.vector.tensor_tensor(a, a, v, ALU.mult))
                    if k < 2:
                        link(nc.vector.scalar_tensor_tensor(yv, a, 1.5, yv, ALU.add, ALU.mult))
                return nc.vector.scalar_tensor_tensor(yv, a, 1.5, yv, ALU.add, ALU.mult)

            def rsqrt1(ss, r, root, n, offset=-0.5 * EPS):
                v, a, yv = stat[:, WK:WK + 1], stat[:, WK + 8:WK + 9], stat[:, r:r + 1]
                dve.wait_ge(root_done, n)
                link(nc.vector.tensor_scalar(v, stat[:, ss:ss + 1], -0.5 / D, offset, ALU.mult, ALU.add))
                link(nc.vector.reciprocal(yv, stat[:, root:root + 1]))
                link(nc.vector.scalar_tensor_tensor(a, yv, v, yv, ALU.mult, ALU.mult))
                return nc.vector.scalar_tensor_tensor(yv, a, 1.5, yv, ALU.add, ALU.mult)

            nc.vector.memset(eps1[:], EPS).then_inc(eps_set, 1)
            link(nc.vector.memset(blk_h[DH:P, :, 0, :].bitcast(F32), 0.0))
            link(nc.vector.memset(blk_h[0:DH, :, 1, :].bitcast(F32), 0.0))
            link(nc.vector.memset(lv1[:, :, :, DV:DV + 1], 1.0))

            def normalise(t):
                link(rsqrt1(SS_X + t, R_X + t, ROOT + t, t + 1))
                if t == 0:
                    dve.wait_ge(gain0_in, 16)
                nc.vector.scalar_tensor_tensor(y[:, t, :], xres[:, t, :], stat[:, R_X + t:R_X + t + 1], gain_a[:],
                                               ALU.mult, ALU.mult).then_inc(hn_ready, 1)

            def chunk_low(c):
                dve.wait_ge(hi_done, c + 1)
                n = size(c) // 2
                r = ring_slot(c)
                nc.vector.tensor_tensor(ring_l[r][:, 0:n], raw[c % RAW][:, 0:n], ring_h[r][:, 0:n].bitcast(F32),
                                        ALU.subtract).then_inc(lo_first, 1)

            def x_low(t):
                for b in range(2):
                    dve.wait_ge(xh_ready, 2 * t + b + 1)
                    nc.vector.tensor_tensor(xT_l[:, 4 * b:4 * b + 4, t * P:(t + 1) * P],
                                            ps[:, 2 * t + b, :].rearrange("p (c q) -> p c q", c=4),
                                            xT_h[:, 4 * b:4 * b + 4, t * P:(t + 1) * P].bitcast(F32),
                                            ALU.subtract).then_inc(xl_ready, 1)

            normalise(0)
            chunk_low(0)
            x_low(0)
            normalise(1)
            chunk_low(1)
            normalise(2)
            x_low(1)
            normalise(3)
            x_low(2)
            x_low(3)

            for t in range(NT):
                dve.wait_ge(job_done, J_B + t + 1)
                nc.vector.tensor_copy(zB[:, t, :], ps[:, (J_B + t) % 8, 0:BN]).then_inc(read_v, 1)

            dve.wait_ge(params_t, 1)
            nc.vector.tensor_copy(cols[:], ps[:, PARAM_BANK, 0:28]).then_inc(params_ready, 1)
            nc.vector.tensor_copy(peT[:], ps[:, PARAM_BANK, 64:96]).then_inc(params_ready, 1)

            def silu(n):
                dve.wait_ge(conv_sig, n + 1)
                nc.vector.scalar_tensor_tensor(qkT[:, n, :], qkT[:, n, :], 1.0 if n < 2 else DH ** -0.5,
                                               sig[:, n % 2, :], ALU.mult, ALU.mult).then_inc(silu_done, 1)

            for n in range(4):
                dve.wait_ge(conv_lin, n + 1)
                for back in (1, 2, 3):
                    ins = nc.vector.scalar_tensor_tensor(
                        qkT[:, n, back:SEQ], ps[:, (J_CONV + n) % 8, 0:SEQ - back],
                        cols[:, 4 * (3 - back) + n:4 * (3 - back) + n + 1], qkT[:, n, back:SEQ], ALU.mult, ALU.add)
                    if back < 3:
                        link(ins)
                    else:
                        ins.then_inc(read_v, 1)
                dve.wait_ge(read_v, reads(J_CONV + n)[1])
                nc.vector.tensor_copy(stat[:, WK:WK + 1], stat[:, WK:WK + 1]).then_inc(conv_acc, 1)
                if n >= 1:
                    silu(n - 1)
            silu(3)
            dve.wait_ge(lf_ready, 1)
            link(nc.vector.tensor_scalar(g_row[:, 1, :], ps[0:HEADS, J_LF % 8, :], gb[:, 1:2], 0.0, ALU.add, ALU.min))
            link(nc.vector.tensor_tensor(g_row[:, 1, :], g_row[:, 1, :], g_row[:, 0, :], ALU.subtract))
            link(nc.vector.tensor_tensor_scan(g_row[:, 0, :], g_row[:, 1, :], zero1[0:HEADS, :].to_broadcast([HEADS, SEQ]),
                                              0.0, ALU.add, ALU.add))
            dve.wait_ge(job_done, J_LI + 1)
            nc.vector.scalar_tensor_tensor(g_row[:, 1, :], ps[0:HEADS, J_LI % 8, :], gb[:, 0:1], g_row[:, 0, :],
                                           ALU.add, ALU.subtract).then_inc(read_v, 1)
            dve.wait_ge(read_v, reads(J_LI)[1])
            link(nc.vector.tensor_tensor_scan(g_row[:, 2, :], g_row[:, 1, :], g_row[:, 1, :], 0.0, ALU.max, ALU.max))
            nc.vector.tensor_tensor(g_row[:, 0, :], g_row[:, 0, :], g_row[:, 2, :], ALU.add).then_inc(read_v, 1)
            dve.wait_ge(silu_done, 4)
            link(nc.vector.memset(blk_l[DH:P, :, 0, :].bitcast(F32), 0.0))
            link(nc.vector.memset(blk_l[0:DH, :, 1, :].bitcast(F32), 0.0))
            dve.wait_ge(blkh_ready, 6)
            for j in range(2):
                rs_ = slice(DH * j, DH * j + DH)
                for a in range(2):
                    src = ps[rs_, J_KV % 8, :].rearrange("p (n b) -> p b n", b=16)[:, :, a:a + NCMP]
                    nc.vector.tensor_tensor(blk_l[rs_, 16 * a:16 * a + 16, j, 0:NCMP], src,
                                            blk_h[rs_, 16 * a:16 * a + 16, j, 0:NCMP].bitcast(F32), ALU.subtract)
                last = nc.vector.tensor_tensor(blk_l[rs_, :, j, NCMP], peT[rs_, :], blk_h[rs_, :, j, NCMP].bitcast(F32),
                                               ALU.subtract)
            last.then_inc(read_v, 1)
            for t in range(NT):
                dve.wait_ge(job_done, J_LV + t + 1)
                nc.vector.tensor_copy(lv1[:, t, :, 0:DV], ps[:, (J_LV + t) % 8, :].rearrange("p (h d) -> p h d", h=HEADS)
                                      ).then_inc(read_v, 1)
            for p in range(2):
                dve.wait_ge(job_done, J_MK + p + 1)
                nc.vector.tensor_copy(mkT[:, p, :], ps[:, (J_MK + p) % 8, :]).then_inc(read_v, 1)
            chunk_low(C_CMP + 3)
            dve.wait_ge(job_done, J_H + 1)
            nc.vector.tensor_copy(hsb[:], ps[0:2 * NP_, J_H % 8, 0:CMP_HID]).then_inc(read_v, 1)
            dve.wait_ge(job_done, J_H + 2)
            nc.vector.tensor_copy(cg[:, 0], ps[:, (J_H + 1) % 8, 0:4 * NP_].rearrange("p (t n) -> p t n", t=2)).then_inc(read_v, 1)

            def gelu():
                dve.wait_ge(read_v, READER.count("v"))
                hv = cg[:, 0].rearrange("p t (j n) -> p (t j) n", n=NP_)
                xv = cg[:, 1].rearrange("p t (j n) -> p (t j) n", n=NP_)
                link(nc.vector.tensor_tensor(xv, hv, hv[:, :, NCMP:NP_].to_broadcast([P, 4, NP_]), ALU.add))
                link(nc.vector.tensor_tensor(cg[:, 2], cg[:, 1], cg[:, 1], ALU.mult))
                link(nc.vector.tensor_scalar(cg[:, 2], cg[:, 2], 0.044715, 1.0, ALU.mult, ALU.add))
                nc.vector.tensor_tensor(cg[:, 2], cg[:, 2], cg[:, 1], ALU.mult).then_inc(gelu_arg, 1)
                dve.wait_ge(gelu_exp, 1)
                link(nc.vector.tensor_scalar(cg[:, 3], cg[:, 3], 1.0, None, ALU.add))
                link(nc.vector.reciprocal(cg[:, 3], cg[:, 3]))
                link(nc.vector.tensor_tensor(gel[:], cg[:, 1], cg[:, 3], ALU.mult))
                gv = gel[:].rearrange("p t (j n) -> p t j n", n=NP_)
                link(nc.vector.memset(gv[:, :, :, NCMP:NP_], 0.0))
                for t in range(2):
                    last = nc.vector.tensor_copy(gelr[:, t], gv[:, t, 1:2, :].to_broadcast([P, HEADS, NP_]))
                last.then_inc(gelu_ready, 1)

            def cmp_values():
                link(nc.vector.memset(vbd[:], 0.0))
                dve.wait_ge(kv_cmp, 2)
                for m in range(2):
                    for p in range(2):
                        r, h = 2 * m + p, 2 * p + m
                        last = nc.vector.tensor_copy(vbd[32 * r:32 * r + 32, DH * h:DH * h + DH],
                                                     ps[32 * r:32 * r + 32, 5, 0:DH])
                last.then_inc(vc_ready, 1)

            def cmp_max():
                dve.wait_ge(cs_done, 1)
                for m in range(2):
                    link(nc.vector.tensor_reduce(wide[:, 32 + 8 * m:40 + 8 * m],
                                                 ps[:, 4 + m, 0:8 * NP_].rearrange("p (a n) -> p a n", n=NP_), AX.X, ALU.max))
                for m in range(2):
                    last = nc.vector.tensor_tensor(
                        cexp[:, :, 2 * m:2 * m + 2, :],
                        ps[:, 4 + m, 0:8 * NP_].rearrange("p (i a n) -> p i a n", i=NT, n=NP_),
                        wide[:, 32 + 8 * m:40 + 8 * m].rearrange("p (i a o) -> p i a o", i=NT, o=1).to_broadcast([P, NT, 2, NP_]),
                        ALU.subtract)
                    if m == 0:
                        link(last)
                last.then_inc(cs_sub, 1)

            def cmp_probs():
                dve.wait_ge(cs_exp, 1)
                link(nc.vector.tensor_reduce(wide[:, 32:48], cexp[:].rearrange("p i a n -> p (i a) n"), AX.X, ALU.add))
                link(nc.vector.reciprocal(wide[:, 32:48], wide[:, 32:48]))
                link(nc.vector.tensor_tensor(cexp[:], cexp[:], vis[:].rearrange("p i (o n) -> p i o n", o=1)
                                             .to_broadcast([P, NT, 4, NP_]), ALU.mult))
                cv = cexp[:].rearrange("p i a n -> p (i a) n")
                nc.vector.tensor_tensor(cv, cv, wide[:, 32:48].rearrange("p (a o) -> p a o", o=1).to_broadcast([P, 16, NP_]),
                                        ALU.mult).then_inc(cs_ready, 1)

            def ml_out(u):
                p, i = ML_UNITS[u]
                dve.wait_ge(ml_o, u + 1)
                if u:
                    dve.wait_ge(ml_used, u)
                ob = ps[:, 6 + u % 2, :].rearrange("p (m d) -> p m d", m=2)
                d = stat[:, WK:WK + 2].rearrange("p (m o) -> p m o", o=1)
                den = ob[:, :, DV:DV + 1]
                link(nc.vector.scalar_tensor_tensor(d, den, -1.0, emc[:, i, 2 * p:2 * p + 2].rearrange("p (m o) -> p m o", o=1),
                                                    ALU.mult, ALU.max))
                link(nc.vector.tensor_tensor(d, den, d, ALU.max))
                link(nc.vector.reciprocal(d, d))
                nc.vector.tensor_tensor(hid[:, i, 2 * p:2 * p + 2, :], ob[:, :, 0:DV], d.to_broadcast([P, 2, DV]),
                                        ALU.mult).then_inc(ml_used, 1)

            def maxes(u, m):
                s = 2 * u + m
                w = (u % NT + 1) * P
                dve.wait_ge(s_done, s + 1)
                nc.vector.tensor_reduce(stat[:, NMAX + s:NMAX + s + 1], ps[:, 2 * (u % 2) + m, 0:w], AX.X, ALU.max,
                                        negate=True).then_inc(mx_done, 1)

            for u, (p, i) in enumerate(ML_UNITS):
                w = (i + 1) * P
                for m in range(2):
                    s, h = 2 * u + m, 2 * p + m
                    dve.wait_ge(ml_s, u + 1)
                    dve.wait_ge(w_ready, h + 1)
                    if s >= 3:
                        dve.wait_ge(ml_o, (s - 3) // 2 + 1)
                    nc.vector.tensor_tensor(probsT[:, s % 3, 0:w], ps[:, 2 * (u % 2) + m, 0:w],
                                            W[:, h, i, 0:i + 1, :].rearrange("p j t -> p (j t)"), ALU.mult).then_inc(ml_p, 1)
                if u == 1:
                    gelu()
                if u == 3:
                    cmp_values()
                if u == 5:
                    cmp_max()
                if u == 6:
                    cmp_probs()
                if u >= 1:
                    ml_out(u - 1)
            maxes(0, 0)
            maxes(0, 1)
            ml_out(len(ML_UNITS) - 1)
            dve.wait_ge(ml_used, len(ML_UNITS))
            for i in range(NT):
                dve.wait_ge(co_done, i // 2 + 1)
                last = nc.vector.tensor_tensor(
                    y[:, i, 768:1024].rearrange("p (h d) -> p h d", h=HEADS),
                    ps[:, 5 - i // 2, 256 * (i % 2):256 * (i % 2) + 256].rearrange("p (h d) -> p h d", h=HEADS),
                    gt[:, i, :].rearrange("p (h b) -> p h b", b=3)[:, :, 0:1].to_broadcast([P, HEADS, DH]), ALU.mult)
            last.then_inc(co_used, 1)

            def copy_t(u):
                g, i = divmod(u, NT)
                dve.wait_ge(t_done, 2 * u + 1)
                if i == 0 and g >= 2:
                    dve.wait_ge(o_done, g - 1)
                nc.vector.tensor_copy(pT[:, g % 2, 0, 0:i + 1, i * P:(i + 1) * P],
                                      ps[:, 4, 0:(i + 1) * P].rearrange("p (j q) -> p j q", q=P)).then_inc(pt_v, 1)

            def coefficients(g):
                br, p = PAIRS[g]
                dve.wait_ge(p_ready, 2 * NT * (g + 1))
                if g:
                    dve.wait_ge(bt_used, g)
                rv = stat[:, WK:WK + 8]
                link(nc.vector.reciprocal(rv, stat[:, rsum(NT * g, 0):rsum(NT * g, 0) + 8]))
                if br != "moba":
                    gates = gt[:].rearrange("p i (h b) -> p i h b", b=3)[:, :, 2 * p:2 * p + 2, 1 if br == "sel" else 2]
                    rv2 = rv.rearrange("p (i m) -> p i m", i=NT)
                    link(nc.vector.tensor_tensor(rv2, rv2, gates, ALU.mult))

            def attn_out(g):
                br, p = PAIRS[g]
                dve.wait_ge(bt_done, g + 1)
                ob = ps[:, 7, :].rearrange("p (a d) -> p a d", d=DH)
                rv = stat[:, WK:WK + 8].rearrange("p (a o) -> p a o", o=1).to_broadcast([P, 8, DH])
                y0 = (0 if br == "moba" else 768) + P * p
                yv = y[:, :, y0:y0 + P]
                if br == "moba":
                    nc.vector.tensor_tensor(yv.rearrange("p i (m d) -> p i m d", m=2),
                                            ob.rearrange("p (i m) d -> p i m d", m=2),
                                            rv.rearrange("p (i m) d -> p i m d", m=2), ALU.mult).then_inc(bt_used, 1)
                else:
                    link(nc.vector.tensor_tensor(work[:].rearrange("p (a d) -> p a d", d=DH), ob, rv, ALU.mult))
                    nc.vector.tensor_tensor(yv, yv, work[:].rearrange("p (i d) -> p i d", i=NT), ALU.add).then_inc(bt_used, 1)

            def head_sums(g):
                br, p = PAIRS[g]
                if br == "sel":
                    return
                dve.wait_ge(y_sq_ready, g - 1)
                c = SS_MB if br == "moba" else SS_NSA
                sums = stat[:, c:c + 16].rearrange("p (i h) -> p i h", h=HEADS)[:, :, 2 * p:2 * p + 2]
                nc.vector.tensor_reduce(sums, ysq[:].rearrange("p (i m d) -> p i m d", i=NT, m=2), AX.X, ALU.add
                                        ).then_inc(y_ss, 1)

            def y_low(k):
                c = K_ORDER[k]
                dve.wait_ge(yh_ready, k + 1)
                nc.vector.scalar_tensor_tensor(xT_l[:, c, :], ps[:, YT_BANK[k], :], cols[:, 20 + c:21 + c],
                                               xT_h[:, c, :].bitcast(F32), ALU.mult, ALU.subtract).then_inc(yl_ready, 1)

            for u in range(NU):
                g, i = divmod(u, NT)
                if u + 1 < NU:
                    maxes(u + 1, 0)
                copy_t(u)
                if u + 1 < NU:
                    maxes(u + 1, 1)
                if g >= 2 and i == 0:
                    attn_out(g - 2)
                if g and i == 1:
                    coefficients(g - 1)
                if g >= 2 and i == 2:
                    head_sums(g - 2)
                if u == 2:
                    dve.wait_ge(ml_ss, 16)
                    rsqrt(SS_ML, R_ML, 16, DV).then_inc(ml_rn, 1)
                    dve.wait_ge(ml_rn, 1)
                if g == N_NSA + 1 and i == 2:
                    dve.wait_ge(y_ss, 2)
                    rsqrt(SS_NSA, R_NSA, 16, DH).then_inc(nsa_rn, 1)
                    dve.wait_ge(nsa_rn, 1)
            last_pair = len(PAIRS) - 1
            attn_out(last_pair - 1)
            coefficients(last_pair)
            attn_out(last_pair)
            head_sums(last_pair - 1)
            for k in range(2):
                y_low(k)
            head_sums(last_pair)
            dve.wait_ge(y_ss, 4)
            link(rsqrt(SS_MB, R_MB, 16, DH))
            ym = y[:, :, 0:256].rearrange("p t (h d) -> p t h d", h=HEADS)
            nc.vector.tensor_tensor(ym, ym, stat[:, R_MB:R_MB + 16].rearrange("p (t h o) -> p t h o", h=HEADS, o=1)
                                    .to_broadcast([P, NT, HEADS, DH]), ALU.mult).then_inc(moba_y, 1)
            for k in range(2, 8):
                y_low(k)

            def hm_low(t):
                for b in range(2):
                    dve.wait_ge(hmh_ready, 2 * t + b + 1)
                    nc.vector.tensor_tensor(xT_l[:, 4 * b:4 * b + 4, t * P:(t + 1) * P],
                                            ps[:, WO_BANK[t] + b, :].rearrange("p (c q) -> p c q", c=4),
                                            xT_h[:, 4 * b:4 * b + 4, t * P:(t + 1) * P].bitcast(F32),
                                            ALU.subtract).then_inc(hml_ready, 1)

            def base(ss, n):
                c = BASE + 2 * n
                link(nc.vector.tensor_scalar(stat[:, c:c + 1], stat[:, ss:ss + 1], 1.0 / D, EPS, ALU.mult, ALU.add))
                nc.vector.tensor_scalar(stat[:, c + 1:c + 2], stat[:, c:c + 1], -0.5, None, ALU.mult).then_inc(base_ready, 1)

            for t in range(NT):
                if t == 0:
                    dve.wait_ge(gain1_in, 16)
                    dve.wait_ge(gain2_in, 16)
                if t >= 2:
                    dve.wait_ge(hmt_done, 2 * t - 2)
                for half in range(2):
                    dve.wait_ge(o_sq, 2 * t + half + 1)
                    if half == 0:
                        base(SS_Y + 2 * t, 2 * t)
                    h = slice(512 * half, 512 * half + 512)
                    link(nc.vector.tensor_tensor(ow[:, t % 2, h], ps[:, WO_BANK[t] + half, :], gain_a[:, h], ALU.mult))
                    if half == 0 and t == NT - 1:
                        chunk_low(C_MLP)
                dve.wait_ge(base_ready, 2 * t + 1)
                c = BASE + 4 * t + 1
                link(rsqrt1(SS_Y + 2 * t + 1, R_O + t, ROOT + t, NT + 2 * t + 1, stat[:, c:c + 1]))
                for half in range(2):
                    h = slice(512 * half, 512 * half + 512)
                    nc.vector.scalar_tensor_tensor(xres[:, t, h], ow[:, t % 2, h], stat[:, R_O + t:R_O + t + 1], xres[:, t, h],
                                                   ALU.mult, ALU.add).then_inc(x1_ready, 1)
                dve.wait_ge(x1_sq, 2 * t + 1)
                base(SS_O + 2 * t, 2 * t + 1)
                dve.wait_ge(base_ready, 2 * t + 2)
                c = BASE + 4 * t + 3
                link(rsqrt1(SS_O + 2 * t + 1, R_X1 + t, ROOT + NT + t, NT + 2 * t + 2, stat[:, c:c + 1]))
                dve.wait_ge(x1_ready, 2 * t + 2)
                for half in range(2):
                    h = slice(512 * half, 512 * half + 512)
                    nc.vector.scalar_tensor_tensor(ow[:, t % 2, h], xres[:, t, h], stat[:, R_X1 + t:R_X1 + t + 1], gain_b[:, h],
                                                   ALU.mult, ALU.mult).then_inc(hm_ready, 1)
                if t >= 1:
                    hm_low(t - 1)
            hm_low(NT - 1)

            def finish(t):
                dve.wait_ge(acc_ready, 8 * (NB - 1) + 4 + t + 1)
                if t == 0:
                    dve.wait_ge(gain3_in, 16)
                if t >= 2:
                    dve.wait_ge(res_ready, 2 * t - 3)
                nc.vector.tensor_tensor(sq[:, t % 2, :], y[:, t, 512:1024], gain_a[:, 512:1024], ALU.mult).then_inc(yg_ready, 1)
                link(rsqrt1(SS_Y + 2 * t + 1, R_Y + t, ROOT + t, 3 * NT + t + 1, stat[:, SS_X1 + t:SS_X1 + t + 1]))
                dve.wait_ge(yg_ready, NT + t + 1)
                for half in (1, 0):
                    src = sq[:, t % 2, :] if half else yg[:, t, :]
                    xv = xres[:, t, 512 * half:512 * half + 512]
                    nc.vector.scalar_tensor_tensor(xv, src, stat[:, R_Y + t:R_Y + t + 1], xv, ALU.mult, ALU.add
                                                   ).then_inc(res_ready, 1)

            for b in range(NB):
                for f in range(FB):
                    n = FB * b + f
                    dve.wait_ge(relu_ready, n + 1)
                    nc.vector.tensor_tensor(sq[:, n % 2, :], relu[:, n % 2, :], relu[:, n % 2, :], ALU.mult).then_inc(sq_ready, 1)
                    dve.wait_ge(sq_ready, n + 1)
                    dve.wait_ge(hh_ready, n + 1)
                    nc.vector.tensor_tensor(hT_l[:, f, :], sq[:, n % 2, :], hT_h[:, f, :].bitcast(F32),
                                            ALU.subtract).then_inc(hl_ready, 1)
                for half in range(2):
                    banks = SETS[(b + 1 + half) % 2]
                    for t in range(NT):
                        n = 8 * b + 4 * half + t
                        dve.wait_ge(down_done, n + 1)
                        ya = y[:, t, 512 * half:512 * half + 512]
                        if b == 0:
                            nc.vector.tensor_copy(ya, ps[:, banks[t], :]).then_inc(acc_ready, 1)
                        else:
                            dve.wait_ge(acc_ready, n - 7)
                            nc.vector.tensor_tensor(ya, ps[:, banks[t], :], ya, ALU.add).then_inc(acc_ready, 1)
                        if b == NB - 1 and half:
                            finish(t)
                    if b == NB - 1 and half == 0:
                        dve.wait_ge(y_sq, NT)
                        ss0 = stat[:, SS_Y:SS_Y + 2 * NT].rearrange("p (t a) -> p t a", a=2)[:, :, 0]
                        link(nc.vector.tensor_scalar(stat[:, SS_O:SS_O + NT], ss0, 1.0 / D, EPS, ALU.mult, ALU.add))
                        link(nc.vector.tensor_scalar(stat[:, SS_X1:SS_X1 + NT], stat[:, SS_O:SS_O + NT], -0.5, None, ALU.mult))
                        nc.vector.memset(zero1[:], 0.0).then_inc(ss0_ready, 1)

        @block.tensor
        def _(pe):
            def mm3(o, sh, sl, mh, ml, start, stop):
                nc.tensor.matmul(o, sh, mh, start=start, stop=False)
                nc.tensor.matmul(o, sh, ml, start=False, stop=False)
                return nc.tensor.matmul(o, sl, mh, start=False, stop=stop)

            def bank_free(n):
                if n >= 8:
                    pe.wait_ge(*reads(n - 8))

            def chunk(c):
                pe.wait_ge(lo_done, c + 1)
                if c in SHARED:
                    pe.wait_ge(lo_first, SHARED.index(c) + 1)
                r = ring_slot(c)
                return grid(ring_h[r], c), grid(ring_l[r], c)

            def x_transposes(t):
                pe.wait_ge(hn_ready, t + 1)
                for c in range(NC):
                    last = nc.tensor.transpose(ps[:, 2 * t + c // 4, (c % 4) * P:(c % 4) * P + P], y[:, t, c * P:(c + 1) * P], ident[:])
                last.then_inc(xt_done, 1)

            def first_group():
                pe.wait_ge(consts, 2)
                x_transposes(0)
                for t in range(NT):
                    pe.wait_ge(xl_ready, 2 * t + 2)
                    for q in range(2):
                        wh, wl = chunk(C_B + q)
                        for k in range(4):
                            kk = 4 * q + k
                            last = mm3(ps[:, (J_B + t) % 8, 0:BN], xT_h[:, kk, t * P:(t + 1) * P], xT_l[:, kk, t * P:(t + 1) * P],
                                       wh[:, k, :], wl[:, k, :], kk == 0, kk == NC - 1)
                        if q == 1:
                            last.then_inc(job_done, 1)
                        elif t == NT - 1:
                            last.then_inc(part_used, 1)
                        if q == 0 and t < NT - 1:
                            x_transposes(t + 1)

            def token_group(j0, c0, n):
                for q in range(2):
                    wh, wl = chunk(c0 + q)
                    for t in range(NT):
                        if q == 0:
                            bank_free(j0 + t)
                        for k in range(4):
                            kk = 4 * q + k
                            last = mm3(ps[:, (j0 + t) % 8, 0:n], xT_h[:, kk, t * P:(t + 1) * P], xT_l[:, kk, t * P:(t + 1) * P],
                                       wh[:, k, :], wl[:, k, :], kk == 0, kk == NC - 1)
                        if q == 1:
                            last.then_inc(job_done, 1)
                        elif t == NT - 1:
                            last.then_inc(part_used, 1)

            def feature_group(j0, c):
                wh, wl = chunk(c)
                for j in range(2):
                    bank_free(j0 + j)
                    if j0 + j == PARAM_BANK:
                        pe.wait_ge(params_ready, 2)
                    for k in range(NC):
                        last = mm3(ps[:, (j0 + j) % 8, :], wh[:, k, j * P:(j + 1) * P], wl[:, k, j * P:(j + 1) * P],
                                   xT_h[:, k, :], xT_l[:, k, :], k == 0, k == NC - 1)
                    last.then_inc(job_done, 1)

            first_group()
            pe.wait_ge(consts, 13)
            pe.wait_ge(small_in, 16 * 8)
            nc.tensor.transpose(ps[:, PARAM_BANK, 0:28], rows[:], ident[0:28, 0:28])
            nc.tensor.transpose(ps[:, PARAM_BANK, 64:96], pe_rows[:], ident[0:32, 0:32]).then_inc(params_t, 1)
            feature_group(J_CONV, C_LQ)
            feature_group(J_CONV + 2, C_LK)
            token_group(J_LO, C_LO, 512)
            pe.wait_ge(read_v, J_B + NT)
            for job, b0 in ((J_LI, BI), (J_LF, BF)):
                bank_free(job)
                for t in range(NT):
                    last = nc.tensor.transpose(ps[0:HEADS, job % 8, t * P:(t + 1) * P], zB[:, t, b0:b0 + HEADS], ident[:])
                last.then_inc(job_done, 1)
            feature_group(J_KV, C_KVS)
            feature_group(J_NQ, C_NQ)
            bank_free(J_GC)
            pe.wait_ge(read_v, reads(J_LF)[1])
            for k, r in enumerate((1, 0)):
                for t in range(NT):
                    c = 16 * k + HEADS * t
                    last = nc.tensor.transpose(ps[:, J_GC % 8, c:c + HEADS], g_row[:, r, t * P:(t + 1) * P], ident[0:HEADS, 0:HEADS])
            last.then_inc(job_done, 1)
            token_group(J_LV, C_LV, 512)
            feature_group(J_MQ, C_MQ)
            feature_group(J_MK, C_MK)
            for h in range(HEADS):
                bank_free(J_MB + h)
                nc.tensor.matmul(ps[:, (J_MB + h) % 8, :], sel[:, h, :], g_row[:, 2, :], start=True, stop=True).then_inc(job_done, 1)
            bank_free(J_H)
            for q in range(4):
                wh, wl = chunk(C_CMP + q)
                for k in range(8):
                    l = 8 * q + k
                    bh, bl = blk_h[:, l].rearrange("p j n -> p (j n)"), blk_l[:, l].rearrange("p j n -> p (j n)")
                    last = mm3(ps[0:2 * NP_, J_H % 8, 0:CMP_HID], bh, bl, wh[:, k, :], wl[:, k, :], l == 0, l == CMP_LEN - 1)
                last.then_inc(job_done if q == 3 else part_used, 1)
            bank_free(J_H + 1)
            pe.wait_ge(read_v, reads(J_H)[1])
            for t in range(2):
                last = nc.tensor.transpose(ps[:, (J_H + 1) % 8, 2 * NP_ * t:2 * NP_ * (t + 1)],
                                           hsb[:, t * P:(t + 1) * P], ident[0:2 * NP_, 0:2 * NP_])
            last.then_inc(job_done, 1)

            def ml_scores(u):
                p, i = ML_UNITS[u]
                if u >= 2:
                    pe.wait_ge(ml_p, 2 * u - 2)
                for j in range(i + 1):
                    for m in range(2):
                        r = slice(DH * m, DH * m + DH)
                        last = nc.tensor.matmul(ps[:, 2 * (u % 2) + m, j * P:(j + 1) * P], qkT[r, 2 + p, j * P:(j + 1) * P],
                                                qkT[r, p, i * P:(i + 1) * P], start=True, stop=True)
                last.then_inc(ml_s, 1)

            def ml_values(u):
                p, i = ML_UNITS[u]
                pe.wait_ge(ml_p, 2 * u + 2)
                if u >= 2:
                    pe.wait_ge(ml_used, u - 1)
                for m in range(2):
                    for j in range(i + 1):
                        last = nc.tensor.matmul(ps[:, 6 + u % 2, 256 * m:256 * m + DV + 1],
                                                probsT[:, (2 * u + m) % 3, j * P:(j + 1) * P],
                                                lv1[:, j, 2 * p + m, :], start=(j == 0), stop=(j == i))
                last.then_inc(ml_o, 1)

            keys = {"sel": kselT, "win": kwinT}

            def scores(u):
                g, i = divmod(u, NT)
                br, p = PAIRS[g]
                if u >= 2:
                    pe.wait_ge(p_ready, 2 * u - 2)
                w = (i + 1) * P
                for m in range(2):
                    r = slice(DH * m, DH * m + DH)
                    q = (mqT if br == "moba" else nqT)[r, p, i * P:(i + 1) * P]
                    k = mkT[r, p, 0:w] if br == "moba" else keys[br][r, 0:w]
                    nc.tensor.matmul(ps[:, 2 * (u % 2) + m, 0:w], q, k, start=True, stop=True)
                for m in range(2):
                    nc.tensor.matmul(ps[:, 2 * (u % 2) + m, w - P:w], identb[:], mask_s[:], start=False,
                                     stop=True, skip_group_check=True).then_inc(s_done, 1)

            pe.wait_ge(read_v, READER.count("v"))
            pe.wait_ge(read_a, READER.count("a"))
            pe.wait_ge(silu_done, 4)
            ml_scores(0)
            for u in range(len(ML_UNITS)):
                if u + 1 < len(ML_UNITS):
                    ml_scores(u + 1)
                ml_values(u)
                if u == 2:
                    pe.wait_ge(gelu_ready, 1)
                    for t in range(2):
                        last = nc.tensor.matmul(ps[:, 4, 0:NP_], w2k[:, t].rearrange("p s d -> p (s d)"), gel[:, t, 0:NP_],
                                                start=(t == 0), stop=(t == 1))
                    last.then_inc(kv_cmp, 1)
                    for t in range(2):
                        last = nc.tensor.matmul(ps[:, 5, 0:DH], gelr[:, t].rearrange("p h n -> p (h n)"), w2v[:, t, :],
                                                start=(t == 0), stop=(t == 1))
                    last.then_inc(kv_cmp, 1)
                if u == 4:
                    pe.wait_ge(kc_ready, 1)
                    pe.wait_ge(vc_ready, 1)
                    for m in range(2):
                        nc.tensor.matmul(ps[:, 4 + m, 0:8 * NP_], identb[:], mask_c[:].rearrange("p i a n -> p (i a n)"),
                                         start=True, stop=True)
                    for i in range(NT):
                        for p in range(2):
                            for m in range(2):
                                r = slice(DH * m, DH * m + DH)
                                c = (2 * i + p) * NP_
                                last = nc.tensor.matmul(ps[:, 4 + m, c:c + NP_], nqT[r, p, i * P:(i + 1) * P], kcT[r, :],
                                                        start=False, stop=True, skip_group_check=True)
                    last.then_inc(cs_done, 1)
                if u == 6:
                    pe.wait_ge(dup_in, 32)
                    pe.wait_ge(ml_p, 14)
                    scores(0)
                if u == 7:
                    scores(1)
                    pe.wait_ge(cs_ready, 1)
                    for i in range(NT):
                        last = nc.tensor.transpose(ps[:, 4, i * P:(i + 1) * P], cexp[:, i].rearrange("p a n -> p (a n)"), ident[:])
                    last.then_inc(ct_done, 1)
            pe.wait_ge(ct_ready, 1)
            for i in range(NT):
                last = nc.tensor.matmul(ps[:, 5 - i // 2, 256 * (i % 2):256 * (i % 2) + 256], cexpT[:, i, :], vbd[:],
                                        start=True, stop=True)
                if i % 2 == 1:
                    last.then_inc(co_done, 1)

            def transposes(u):
                for m in range(2):
                    s = 2 * u + m
                    pe.wait_ge(p_ready, s + 1)
                    if u >= 1:
                        pe.wait_ge(pt_a if m else pt_v, u)
                    for j in range(u % NT + 1):
                        last = nc.tensor.transpose(ps[:, 4 + m, j * P:(j + 1) * P], probs[:, s % 3, j * P:(j + 1) * P], ident[:])
                    last.then_inc(t_done, 1)

            def values(g):
                br, p = PAIRS[g]
                pe.wait_ge(pt_v, NT * (g + 1))
                pe.wait_ge(pt_a, NT * (g + 1))
                if g:
                    pe.wait_ge(ot_ready, g)
                for m in range(2):
                    v0 = {"sel": BS, "win": BW, "moba": BV + DH * (2 * p + m)}[br]
                    for j in range(NT):
                        last = nc.tensor.matmul(ps[DH * m:DH * m + DH, 6, j * P:SEQ], zB[:, j, v0:v0 + DH],
                                                pT[:, g % 2, m, j, j * P:SEQ], start=(j == 0), stop=True,
                                                skip_group_check=(j > 0))
                last.then_inc(o_done, 1)

            def back(g):
                pe.wait_ge(ot_ready, g + 1)
                if g:
                    pe.wait_ge(bt_used, g)
                for i in range(NT):
                    last = nc.tensor.transpose(ps[:, 7, i * P:(i + 1) * P], oT[:, i * P:(i + 1) * P], ident[:])
                last.then_inc(bt_done, 1)

            def y_transposes(k):
                c = K_ORDER[k]
                for t in range(NT):
                    last = nc.tensor.transpose(ps[:, YT_BANK[k], t * P:(t + 1) * P], y[:, t, c * P:(c + 1) * P], ident[:])
                last.then_inc(yt_done, 1)

            pe.wait_ge(co_used, 1)
            pe.wait_ge(ml_used, len(ML_UNITS))
            for u in range(NU):
                g, i = divmod(u, NT)
                if 0 < u < NU - 1:
                    scores(u + 1)
                if g and i == 3:
                    values(g - 1)
                transposes(u)
                if g and i == 3:
                    back(g - 1)
            values(len(PAIRS) - 1)

            def project(t, half, k_lo, k_hi):
                for k in range(k_lo, k_hi):
                    kset, kk = divmod(k, 4)
                    wh, wl = grid(ring_h[ring_slot(C_WO + 2 * kset + half)], C_WO), grid(ring_l[ring_slot(C_WO + 2 * kset + half)], C_WO)
                    c = K_ORDER[k]
                    last = mm3(ps[:, WO_BANK[t] + half, :], xT_h[:, c, t * P:(t + 1) * P], xT_l[:, c, t * P:(t + 1) * P],
                               wh[:, kk, :], wl[:, kk, :], k == 0, k == NC - 1)
                    if t == NT - 1 and k == 3:
                        last.then_inc(part_used, 1)
                if k_hi == NC:
                    last.then_inc(wo_done, 1)

            def hm_transposes(t):
                for b in range(2):
                    pe.wait_ge(hm_ready, 2 * t + b + 1)
                    for c in range(4):
                        last = nc.tensor.transpose(ps[:, WO_BANK[t] + b, c * P:c * P + P],
                                                   ow[:, t % 2, (4 * b + c) * P:(4 * b + c + 1) * P], ident[:])
                    last.then_inc(hmt_done, 1)

            pe.wait_ge(lo_done, C_WO + 4)
            pe.wait_ge(ml_y, 2)
            pe.wait_ge(pt_v, NU)
            pe.wait_ge(pt_a, NU)
            y_transposes(0)
            y_transposes(1)
            back(len(PAIRS) - 1)
            y_transposes(2)
            y_transposes(3)
            for k in range(4):
                pe.wait_ge(yl_ready, k + 1)
                project(0, 0, k, k + 1)
                project(0, 1, k, k + 1)
                if k == 1:
                    pe.wait_ge(nsa_y, 1)
                    y_transposes(4)
                    y_transposes(5)
            for k in range(4, NC):
                if k == 6:
                    pe.wait_ge(moba_y, 1)
                    y_transposes(6)
                    y_transposes(7)
                pe.wait_ge(yl_ready, k + 1)
                project(0, 0, k, k + 1)
                project(0, 1, k, k + 1)
            for t in range(1, NT):
                project(t, 0, 0, NC)
                project(t, 1, 0, NC)
                hm_transposes(t - 1)
            wh, wl = chunk(C_MLP)
            pe.wait_ge(hml_ready, 2 * EARLY_T)
            for f in range(EARLY_F):
                for k in range(NC):
                    last = mm3(ps[:, SETS[0][f], 0:EARLY_T * P], wh[:, k, f * P:f * P + P], wl[:, k, f * P:f * P + P],
                               xT_h[:, k, 0:EARLY_T * P], xT_l[:, k, 0:EARLY_T * P], k == 0, k == NC - 1)
                    if f == EARLY_F - 1 and k == 3:
                        hm_transposes(NT - 1)
            pe.wait_ge(hml_ready, 2 * NT)

            for b in range(NB):
                c0 = C_MLP + PER_BLOCK * b
                for f in range(FB):
                    n = FB * b + f
                    wh, wl = chunk(c0 + f // 2)
                    if f >= 4:
                        pe.wait_ge(relu_ready, n - 3)
                    elif b >= 1:
                        pe.wait_ge(acc_ready, 8 * (b - 1) + f + 1)
                    t0 = EARLY_T * P if n < EARLY_F else 0
                    for k in range(NC):
                        last = mm3(ps[:, SETS[b % 2][f % 4], t0:SEQ], wh[:, k, (f % 2) * P:(f % 2) * P + P], wl[:, k, (f % 2) * P:(f % 2) * P + P],
                                   xT_h[:, k, t0:SEQ], xT_l[:, k, t0:SEQ], k == 0, k == NC - 1)
                    last.then_inc(up_done, 1)
                def down_tile(t, q, half, banks, wh, wl):
                    for k in range(4):
                        f = 4 * q + k
                        last = mm3(ps[:, banks[t], :], hT_h[:, f, t * P:(t + 1) * P], hT_l[:, f, t * P:(t + 1) * P],
                                   wh[:, k, :], wl[:, k, :], f == 0, f == FB - 1)
                    return last

                for half in range(2):
                    banks = SETS[(b + 1 + half) % 2]
                    if b == NB - 1 and half == 1:
                        pe.wait_ge(relu_ready, FB * b + FB)
                        both = [chunk(c0 + FB // 2 + 2 * half + q) for q in range(2)]
                        for t in range(NT):
                            for q in range(2):
                                last = down_tile(t, q, half, banks, *both[q])
                            last.then_inc(down_done, 1)
                        continue
                    for q in range(2):
                        wh, wl = chunk(c0 + FB // 2 + 2 * half + q)
                        for t in range(NT):
                            if q == 0 and half == 0 and b >= 1:
                                pe.wait_ge(acc_ready, 8 * (b - 1) + 4 + t + 1)
                            if q == 0 and half == 1:
                                pe.wait_ge(relu_ready, FB * b + FB)
                            for k in range(4):
                                f = 4 * q + k
                                if t == 0 and half == 0:
                                    pe.wait_ge(hl_ready, FB * b + f + 1)
                                last = mm3(ps[:, banks[t], :], hT_h[:, f, t * P:(t + 1) * P], hT_l[:, f, t * P:(t + 1) * P],
                                           wh[:, k, :], wl[:, k, :], f == 0, f == FB - 1)
                            if q == 1:
                                last.then_inc(down_done, 1)
                            elif t == NT - 1:
                                last.then_inc(part_used, 1)


_INS = ["x", "norm_g", "w_in", "mlstm_conv_w", "mlstm_conv_b", "mlstm_gate_b", "nsa_cmp_pe", "nsa_cmp_w1",
        "nsa_cmp_w2", "head_g", "w_out", "w_mlp1", "w_mlp2"]


def kernel(**inputs):
    import numpy as np
    import concourse.bacc as bacc
    from concourse.bass_utils import run_bass_kernel_spmd

    nc = bacc.Bacc("TRN2", target_bir_lowering=False, num_devices=1)
    arrays, args = {}, []
    for name in _INS:
        a = np.ascontiguousarray(inputs[name])
        arrays[f"in_{name}"] = a
        args.append(nc.dram_tensor(f"in_{name}", a.shape, mybir.dt.from_np(a.dtype), kind="ExternalInput").ap())
    o = nc.dram_tensor("out_0", (1, SEQ, D), F32, kind="ExternalOutput").ap()
    build(nc, *args, o)
    r = run_bass_kernel_spmd(nc, [arrays], core_ids=[0])
    return r.results[0]["out_0"]
```

```python
from contextlib import ExitStack

import concourse.bass as bass
from concourse import mybir

ALU = mybir.AluOpType
ACT = mybir.ActivationFunctionType
AX = mybir.AxisListType
F32 = mybir.dt.float32
F32R = mybir.dt.float32r
BF16 = mybir.dt.bfloat16
I32 = mybir.dt.int32

P = 128
SEQ = 512
D = 1024
NT = SEQ // P
NC = D // P
DH = 64
DV = 128
HEADS = 4
FF = 4 * D
EPS = 1e-6
NEG = -1e30
CMP_STRIDE, CMP_LEN, CMP_HID = 16, 32, 256
NCMP = (SEQ - CMP_LEN) // CMP_STRIDE + 1
NP_ = NCMP + 1

MQ, MK, MV, LQ, LK, LV, LO, LI, LF, NQ, KC, VC, KSL, VSL, KWN, VWN, NG, DIN = (
    0, 256, 512, 768, 1024, 1280, 1792, 2304, 2308, 2312, 2568, 2632, 2696, 2760, 2824, 2888, 2952, 2964)
BV, BS, BW, BG, BI, BF, BN = 0, 256, 320, 384, 396, 400, 404

CHUNK = 2048
RAW = 2

C_B, C_LQ, C_LK, C_LO, C_KVS, C_NQ, C_LV, C_MQ, C_MK, C_CMP, C_WO, C_MLP = 0, 2, 3, 4, 6, 7, 8, 10, 11, 12, 16, 20
FB = 8
NB = FF // P // FB
PER_BLOCK = FB // 2 + FB // 2
NCHUNK = C_MLP + NB * PER_BLOCK

J_B, J_CONV, J_LO, J_LI, J_LF, J_KV, J_KS, J_NQ, J_GC, J_LV, J_MQ, J_MK, J_MB, J_H = (
    0, 4, 8, 12, 13, 14, 15, 16, 18, 19, 23, 25, 27, 31)
NJOB = 33
HT_BANK = 4
PARAM_BANK = 7
READER = "vvvv" "vvvv" "aaaa" "v" "v" "v" "a" "aa" "a" "vvvv" "aa" "vv" "aaaa" "vv"

K_ORDER = [2, 3, 4, 5, 6, 7, 0, 1]
PAIRS = [("sel", 0), ("sel", 1), ("win", 0), ("win", 1), ("moba", 0), ("moba", 1)]
SHARED = (0, 1, C_CMP + 3, C_MLP)
N_NSA = 4
NU = NT * len(PAIRS)
ML_UNITS = [(p, i) for p in range(2) for i in range(NT)]
ML_BANK = [2, 0]
S_BANK = [2, 3, 0, 1, 7]
O_BANK = [6, 6, 6, 6, 6, 7]
WO_BANK = [0, 6, 2, 4]
YT_BANK = [1, 2, 3, 2, 4, 5, 3, 2]
CT_S, CO_S = 1, (3, 6)
MB_ORDER = [("k", 0), ("k", 1), ("q", 0), ("q", 1), ("k", 2), ("k", 3), ("q", 2), ("q", 3)]
MB_UNITS = [7, 8, 9, 10, 11, 12]
EARLY_F, EARLY_T = 4, 2
SETS = [(0, 1, 6, 7), (2, 3, 4, 5)]


def ring_slot(c):
    return c % 3 if c < C_WO + 3 else [1, 2, 0, 3][(c - C_WO) % 4]


def ring_previous(c):
    return c - 3 if c < C_WO + 3 else c - 4


def build(nc, x, norm_g, w_in, conv_w, conv_b, gate_b, cmp_pe, cmp_w1, cmp_w2, head_g, w_out, w1, w2, out):
    ctx = ExitStack()
    with ctx:
        base = (nc.sbuf_base + 63) // 64 * 64
        cursor = [base]

        def at(name, shape, dt, offset):
            return nc.alloc_sbuf_tensor_at(name, shape, dt, offset=offset)

        def put(name, shape, dt):
            size = 2 if dt == BF16 else 4
            for d in shape[1:]:
                size *= d
            size = (size + 63) // 64 * 64
            cursor[0] += size
            return at(name, shape, dt, cursor[0] - size)

        raw = [put(f"raw{r}", [P, CHUNK], F32) for r in range(RAW)]
        ring_h = [put(f"ring_h{r}", [P, CHUNK], F32R) for r in range(3)]
        ring_l = [put(f"ring_l{r}", [P, CHUNK], F32R) for r in range(3)]
        o_xt = cursor[0]
        xT_h = put("xT_h", [P, NC, SEQ], F32R)
        xT_l = put("xT_l", [P, NC, SEQ], F32R)
        W = at("W", [P, 2, NT, NT + 1, P], F32, o_xt)
        pT = at("pT", [P, 2, NT, NT + 1, P], F32, o_xt)
        nq_st = at("nq_st", [P, HEADS, SEQ], F32R, o_xt + 20480)
        nk_st = at("nk_st", [P, 2, SEQ], F32R, o_xt + 28672)
        xres = put("xres", [P, NT, D], F32)
        gain_a = put("gain_a", [P, D], F32)
        ident = put("ident", [P, P], F32)
        identb = put("identb", [P, P], BF16)
        mask_s = put("mask_s", [P, P], BF16)
        mask_c = put("mask_c", [P, NT, 2, NP_], BF16)
        vis = put("vis", [P, NT], F32)
        rows = put("rows", [28, P], F32)
        cols = put("cols", [P, 28], F32)
        pe_rows = put("pe_rows", [CMP_LEN, P], F32)
        gb = put("gb", [HEADS, 2], F32)
        w2k = put("w2k", [P, 2, 2, DH], F32)
        w2v = put("w2v", [P, 2, DH], F32)
        peT = put("peT", [P, CMP_LEN], F32)
        junkb = put("junkb", [P, DV], F32)
        wide = put("wide", [P, 48], F32)
        zero1 = put("zero1", [P, 1], F32)
        eps1 = put("eps1", [P, 1], F32)
        stat = put("stat", [P, 256], F32)
        gt = put("gt", [P, NT, 12], F32)
        gcol = put("gcol", [P, NT, HEADS], F32)
        emc = put("emc", [P, NT, HEADS], F32)
        kcT = put("kcT", [P, NP_], F32)
        gel = put("gel", [P, 2, 2 * NP_], F32)
        gelr = put("gelr", [P, 2, HEADS, NP_], F32)
        o_cg = cursor[0]
        cg = put("cg", [P, 4, 2, 2 * NP_], F32)
        hsb = at("hsb", [2 * NP_, CMP_HID], F32, o_cg + 1024)
        sel = at("sel", [HEADS, HEADS, P], F32R, o_cg)

        o_a = cursor[0]
        lv1 = at("lv1", [P, NT, HEADS, DV + 1], F32, o_a)
        qkT = at("qkT", [P, 4, SEQ], F32, o_a + 8320)
        ring_h.append(at("ring_h3", [P, CHUNK], F32R, o_a))
        ring_l.append(at("ring_l3", [P, CHUNK], F32R, o_a + 8320))
        y = at("y", [P, NT, D], F32, o_a + 16512)
        o_m = o_a + 32896
        mqT = at("mqT", [P, 2, SEQ], F32, o_m)
        mkT = at("mkT", [P, 2, SEQ], F32, o_m + 4096)
        nqT = at("nqT", [P, 2, SEQ], F32, o_m + 8192)
        gain_b = at("gain_b", [P, D], F32, o_m + 8192)
        mq_lo, mk_lo = at("mq_lo", [P, 2, SEQ], F32R, o_m), at("mk_lo", [P, 2, SEQ], F32R, o_m + 4096)
        nk_lo = at("nk_lo", [P, 2, SEQ], F32R, o_m + 12288)
        kselT = at("kselT", [P, SEQ], F32, o_m + 12288)
        kwinT = at("kwinT", [P, SEQ], F32, o_m + 14336)
        zB = at("zB", [P, NT, BN], F32, o_m + 16384)
        hid = at("hid", [P, NT, HEADS, DV], F32, o_m + 22848)
        blk_h = at("blk_h", [P, CMP_LEN, 2, NP_], F32R, o_m + 22848)
        mq_st = at("mq_st", [P, HEADS, SEQ], F32R, o_m + 22848)
        o_p = o_m + 31040
        probs = at("probs", [P, 3, SEQ], F32, o_p)
        probsT = at("probsT", [P, 3, SEQ], F32, o_p + 6144)
        blk_l = at("blk_l", [P, CMP_LEN, 2, NP_], F32R, o_p)
        sig = at("sig", [P, 2, SEQ], F32, o_p)
        oT = at("oT", [P, SEQ], F32, o_p + 6144)
        work = at("work", [P, SEQ], F32, o_p + 8192)
        ysq = at("ysq", [P, SEQ], F32, o_p + 10240)
        junk = at("junk", [P, D], F32, o_p + 8192)
        o_r = o_p + 12288
        g_row = at("g_row", [HEADS, 3, SEQ], F32, o_r)
        m_split = at("m_split", [HEADS, 2, SEQ], F32R, o_r)
        nq_lo = at("nq_lo", [P, 2, SEQ], F32R, o_r)
        mk_st = [at("mk_st0", [P, 2, SEQ], F32R, o_m + 8192), at("mk_st1", [P, 2, SEQ], F32R, o_r)]
        junk_w = at("junk_w", [P, D], F32, o_m)
        cexp = at("cexp", [P, NT, 4, NP_], F32, o_r)
        cexpT = at("cexpT", [P, NT, P], F32, o_r + 2048)
        vbd = at("vbd", [P, HEADS * DH], F32, o_r + 4096)
        hT_h = at("hT_h", [P, FB, SEQ], F32R, o_m)
        hT_l = at("hT_l", [P, FB, SEQ], F32R, o_m + 16384)
        ow = at("ow", [P, 2, D], F32, o_m + 32768)
        relu = at("relu", [P, 2, SEQ], F32, o_m + 40960)
        sq = at("sq", [P, 2, SEQ], F32, o_m + 45056)
        yg = at("yg", [P, NT, D // 2], F32, o_m + 32768)
        assert o_r + 6144 <= nc.sbuf_usable_end and o_m + 49152 <= nc.sbuf_usable_end, (o_r + 6144, nc.sbuf_usable_end)

        ps = ctx.enter_context(nc.psum_tensor("ps", [P, 8, 512], F32))

        SS_X, SS_ML, SS_NSA, SS_MB, SS_O, SS_X1, SS_Y = 0, 4, 20, 36, 52, 56, 60
        R_X, R_ML, R_NSA, R_MB, R_O, R_X1, R_Y = 68, 72, 88, 104, 120, 124, 128
        NMAX, RSUM, WK, ROOT = 132, 180, 228, 244
        BASE = 4

        def half_rows(m):
            return slice(DH * m, DH * m + DH)

        def rsum(u, m):
            return RSUM + 2 * u + m

        def block_of(grid_, odd, i, j):
            if odd:
                return grid_[:, i, j, :]
            up = slice(i.start + 1, i.stop + 1) if isinstance(i, slice) else i + 1
            return grid_[:, j, up, :]

        def sem(name):
            return ctx.enter_context(nc.semaphore(name))

        x_in = [sem(f"x_in{t}") for t in range(NT)]
        small_in = sem("small_in")
        gain0_in = sem("gain0_in")
        gain1_in, gain2_in, gain3_in = sem("gain1_in"), sem("gain2_in"), sem("gain3_in")
        raw_in = [sem(f"raw_in{r}") for r in range(RAW)]
        nq_hi, nq_lo_ready, nk_hi, nk_lo_ready = (sem(n) for n in ("nq_hi", "nq_lo_ready", "nk_hi", "nk_lo_ready"))
        mq_hi, mq_lo_ready, mk_hi, mk_lo_ready = (sem(n) for n in ("mq_hi", "mq_lo_ready", "mk_hi", "mk_lo_ready"))
        nq_in, mk_in, mq_in = sem("nq_in"), [sem("mk_in0"), sem("mk_in1")], [sem("mq_in0"), sem("mq_in1")]
        dup_in = sem("dup_in")
        stored = sem("stored")
        consts = sem("consts")
        hi_done, lo_done = sem("hi_done"), sem("lo_done")
        part_used = sem("part_used")
        x_sq, hn_ready, xt_done, xh_ready, xl_ready = (sem(n) for n in
                                                      ("x_sq", "hn_ready", "xt_done", "xh_ready", "xl_ready"))
        lo_first = sem("lo_first")
        eps_set, root_done = sem("eps_set"), sem("root_done")
        params_t = sem("params_t")
        params_ready = sem("params_ready")
        job_done = sem("job_done")
        read_v, read_a = sem("read_v"), sem("read_a")
        chain = sem("chain")
        conv_lin, conv_acc, conv_sig = sem("conv_lin"), sem("conv_acc"), sem("conv_sig")
        silu_done = sem("silu_done")
        blkh_ready = sem("blkh_ready")
        ks_ready = sem("ks_ready")
        gates_ready = sem("gates_ready")
        lf_step, lf_ready = sem("lf_step"), sem("lf_ready")
        gcol_ready, m_ready = sem("gcol_ready"), sem("m_ready")
        w_exp, w_ready = sem("w_exp"), sem("w_ready")
        gelu_arg, gelu_exp, gelu_ready = sem("gelu_arg"), sem("gelu_exp"), sem("gelu_ready")
        kv_cmp, kc_ready, vc_ready = sem("kv_cmp"), sem("kc_ready"), sem("vc_ready")
        cs_done, cs_sub, cs_exp, cs_ready = sem("cs_done"), sem("cs_sub"), sem("cs_exp"), sem("cs_ready")
        ct_done, ct_ready, co_done, co_used = sem("ct_done"), sem("ct_ready"), sem("co_done"), sem("co_used")
        ml_s, ml_p, ml_o, ml_used, ml_ss = sem("ml_s"), sem("ml_p"), sem("ml_o"), sem("ml_used"), sem("ml_ss")
        ml_rn, nsa_rn, ml_y, nsa_y, moba_y = (sem(n) for n in ("ml_rn", "nsa_rn", "ml_y", "nsa_y", "moba_y"))
        s_done, mx_done, p_ready = sem("s_done"), sem("mx_done"), sem("p_ready")
        t_done, pt_v, pt_a = sem("t_done"), sem("pt_v"), sem("pt_a")
        o_done, ot_ready, bt_done = sem("o_done"), sem("ot_ready"), sem("bt_done")
        bt_used, y_sq_ready, y_ss = sem("bt_used"), sem("y_sq_ready"), sem("y_ss")
        yt_done, yh_ready, yl_ready = sem("yt_done"), sem("yh_ready"), sem("yl_ready")
        wo_done, o_sq, x1_ready, x1_sq, hm_ready = (sem(n) for n in ("wo_done", "o_sq", "x1_ready", "x1_sq", "hm_ready"))
        hmt_done, hmh_ready, hml_ready = sem("hmt_done"), sem("hmh_ready"), sem("hml_ready")
        up_done, relu_ready, sq_ready, hh_ready, hl_ready = (sem(n) for n in (
            "up_done", "relu_ready", "sq_ready", "hh_ready", "hl_ready"))
        down_done, acc_ready, y_sq, res_ready = sem("down_done"), sem("acc_ready"), sem("y_sq"), sem("res_ready")
        base_ready = sem("base_ready")
        yg_ready, ss0_ready = sem("yg_ready"), sem("ss0_ready")

        def reads(n):
            return (read_v if READER[n] == "v" else read_a), READER[:n + 1].count(READER[n])

        def released(c):
            inside = [C_B, C_LO, C_LV, C_CMP, C_CMP + 1, C_CMP + 2, C_WO, C_WO + 1]
            if c in inside:
                return part_used, inside.index(c) + 1
            if c < C_WO:
                return job_done, {C_B + 1: J_B + 4, C_LQ: J_CONV + 2, C_LK: J_CONV + 4, C_LO + 1: J_LO + 4,
                                  C_KVS: J_KS + 1, C_NQ: J_NQ + 2, C_LV + 1: J_LV + 4, C_MQ: J_MQ + 2,
                                  C_MK: J_MK + 2, C_CMP + 3: J_H + 1}[c]
            if c < C_MLP:
                return wo_done, {C_WO + 2: 7, C_WO + 3: 8}[c]
            b, k = divmod(c - C_MLP, PER_BLOCK)
            if k < FB // 2:
                return up_done, FB * b + 2 * (k + 1)
            half, q = divmod(k - FB // 2, 2)
            if q == 0:
                return part_used, len(inside) + 2 * b + half + 1
            return down_done, 8 * b + 4 * (half + 1)

        def chunk_parts(c):
            def kn(lo, n, k0=0, kn_=NC):
                return w_in[0, k0 * P:(k0 + kn_) * P, lo:lo + n].rearrange("(k p) n -> p k n", p=P)
            if c in (C_B, C_B + 1):
                k0 = 4 * (c - C_B)
                return BN, [((0, 256), kn(MV, 256, k0, 4)), ((BS, 64), kn(VSL, 64, k0, 4)),
                            ((BW, 76), kn(VWN, 76, k0, 4)), ((BI, 8), kn(LI, 8, k0, 4))]
            if c in (C_LO, C_LO + 1):
                return 512, [((0, 512), kn(LO, 512, 4 * (c - C_LO), 4))]
            if c in (C_LV, C_LV + 1):
                return 512, [((0, 512), kn(LV, 512, 4 * (c - C_LV), 4))]
            if c == C_KVS:
                return 256, [((0, 192), kn(KC, 192)), ((192, 64), kn(KWN, 64))]
            if c < C_CMP:
                return 256, [((0, 256), kn({C_LQ: LQ, C_LK: LK, C_NQ: NQ, C_MQ: MQ, C_MK: MK}[c], 256))]
            if c < C_WO:
                l0 = 8 * (c - C_CMP)
                return 256, [((0, 256), cmp_w1[0, j, l0 * DH:(l0 + 8) * DH, :].rearrange("(l d) h -> d l h", d=DH))
                             for j in range(2)]
            if c < C_MLP:
                kset, half = divmod(c - C_WO, 2)
                ks = K_ORDER[4 * kset:4 * kset + 4]
                runs = [(ks[0], 4)] if kset == 0 else [(ks[0], 2), (ks[2], 2)]
                return 512, [((0, 512), w_out[0, k0 * P:(k0 + n) * P, 512 * half:512 * half + 512]
                              .rearrange("(k p) n -> p k n", p=P)) for k0, n in runs]
            b, k = divmod(c - C_MLP, PER_BLOCK)
            if k < FB // 2:
                f0 = (FB * b + 2 * k) * P
                return 256, [((0, 256), w1[0, :, f0:f0 + 256].rearrange("(k p) n -> p k n", p=P))]
            half, q = divmod(k - FB // 2, 2)
            f0 = (FB * b + 4 * q) * P
            return 512, [((0, 512), w2[0, f0:f0 + 512, 512 * half:512 * half + 512]
                          .rearrange("(k p) n -> p k n", p=P))]

        def size(c):
            n = chunk_parts(c)[0]
            return n * (4 if n > 256 else 8)

        def grid(t, c):
            n = chunk_parts(c)[0]
            return t[:, 0:size(c)].rearrange("p (k n) -> p k n", n=n)

        block = ctx.enter_context(nc.Block())

        @block.sync
        def _(sp):
            def load_chunk(c):
                if c >= RAW:
                    sp.wait_ge(lo_done, c - RAW + 1)
                    if c - RAW in SHARED:
                        sp.wait_ge(lo_first, SHARED.index(c - RAW) + 1)
                view = grid(raw[c % RAW], c)
                parts = chunk_parts(c)[1]
                k0 = 0
                for j, ((n0, n), src) in enumerate(parts):
                    if C_CMP <= c < C_WO:
                        dst = view[DH * j:DH * j + DH, :, :]
                    elif C_WO <= c < C_MLP:
                        kk = src.shape[1]
                        dst = view[:, k0:k0 + kk, :]
                        k0 += kk
                    else:
                        dst = view[:, :, n0:n0 + n]
                    sp.dma_start(dst, src).then_inc(raw_in[c % RAW], 16)

            def load_x(t):
                sp.dma_start(xres[:, t, :], x[0, t * P:(t + 1) * P, :]).then_inc(x_in[t], 16)

            load_x(0)
            sp.dma_start(gain_a[:], norm_g[0, 0:1, :].to_broadcast([P, D])).then_inc(gain0_in, 16)
            load_chunk(0)
            load_x(1)
            load_chunk(1)
            load_x(2)
            load_x(3)
            sp.dma_start(rows[0:16, :], conv_w[0].rearrange("k (c p) -> (k c) p", p=P)).then_inc(small_in, 16)
            sp.dma_start(rows[16:20, :], conv_b[0].rearrange("(c p) -> c p", p=P)).then_inc(small_in, 16)
            sp.dma_start(rows[20:28, :], head_g[0].rearrange("(c p) -> c p", p=P)).then_inc(small_in, 16)
            sp.dma_start(pe_rows[:].rearrange("l (j d) -> l j d", j=2), cmp_pe[0].rearrange("j l d -> l j d")).then_inc(small_in, 16)
            with nc.allow_non_contiguous_dma(reason="eight gate biases"):
                sp.dma_start(gb[:], gate_b[0].rearrange("j h -> h j")).then_inc(small_in, 16)
            load_chunk(2)
            for s in range(2):
                sp.dma_start(w2k[:, :, s, :], cmp_w2[0, 0].rearrange("(t p) d -> p t d", p=P)).then_inc(small_in, 16)
            sp.dma_start(w2v[:], cmp_w2[0, 1].rearrange("(t p) d -> p t d", p=P)).then_inc(small_in, 16)
            for c in range(3, NCHUNK):
                if c == C_WO:
                    sp.wait_ge(hn_ready, NT)
                    sp.dma_start(gain_a[:], norm_g[0, 1:2, :].to_broadcast([P, D])).then_inc(gain1_in, 16)
                    for h in range(HEADS):
                        p, m = divmod(h, 2)
                        sp.wait_ge(nq_lo_ready, h + 1)
                        sp.dma_start(nq_st[half_rows(1 - m), h, :].bitcast(F32), nq_lo[half_rows(m), p, :].bitcast(F32)).then_inc(nq_in, 16)
                if c == C_MLP:
                    for kind, h in MB_ORDER:
                        p, m = divmod(h, 2)
                        if kind == "k":
                            sp.wait_ge(mk_hi, h + 1)
                            sp.dma_start(mk_st[p][half_rows(1 - m), m, :].bitcast(F32),
                                         mk_st[p][half_rows(m), m, :].bitcast(F32)).then_inc(mk_in[p], 16)
                        else:
                            sp.wait_ge(mq_lo_ready, h + 1)
                            sp.dma_start(mq_st[half_rows(1 - m), h, :].bitcast(F32),
                                         mq_lo[half_rows(m), p, :].bitcast(F32)).then_inc(mq_in[p], 16)
                if c == C_MLP + 1:
                    sp.wait_ge(s_done, 2 * NU)
                    sp.dma_start(gain_b[:], norm_g[0, 2:3, :].to_broadcast([P, D])).then_inc(gain2_in, 16)
                if c == C_MLP + PER_BLOCK:
                    sp.wait_ge(x1_ready, 2 * NT)
                    sp.dma_start(gain_a[:], norm_g[0, 3:4, :].to_broadcast([P, D])).then_inc(gain3_in, 16)
                load_chunk(c)
            for t in range(NT):
                for k, half in enumerate((1, 0)):
                    sp.wait_ge(res_ready, 2 * t + k + 1)
                    h0 = 512 * half
                    sp.dma_start(out[0, t * P:(t + 1) * P, h0:h0 + 512], xres[:, t, h0:h0 + 512]).then_inc(stored, 16)
            sp.wait_ge(stored, 16 * 2 * NT)

        def raw_full(c):
            return 16 * sum(len(chunk_parts(k)[1]) for k in range(c % RAW, c + 1, RAW))

        @block.gpsimd
        def _(pool):
            nc.gpsimd.memset(ident[:], 0.0).then_inc(consts, 1)
            pool.wait_ge(consts, 1)
            nc.gpsimd.affine_select(out=ident[:], in_=ident[:], compare_op=ALU.not_equal, fill=1.0, base=0,
                                    pattern=[[-1, P]], channel_multiplier=1).then_inc(consts, 1)
            nc.gpsimd.memset(identb[:], 0.0).then_inc(consts, 1)
            nc.gpsimd.memset(mask_s[:], 0.0).then_inc(consts, 1)
            nc.gpsimd.memset(mask_c[:], 0.0).then_inc(consts, 1)
            nc.gpsimd.memset(vis[:], 1.0).then_inc(consts, 1)
            nc.gpsimd.memset(sel[:].bitcast(F32), 0.0).then_inc(consts, 1)
            nc.gpsimd.memset(zero1[:], 0.0).then_inc(consts, 1)
            pool.wait_ge(consts, 8)
            nc.gpsimd.affine_select(out=identb[:], in_=identb[:], compare_op=ALU.not_equal, fill=1.0, base=0,
                                    pattern=[[-1, P]], channel_multiplier=1).then_inc(consts, 1)
            nc.gpsimd.affine_select(out=mask_s[:], in_=mask_s[:], compare_op=ALU.is_ge, fill=NEG, base=0,
                                    pattern=[[-1, P]], channel_multiplier=1).then_inc(consts, 1)
            nc.gpsimd.affine_select(out=mask_c[:], in_=mask_c[:], compare_op=ALU.is_ge, fill=NEG,
                                    base=1 - CMP_LEN, pattern=[[P, NT], [0, 2], [-CMP_STRIDE, NP_]],
                                    channel_multiplier=1).then_inc(consts, 1)
            nc.gpsimd.affine_select(out=vis[:], in_=vis[:], compare_op=ALU.is_ge, fill=0.0,
                                    base=1 - CMP_LEN, pattern=[[P, NT]],
                                    channel_multiplier=1).then_inc(consts, 1)
            nc.gpsimd.affine_select(out=sel[:], in_=sel[:].bitcast(F32), compare_op=ALU.not_equal, fill=1.0, base=0,
                                    pattern=[[-1, HEADS], [0, P]], channel_multiplier=1).then_inc(consts, 1)

            def low_half(c):
                pool.wait_ge(hi_done, c + 1)
                n, r = size(c), ring_slot(c)
                n0 = n // 2 if c in SHARED else 0
                nc.gpsimd.tensor_tensor(ring_l[r][:, n0:n], raw[c % RAW][:, n0:n], ring_h[r][:, n0:n].bitcast(F32),
                                        ALU.subtract).then_inc(lo_done, 1)

            for c in range(C_WO):
                low_half(c)
            for h in range(HEADS):
                pool.wait_ge(w_exp, h + 1)
                for i in range(NT):
                    last = nc.gpsimd.affine_select(out=block_of(W[:, h // 2], h % 2, i, i), in_=block_of(W[:, h // 2], h % 2, i, i), compare_op=ALU.is_ge,
                                                   fill=0.0, base=0, pattern=[[1, P]], channel_multiplier=-1)
                last.then_inc(w_ready, 1)
            low_half(C_WO)
            low_half(C_WO + 1)
            def moba_low(n):
                kind, h = MB_ORDER[n]
                p, m = divmod(h, 2)
                r = half_rows(m)
                if kind == "k":
                    pool.wait_ge(mk_hi, h + 1)
                    nc.gpsimd.tensor_tensor(mk_lo[r, p, :], mkT[r, p, :], mk_st[p][r, m, :].bitcast(F32), ALU.subtract
                                            ).then_inc(mk_lo_ready, 1)
                    pool.wait_ge(mk_lo_ready, h + 1)
                else:
                    pool.wait_ge(mq_hi, h + 1)
                    nc.gpsimd.tensor_tensor(mq_lo[r, p, :], mqT[r, p, :], mq_st[r, h, :].bitcast(F32), ALU.subtract
                                            ).then_inc(mq_lo_ready, 1)
                    pool.wait_ge(mq_lo_ready, h + 1)

            pool.wait_ge(lo_done, C_WO + 2)
            for n in range(2):
                moba_low(n)
            pool.wait_ge(ml_rn, 1)
            rn = stat[:, R_ML:R_ML + 16].rearrange("p (t h o) -> p t h o", h=HEADS, o=1).to_broadcast([P, NT, HEADS, DV])
            nc.gpsimd.tensor_tensor(hid[:], hid[:], rn, ALU.mult).then_inc(ml_y, 1)
            pool.wait_ge(ml_y, 1)
            yml = y[:, :, 256:768].rearrange("p t (h d) -> p t h d", h=HEADS)
            nc.gpsimd.tensor_tensor(yml, yml, hid[:], ALU.mult).then_inc(ml_y, 1)
            pool.wait_ge(ml_y, 2)
            for n in range(2, 2 * HEADS):
                moba_low(n)
            low_half(C_WO + 2)
            low_half(C_WO + 3)
            pool.wait_ge(nsa_rn, 1)
            rn = stat[:, R_NSA:R_NSA + 16].rearrange("p (t h o) -> p t h o", h=HEADS, o=1).to_broadcast([P, NT, HEADS, DH])
            yn = y[:, :, 768:1024].rearrange("p t (h d) -> p t h d", h=HEADS)
            nc.gpsimd.tensor_tensor(yn, yn, rn, ALU.mult).then_inc(nsa_y, 1)
            for c in range(C_MLP, NCHUNK):
                low_half(c)
            pool.wait_ge(gain3_in, 16)
            for t in range(NT):
                pool.wait_ge(acc_ready, 8 * (NB - 1) + t + 1)
                nc.gpsimd.tensor_tensor(yg[:, t, :], y[:, t, 0:512], gain_a[:, 0:512], ALU.mult).then_inc(yg_ready, 1)

        @block.scalar
        def _(act):
            def high_half(c):
                act.wait_ge(raw_in[c % RAW], raw_full(c))
                if c == C_WO + 3:
                    act.wait_ge(ml_o, len(ML_UNITS))
                elif c >= 3:
                    act.wait_ge(*released(ring_previous(c)))
                n, r = size(c), ring_slot(c)
                nc.scalar.activation(ring_h[r][:, 0:n], raw[c % RAW][:, 0:n], ACT.Copy).then_inc(hi_done, 1)

            act.wait_ge(eps_set, 1)
            nc.scalar.activation(stat[:, ROOT + 8:ROOT + 9], eps1[:], ACT.Sqrt)

            def root(ss, r, beside=eps1[:]):
                nc.scalar.activation(stat[:, r:r + 1], stat[:, ss:ss + 1], ACT.Sqrt, scale=1.0 / D,
                                     bias=beside).then_inc(root_done, 1)

            def x_root(t):
                act.wait_ge(x_in[t], 16)
                nc.scalar.activation(junk[:], xres[:, t, :], ACT.Square,
                                     accum_out=stat[:, SS_X + t:SS_X + t + 1]).then_inc(x_sq, 1)
                act.wait_ge(x_sq, t + 1)
                root(SS_X + t, ROOT + t)

            def x_high(t):
                act.wait_ge(xt_done, t + 1)
                for b in range(2):
                    nc.scalar.activation(xT_h[:, 4 * b:4 * b + 4, t * P:(t + 1) * P],
                                         ps[:, 2 * t + b, :].rearrange("p (c q) -> p c q", c=4),
                                         ACT.Copy).then_inc(xh_ready, 1)

            x_root(0)
            high_half(0)
            x_high(0)
            x_root(1)
            high_half(1)
            x_root(2)
            x_high(1)
            x_root(3)
            x_high(2)
            high_half(2)
            x_high(3)
            high_half(3)

            def conv_linear(n):
                act.wait_ge(job_done, J_CONV + n + 1)
                if n == 0:
                    act.wait_ge(params_ready, 1)
                nc.scalar.activation(qkT[:, n, :], ps[:, (J_CONV + n) % 8, :], ACT.Identity,
                                     scale=cols[:, 12 + n:13 + n], bias=cols[:, 16 + n:17 + n]).then_inc(conv_lin, 1)

            def conv_sigmoid(n):
                act.wait_ge(conv_acc, n + 1)
                nc.scalar.activation(sig[:, n % 2, :], qkT[:, n, :], ACT.Sigmoid).then_inc(conv_sig, 1)

            for n in range(4):
                conv_linear(n)
                if n >= 1:
                    conv_sigmoid(n - 1)
                if n == 1:
                    high_half(4)
            conv_sigmoid(3)
            high_half(5)
            act.wait_ge(read_v, J_B + NT)
            nc.scalar.activation(gt[:], zB[:, :, BG:BG + 12], ACT.Sigmoid).then_inc(gates_ready, 1)
            high_half(6)
            for t in range(NT):
                act.wait_ge(job_done, J_LO + t + 1)
                nc.scalar.activation(y[:, t, 256:768], ps[:, (J_LO + t) % 8, :], ACT.Sigmoid).then_inc(read_a, 1)
            high_half(7)
            act.wait_ge(job_done, J_LF + 1)
            nc.scalar.activation(g_row[:, 0, :], ps[0:HEADS, J_LF % 8, :], ACT.Abs, bias=gb[:, 1:2]).then_inc(lf_step, 1)
            act.wait_ge(lf_step, 1)
            nc.scalar.activation(g_row[:, 0, :], g_row[:, 0, :], ACT.Exp, scale=-1.0).then_inc(lf_step, 1)
            act.wait_ge(lf_step, 2)
            nc.scalar.activation(g_row[:, 0, :], g_row[:, 0, :], ACT.Ln, bias=1.0).then_inc(lf_ready, 1)
            act.wait_ge(job_done, J_KV + 1)
            for j in range(2):
                for a in range(2):
                    src = ps[DH * j:DH * j + DH, J_KV % 8, :].rearrange("p (n b) -> p b n", b=16)[:, :, a:a + NCMP]
                    nc.scalar.activation(blk_h[DH * j:DH * j + DH, 16 * a:16 * a + 16, j, 0:NCMP], src,
                                         ACT.Copy).then_inc(blkh_ready, 1)
                act.wait_ge(params_ready, 2)
                nc.scalar.activation(blk_h[DH * j:DH * j + DH, :, j, NCMP], peT[DH * j:DH * j + DH, :],
                                     ACT.Copy).then_inc(blkh_ready, 1)
            act.wait_ge(job_done, J_KS + 1)
            nc.scalar.activation(kselT[0:DH, :], ps[0:DH, J_KS % 8, :], ACT.Copy).then_inc(ks_ready, 1)
            nc.scalar.activation(kwinT[DH:P, :], ps[DH:P, J_KS % 8, :], ACT.Copy).then_inc(read_a, 1)
            act.wait_ge(ks_ready, 1)
            act.dma_start(kselT[DH:P, :], kselT[0:DH, :]).then_inc(dup_in, 16)
            act.wait_ge(read_a, reads(J_KS)[1])
            act.dma_start(kwinT[0:DH, :], kwinT[DH:P, :]).then_inc(dup_in, 16)
            high_half(8)
            high_half(9)
            for p in range(2):
                act.wait_ge(job_done, J_NQ + p + 1)
                nc.scalar.activation(nqT[:, p, :], ps[:, (J_NQ + p) % 8, :], ACT.Copy, scale=DH ** -0.5).then_inc(read_a, 1)
            act.wait_ge(job_done, J_GC + 1)
            nc.scalar.activation(gcol[:].rearrange("p t h -> p (t h)"), ps[:, J_GC % 8, 0:16], ACT.Copy).then_inc(gcol_ready, 1)
            nc.scalar.activation(emc[:].rearrange("p t h -> p (t h)"), ps[:, J_GC % 8, 16:32], ACT.Exp,
                                 scale=-1.0).then_inc(read_a, 1)
            high_half(10)
            high_half(11)
            high_half(12)
            for p in range(2):
                act.wait_ge(job_done, J_MQ + p + 1)
                nc.scalar.activation(mqT[:, p, :], ps[:, (J_MQ + p) % 8, :], ACT.Copy, scale=DH ** -0.5).then_inc(read_a, 1)
            high_half(13)
            high_half(14)
            act.wait_ge(job_done, J_MK + 2)
            act.wait_ge(dup_in, 32)
            for k, keys_ in enumerate((kselT, kwinT)):
                nc.scalar.activation(nk_st[:, k, :], keys_[:], ACT.Copy).then_inc(nk_hi, 1)
            for h in range(HEADS):
                p, m = divmod(h, 2)
                if h == 0:
                    act.wait_ge(read_a, reads(J_NQ + 1)[1])
                nc.scalar.activation(nq_st[half_rows(m), h, :], nqT[half_rows(m), p, :], ACT.Copy).then_inc(nq_hi, 1)
            high_half(15)
            act.wait_ge(gcol_ready, 1)
            for h in range(HEADS):
                act.wait_ge(job_done, J_MB + h + 1)
                for j in range(NT):
                    last = nc.scalar.activation(block_of(W[:, h // 2], h % 2, slice(j, NT), j),
                                                ps[:, (J_MB + h) % 8, j * P:SEQ].rearrange("p (i t) -> p i t", t=P),
                                                ACT.Exp, scale=-1.0, bias=gcol[:, j, h:h + 1])
                last.then_inc(read_a, 1)
                act.wait_ge(read_a, reads(J_MB + h)[1])
                nc.scalar.activation(zero1[:], zero1[:], ACT.Copy).then_inc(w_exp, 1)
            def ml_squares(u):
                p, i = ML_UNITS[u]
                act.wait_ge(ml_used, u + 1)
                for m in range(2):
                    h = 2 * p + m
                    c = SS_ML + HEADS * i + h
                    if 2 * u + m:
                        act.wait_ge(ml_ss, 2 * u + m)
                    nc.scalar.activation(junkb[:, 0:DV], hid[:, i, h, :], ACT.Square,
                                         accum_out=stat[:, c:c + 1]).then_inc(ml_ss, 1)

            def moba_high(n):
                kind, h = MB_ORDER[n]
                p, m = divmod(h, 2)
                r = half_rows(m)
                if kind == "k":
                    if h == 0:
                        act.wait_ge(cs_done, 1)
                        act.wait_ge(read_v, reads(J_MK + 1)[1])
                    if h == 2:
                        act.wait_ge(co_done, 2)
                    nc.scalar.activation(mk_st[p][r, m, :], mkT[r, p, :], ACT.Copy).then_inc(mk_hi, 1)
                else:
                    if h == 0:
                        act.wait_ge(ml_y, 2)
                        act.wait_ge(read_a, reads(J_MQ + 1)[1])
                    nc.scalar.activation(mq_st[r, h, :], mqT[r, p, :], ACT.Copy).then_inc(mq_hi, 1)

            for u in range(len(ML_UNITS)):
                if u == 1:
                    act.wait_ge(gelu_arg, 1)
                    nc.scalar.activation(cg[:, 3], cg[:, 2], ACT.Exp, scale=-1.5957691216057308).then_inc(gelu_exp, 1)
                if u == 3:
                    act.wait_ge(kv_cmp, 1)
                    nc.scalar.activation(kcT[:], ps[:, 4, 0:NP_], ACT.Copy).then_inc(kc_ready, 1)
                if u in (3, 4):
                    high_half(C_WO + u - 3)
                if u == 5:
                    act.wait_ge(cs_sub, 1)
                    nc.scalar.activation(cexp[:], cexp[:], ACT.Exp).then_inc(cs_exp, 1)
                if u >= 1:
                    ml_squares(u - 1)
                if u >= 6:
                    moba_high(u - 6)

            def exp(s):
                w = (s // 2 % NT + 1) * P
                act.wait_ge(mx_done, s + 1)
                if s >= 3:
                    act.wait_ge(t_done, s - 2)
                nc.scalar.activation(probs[:, s % 3, 0:w], ps[:, S_BANK[s % 5], 0:w], ACT.Exp,
                                     bias=stat[:, NMAX + s:NMAX + s + 1],
                                     accum_out=stat[:, RSUM + s:RSUM + s + 1]).then_inc(p_ready, 1)

            def copy_t(u):
                g, i = divmod(u, NT)
                act.wait_ge(t_done, 2 * u + 2)
                if i == 0 and g >= 2:
                    act.wait_ge(o_done, g - 1)
                nc.scalar.activation(block_of(pT[:, g % 2], 1, i, slice(0, i + 1)),
                                     ps[:, 5, 0:(i + 1) * P].rearrange("p (j q) -> p j q", q=P), ACT.Copy).then_inc(pt_a, 1)

            def copy_o(g):
                act.wait_ge(o_done, g + 1)
                if g:
                    act.wait_ge(bt_done, g)
                nc.scalar.activation(oT[:], ps[:, O_BANK[g], :], ACT.Copy).then_inc(ot_ready, 1)

            def squares(g):
                br, p = PAIRS[g]
                if br == "sel":
                    return
                act.wait_ge(bt_used, g + 1)
                if g > 2:
                    act.wait_ge(y_ss, g - 2)
                y0 = (0 if br == "moba" else 768) + P * p
                nc.scalar.activation(ysq[:].rearrange("p (i d) -> p i d", i=NT), y[:, :, y0:y0 + P],
                                     ACT.Square).then_inc(y_sq_ready, 1)

            def y_high(k):
                c = K_ORDER[k]
                act.wait_ge(yt_done, k + 1)
                nc.scalar.activation(xT_h[:, c, :], ps[:, YT_BANK[k], :], ACT.Copy,
                                     scale=cols[:, 20 + c:21 + c]).then_inc(yh_ready, 1)

            exp(0)
            exp(1)
            ml_squares(len(ML_UNITS) - 1)
            for u in range(NU):
                g, i = divmod(u, NT)
                if u + 1 < NU:
                    exp(2 * u + 2)
                if g and i == 2:
                    copy_o(g - 1)
                if u + 1 < NU:
                    exp(2 * u + 3)
                copy_t(u)
                if u == 0:
                    act.wait_ge(ct_done, 1)
                    nc.scalar.activation(cexpT[:].rearrange("p t q -> p (t q)"), ps[:, 6, :], ACT.Copy).then_inc(ct_ready, 1)
                if g >= 2 and i == 0:
                    squares(g - 2)
                if u in (15, 19):
                    high_half(C_WO + 2 + (u == 19))
                if u in MB_UNITS:
                    moba_high(2 + MB_UNITS.index(u))
            y_high(0)
            y_high(1)
            squares(len(PAIRS) - 2)
            copy_o(len(PAIRS) - 1)
            y_high(2)
            y_high(3)
            squares(len(PAIRS) - 1)
            for k in range(4, 8):
                y_high(k)

            def hm_high(t):
                for b in range(2):
                    act.wait_ge(hmt_done, 2 * t + b + 1)
                    nc.scalar.activation(xT_h[:, 4 * b:4 * b + 4, t * P:(t + 1) * P],
                                         ps[:, WO_BANK[t] + b, :].rearrange("p (c q) -> p c q", c=4),
                                         ACT.Copy).then_inc(hmh_ready, 1)

            for t in range(NT):
                for half in range(2):
                    act.wait_ge(wo_done, 2 * t + half + 1)
                    if t:
                        act.wait_ge(x1_sq, 2 * t)
                    c = SS_Y + 2 * t + half
                    nc.scalar.activation(junk_w[:, 512 * half:512 * half + 512], ps[:, WO_BANK[t] + half, :], ACT.Square,
                                         accum_out=stat[:, c:c + 1]).then_inc(o_sq, 1)
                    if t == NT - 1 and half == 0:
                        high_half(C_MLP + 1)
                act.wait_ge(o_sq, 2 * t + 2)
                act.wait_ge(base_ready, 2 * t + 1)
                root(SS_Y + 2 * t + 1, ROOT + t, stat[:, BASE + 4 * t:BASE + 4 * t + 1])
                if t == NT - 2:
                    high_half(C_MLP)
                if t >= 1:
                    hm_high(t - 1)
                for half in range(2):
                    act.wait_ge(x1_ready, 2 * t + half + 1)
                    c = SS_O + 2 * t + half
                    nc.scalar.activation(junk_w[:, 512 * half:512 * half + 512], xres[:, t, 512 * half:512 * half + 512], ACT.Square,
                                         accum_out=stat[:, c:c + 1]).then_inc(x1_sq, 1)
                act.wait_ge(x1_sq, 2 * t + 2)
                act.wait_ge(base_ready, 2 * t + 2)
                root(SS_O + 2 * t + 1, ROOT + NT + t, stat[:, BASE + 4 * t + 2:BASE + 4 * t + 3])
            high_half(C_MLP + 2)
            hm_high(NT - 1)

            c = C_MLP + 3
            for b in range(NB):
                for f in range(FB):
                    n = FB * b + f
                    act.wait_ge(up_done, n + 1)
                    if n >= 2:
                        act.wait_ge(sq_ready, n - 1)
                    nc.scalar.activation(relu[:, n % 2, :], ps[:, SETS[b % 2][f % 4], :], ACT.Relu).then_inc(relu_ready, 1)
                    act.wait_ge(relu_ready, n + 1)
                    nc.scalar.activation(hT_h[:, f, :], relu[:, n % 2, :], ACT.Square).then_inc(hh_ready, 1)
                    if f % 2 == 1 and c < NCHUNK:
                        high_half(c)
                        c += 1
                for q in range(FB // 2):
                    if c < NCHUNK:
                        high_half(c)
                        c += 1
            for half in range(2):
                for t in range(NT):
                    act.wait_ge(acc_ready, 8 * (NB - 1) + 4 * half + t + 1)
                    if 4 * half + t:
                        act.wait_ge(y_sq, 4 * half + t)
                    cc = SS_Y + 2 * t + half
                    nc.scalar.activation(relu[:, 0, :], y[:, t, 512 * half:512 * half + 512], ACT.Square,
                                         accum_out=stat[:, cc:cc + 1]).then_inc(y_sq, 1)
                    if half:
                        act.wait_ge(y_sq, 4 + t + 1)
                        act.wait_ge(ss0_ready, 1)
                        nc.scalar.activation(stat[:, ROOT + t:ROOT + t + 1], stat[:, cc:cc + 1], ACT.Sqrt, scale=1.0 / D,
                                             bias=stat[:, SS_O + t:SS_O + t + 1]).then_inc(root_done, 1)

        @block.vector
        def _(dve):
            steps = [0]

            def link(ins):
                steps[0] += 1
                ins.then_inc(chain, 1)
                dve.wait_ge(chain, steps[0])

            def rsqrt(ss, r, n, width):
                v, a, yv = stat[:, WK:WK + n], stat[:, WK + 8:WK + 8 + n], stat[:, r:r + n]
                if n > 8:
                    v, a = wide[:, 0:n], wide[:, 16:16 + n]
                link(nc.vector.tensor_scalar(v, stat[:, ss:ss + n], 1.0 / width, EPS, ALU.mult, ALU.add))
                link(nc.vector.tensor_scalar(yv.bitcast(I32), v.bitcast(I32), -0.5, float(0x5f3759df), ALU.mult, ALU.add))
                link(nc.vector.tensor_scalar(v, v, -0.5, None, ALU.mult))
                for k in range(3):
                    if n == 1:
                        link(nc.vector.scalar_tensor_tensor(a, yv, v, yv, ALU.mult, ALU.mult))
                    else:
                        link(nc.vector.tensor_tensor(a, yv, yv, ALU.mult))
                        link(nc.vector.tensor_tensor(a, a, v, ALU.mult))
                    if k < 2:
                        link(nc.vector.scalar_tensor_tensor(yv, a, 1.5, yv, ALU.add, ALU.mult))
                return nc.vector.scalar_tensor_tensor(yv, a, 1.5, yv, ALU.add, ALU.mult)

            def rsqrt1(ss, r, root, n, offset=-0.5 * EPS):
                v, a, yv = stat[:, WK:WK + 1], stat[:, WK + 8:WK + 9], stat[:, r:r + 1]
                dve.wait_ge(root_done, n)
                link(nc.vector.tensor_scalar(v, stat[:, ss:ss + 1], -0.5 / D, offset, ALU.mult, ALU.add))
                link(nc.vector.reciprocal(yv, stat[:, root:root + 1]))
                link(nc.vector.scalar_tensor_tensor(a, yv, v, yv, ALU.mult, ALU.mult))
                return nc.vector.scalar_tensor_tensor(yv, a, 1.5, yv, ALU.add, ALU.mult)

            nc.vector.memset(eps1[:], EPS).then_inc(eps_set, 1)
            link(nc.vector.memset(blk_h[DH:P, :, 0, :].bitcast(F32), 0.0))
            link(nc.vector.memset(blk_h[0:DH, :, 1, :].bitcast(F32), 0.0))
            link(nc.vector.memset(lv1[:, :, :, DV:DV + 1], 1.0))

            def normalise(t):
                link(rsqrt1(SS_X + t, R_X + t, ROOT + t, t + 1))
                if t == 0:
                    dve.wait_ge(gain0_in, 16)
                nc.vector.scalar_tensor_tensor(y[:, t, :], xres[:, t, :], stat[:, R_X + t:R_X + t + 1], gain_a[:],
                                               ALU.mult, ALU.mult).then_inc(hn_ready, 1)

            def chunk_low(c):
                dve.wait_ge(hi_done, c + 1)
                n = size(c) // 2
                r = ring_slot(c)
                nc.vector.tensor_tensor(ring_l[r][:, 0:n], raw[c % RAW][:, 0:n], ring_h[r][:, 0:n].bitcast(F32),
                                        ALU.subtract).then_inc(lo_first, 1)

            def x_low(t):
                for b in range(2):
                    dve.wait_ge(xh_ready, 2 * t + b + 1)
                    nc.vector.tensor_tensor(xT_l[:, 4 * b:4 * b + 4, t * P:(t + 1) * P],
                                            ps[:, 2 * t + b, :].rearrange("p (c q) -> p c q", c=4),
                                            xT_h[:, 4 * b:4 * b + 4, t * P:(t + 1) * P].bitcast(F32),
                                            ALU.subtract).then_inc(xl_ready, 1)

            normalise(0)
            chunk_low(0)
            x_low(0)
            normalise(1)
            chunk_low(1)
            normalise(2)
            x_low(1)
            normalise(3)
            x_low(2)
            x_low(3)

            for t in range(NT):
                dve.wait_ge(job_done, J_B + t + 1)
                nc.vector.tensor_copy(zB[:, t, :], ps[:, (J_B + t) % 8, 0:BN]).then_inc(read_v, 1)

            dve.wait_ge(params_t, 1)
            nc.vector.tensor_copy(cols[:], ps[:, PARAM_BANK, 0:28]).then_inc(params_ready, 1)
            nc.vector.tensor_copy(peT[:], ps[:, PARAM_BANK, 64:96]).then_inc(params_ready, 1)

            def silu(n):
                dve.wait_ge(conv_sig, n + 1)
                nc.vector.scalar_tensor_tensor(qkT[:, n, :], qkT[:, n, :], 1.0 if n < 2 else DH ** -0.5,
                                               sig[:, n % 2, :], ALU.mult, ALU.mult).then_inc(silu_done, 1)

            for n in range(4):
                dve.wait_ge(conv_lin, n + 1)
                for back in (1, 2, 3):
                    ins = nc.vector.scalar_tensor_tensor(
                        qkT[:, n, back:SEQ], ps[:, (J_CONV + n) % 8, 0:SEQ - back],
                        cols[:, 4 * (3 - back) + n:4 * (3 - back) + n + 1], qkT[:, n, back:SEQ], ALU.mult, ALU.add)
                    if back < 3:
                        link(ins)
                    else:
                        ins.then_inc(read_v, 1)
                dve.wait_ge(read_v, reads(J_CONV + n)[1])
                nc.vector.tensor_copy(stat[:, WK:WK + 1], stat[:, WK:WK + 1]).then_inc(conv_acc, 1)
                if n >= 1:
                    silu(n - 1)
            silu(3)
            dve.wait_ge(lf_ready, 1)
            link(nc.vector.tensor_scalar(g_row[:, 1, :], ps[0:HEADS, J_LF % 8, :], gb[:, 1:2], 0.0, ALU.add, ALU.min))
            link(nc.vector.tensor_tensor(g_row[:, 1, :], g_row[:, 1, :], g_row[:, 0, :], ALU.subtract))
            link(nc.vector.tensor_tensor_scan(g_row[:, 0, :], g_row[:, 1, :], zero1[0:HEADS, :].to_broadcast([HEADS, SEQ]),
                                              0.0, ALU.add, ALU.add))
            dve.wait_ge(job_done, J_LI + 1)
            nc.vector.scalar_tensor_tensor(g_row[:, 1, :], ps[0:HEADS, J_LI % 8, :], gb[:, 0:1], g_row[:, 0, :],
                                           ALU.add, ALU.subtract).then_inc(read_v, 1)
            dve.wait_ge(read_v, reads(J_LI)[1])
            link(nc.vector.tensor_tensor_scan(g_row[:, 2, :], g_row[:, 1, :], g_row[:, 1, :], 0.0, ALU.max, ALU.max))
            nc.vector.tensor_tensor(g_row[:, 0, :], g_row[:, 0, :], g_row[:, 2, :], ALU.add).then_inc(read_v, 1)
            dve.wait_ge(silu_done, 4)
            link(nc.vector.memset(blk_l[DH:P, :, 0, :].bitcast(F32), 0.0))
            link(nc.vector.memset(blk_l[0:DH, :, 1, :].bitcast(F32), 0.0))
            dve.wait_ge(blkh_ready, 6)
            for j in range(2):
                rs_ = slice(DH * j, DH * j + DH)
                for a in range(2):
                    src = ps[rs_, J_KV % 8, :].rearrange("p (n b) -> p b n", b=16)[:, :, a:a + NCMP]
                    nc.vector.tensor_tensor(blk_l[rs_, 16 * a:16 * a + 16, j, 0:NCMP], src,
                                            blk_h[rs_, 16 * a:16 * a + 16, j, 0:NCMP].bitcast(F32), ALU.subtract)
                last = nc.vector.tensor_tensor(blk_l[rs_, :, j, NCMP], peT[rs_, :], blk_h[rs_, :, j, NCMP].bitcast(F32),
                                               ALU.subtract)
            last.then_inc(read_v, 1)
            dve.wait_ge(job_done, J_GC + 1)
            nc.vector.tensor_copy(m_split[:, 0, :], g_row[:, 2, :]).then_inc(m_ready, 1)
            dve.wait_ge(m_ready, 1)
            nc.vector.tensor_tensor(m_split[:, 1, :], g_row[:, 2, :], m_split[:, 0, :].bitcast(F32), ALU.subtract).then_inc(m_ready, 1)
            for t in range(NT):
                dve.wait_ge(job_done, J_LV + t + 1)
                nc.vector.tensor_copy(lv1[:, t, :, 0:DV], ps[:, (J_LV + t) % 8, :].rearrange("p (h d) -> p h d", h=HEADS)
                                      ).then_inc(read_v, 1)
            for p in range(2):
                dve.wait_ge(job_done, J_MK + p + 1)
                nc.vector.tensor_copy(mkT[:, p, :], ps[:, (J_MK + p) % 8, :]).then_inc(read_v, 1)
            for k, keys_ in enumerate((kselT, kwinT)):
                dve.wait_ge(nk_hi, k + 1)
                nc.vector.tensor_tensor(nk_lo[:, k, :], keys_[:], nk_st[:, k, :].bitcast(F32), ALU.subtract).then_inc(nk_lo_ready, 1)
            dve.wait_ge(job_done, J_MB + HEADS)
            for h in range(HEADS):
                p, m = divmod(h, 2)
                r = half_rows(m)
                dve.wait_ge(nq_hi, h + 1)
                nc.vector.tensor_tensor(nq_lo[r, p, :], nqT[r, p, :], nq_st[r, h, :].bitcast(F32), ALU.subtract).then_inc(nq_lo_ready, 1)
            chunk_low(C_CMP + 3)
            dve.wait_ge(job_done, J_H + 1)
            nc.vector.tensor_copy(hsb[:], ps[0:2 * NP_, J_H % 8, 0:CMP_HID]).then_inc(read_v, 1)
            dve.wait_ge(job_done, J_H + 2)
            nc.vector.tensor_copy(cg[:, 0], ps[:, HT_BANK, 0:4 * NP_].rearrange("p (t n) -> p t n", t=2)).then_inc(read_v, 1)

            def gelu():
                dve.wait_ge(read_v, READER.count("v"))
                hv = cg[:, 0].rearrange("p t (j n) -> p (t j) n", n=NP_)
                xv = cg[:, 1].rearrange("p t (j n) -> p (t j) n", n=NP_)
                link(nc.vector.tensor_tensor(xv, hv, hv[:, :, NCMP:NP_].to_broadcast([P, 4, NP_]), ALU.add))
                link(nc.vector.tensor_tensor(cg[:, 2], cg[:, 1], cg[:, 1], ALU.mult))
                link(nc.vector.tensor_scalar(cg[:, 2], cg[:, 2], 0.044715, 1.0, ALU.mult, ALU.add))
                nc.vector.tensor_tensor(cg[:, 2], cg[:, 2], cg[:, 1], ALU.mult).then_inc(gelu_arg, 1)

            def gelu_rest():
                dve.wait_ge(gelu_exp, 1)
                link(nc.vector.tensor_scalar(cg[:, 3], cg[:, 3], 1.0, None, ALU.add))
                link(nc.vector.reciprocal(cg[:, 3], cg[:, 3]))
                link(nc.vector.tensor_tensor(gel[:], cg[:, 1], cg[:, 3], ALU.mult))
                gv = gel[:].rearrange("p t (j n) -> p t j n", n=NP_)
                link(nc.vector.memset(gv[:, :, :, NCMP:NP_], 0.0))
                for t in range(2):
                    last = nc.vector.tensor_copy(gelr[:, t], gv[:, t, 1:2, :].to_broadcast([P, HEADS, NP_]))
                last.then_inc(gelu_ready, 1)

            def cmp_values():
                link(nc.vector.memset(vbd[:], 0.0))
                dve.wait_ge(kv_cmp, 2)
                for m in range(2):
                    for p in range(2):
                        r, h = 2 * m + p, 2 * p + m
                        last = nc.vector.tensor_copy(vbd[32 * r:32 * r + 32, DH * h:DH * h + DH],
                                                     ps[32 * r:32 * r + 32, 5, 0:DH])
                last.then_inc(vc_ready, 1)

            def cmp_max():
                dve.wait_ge(cs_done, 1)
                dve.wait_ge(nq_in, 16 * HEADS)
                for m in range(2):
                    link(nc.vector.tensor_reduce(wide[:, 32 + 8 * m:40 + 8 * m],
                                                 ps[:, 4 + m, 0:8 * NP_].rearrange("p (a n) -> p a n", n=NP_), AX.X, ALU.max))
                for m in range(2):
                    last = nc.vector.tensor_tensor(
                        cexp[:, :, 2 * m:2 * m + 2, :],
                        ps[:, 4 + m, 0:8 * NP_].rearrange("p (i a n) -> p i a n", i=NT, n=NP_),
                        wide[:, 32 + 8 * m:40 + 8 * m].rearrange("p (i a o) -> p i a o", i=NT, o=1).to_broadcast([P, NT, 2, NP_]),
                        ALU.subtract)
                    if m == 0:
                        link(last)
                last.then_inc(cs_sub, 1)

            def cmp_probs():
                dve.wait_ge(cs_exp, 1)
                link(nc.vector.tensor_reduce(wide[:, 32:48], cexp[:].rearrange("p i a n -> p (i a) n"), AX.X, ALU.add))
                link(nc.vector.reciprocal(wide[:, 32:48], wide[:, 32:48]))
                rs = wide[:, 32:48].rearrange("p (i a) -> p i a", i=NT)
                link(nc.vector.tensor_tensor(rs, rs, vis[:].rearrange("p (i o) -> p i o", o=1).to_broadcast([P, NT, 4]), ALU.mult))
                cv = cexp[:].rearrange("p i a n -> p (i a) n")
                nc.vector.tensor_tensor(cv, cv, wide[:, 32:48].rearrange("p (a o) -> p a o", o=1).to_broadcast([P, 16, NP_]),
                                        ALU.mult).then_inc(cs_ready, 1)

            def ml_out(u):
                p, i = ML_UNITS[u]
                dve.wait_ge(ml_o, u + 1)
                if u:
                    dve.wait_ge(ml_used, u)
                ob = ps[:, 7 - u % 2, :].rearrange("p (m d) -> p m d", m=2)
                d = stat[:, WK:WK + 2].rearrange("p (m o) -> p m o", o=1)
                den = ob[:, :, DV:DV + 1]
                link(nc.vector.scalar_tensor_tensor(d, den, -1.0, emc[:, i, 2 * p:2 * p + 2].rearrange("p (m o) -> p m o", o=1),
                                                    ALU.mult, ALU.max))
                link(nc.vector.tensor_tensor(d, den, d, ALU.max))
                link(nc.vector.reciprocal(d, d))
                nc.vector.tensor_tensor(hid[:, i, 2 * p:2 * p + 2, :], ob[:, :, 0:DV], d.to_broadcast([P, 2, DV]),
                                        ALU.mult).then_inc(ml_used, 1)

            def row_max(s):
                w = (s // 2 % NT + 1) * P
                dve.wait_ge(s_done, s + 1)
                nc.vector.tensor_reduce(stat[:, NMAX + s:NMAX + s + 1], ps[:, S_BANK[s % 5], 0:w], AX.X, ALU.max,
                                        negate=True).then_inc(mx_done, 1)

            for u, (p, i) in enumerate(ML_UNITS):
                w = (i + 1) * P
                for m in range(2):
                    s, h = 2 * u + m, 2 * p + m
                    dve.wait_ge(ml_s, u + 1)
                    dve.wait_ge(w_ready, h + 1)
                    if s >= 3:
                        dve.wait_ge(ml_o, (s - 3) // 2 + 1)
                    nc.vector.tensor_tensor(probsT[:, s % 3, 0:w].rearrange("p (j t) -> p j t", t=P),
                                            ps[:, ML_BANK[u % 2] + m, 0:w].rearrange("p (j t) -> p j t", t=P),
                                            block_of(W[:, h // 2], h % 2, i, slice(0, i + 1)), ALU.mult).then_inc(ml_p, 1)
                if u == 2:
                    gelu_rest()
                if u >= 1:
                    ml_out(u - 1)
                if u == 1:
                    gelu()
                if u == 3:
                    cmp_values()
                if u == 5:
                    cmp_max()
                if u == 6:
                    cmp_probs()
            row_max(0)
            row_max(1)
            ml_out(len(ML_UNITS) - 1)
            dve.wait_ge(ml_used, len(ML_UNITS))
            row_max(2)
            def cmp_gated(half):
                dve.wait_ge(co_done, half + 1)
                if half == 0:
                    dve.wait_ge(gates_ready, 1)
                for i in (2 * half, 2 * half + 1):
                    last = nc.vector.tensor_tensor(
                        y[:, i, 768:1024].rearrange("p (h d) -> p h d", h=HEADS),
                        ps[:, 6, 256 * (i % 2):256 * (i % 2) + 256].rearrange("p (h d) -> p h d", h=HEADS),
                        gt[:, i, :].rearrange("p (h b) -> p h b", b=3)[:, :, 0:1].to_broadcast([P, HEADS, DH]), ALU.mult)
                last.then_inc(co_used, 1)

            def copy_t(u):
                g, i = divmod(u, NT)
                dve.wait_ge(t_done, 2 * u + 1)
                if i == 0 and g >= 2:
                    dve.wait_ge(o_done, g - 1)
                nc.vector.tensor_copy(block_of(pT[:, g % 2], 0, i, slice(0, i + 1)),
                                      ps[:, 4, 0:(i + 1) * P].rearrange("p (j q) -> p j q", q=P)).then_inc(pt_v, 1)

            def coefficients(g):
                br, p = PAIRS[g]
                dve.wait_ge(p_ready, 2 * NT * (g + 1))
                if g:
                    dve.wait_ge(bt_used, g)
                rv = stat[:, WK:WK + 8]
                link(nc.vector.reciprocal(rv, stat[:, rsum(NT * g, 0):rsum(NT * g, 0) + 8]))
                if br != "moba":
                    gates = gt[:].rearrange("p i (h b) -> p i h b", b=3)[:, :, 2 * p:2 * p + 2, 1 if br == "sel" else 2]
                    rv2 = rv.rearrange("p (i m) -> p i m", i=NT)
                    link(nc.vector.tensor_tensor(rv2, rv2, gates, ALU.mult))

            def attn_out(g):
                br, p = PAIRS[g]
                dve.wait_ge(bt_done, g + 1)
                ob = ps[:, O_BANK[g], :].rearrange("p (a d) -> p a d", d=DH)
                rv = stat[:, WK:WK + 8].rearrange("p (a o) -> p a o", o=1).to_broadcast([P, 8, DH])
                y0 = (0 if br == "moba" else 768) + P * p
                yv = y[:, :, y0:y0 + P]
                if br == "moba":
                    nc.vector.tensor_tensor(yv.rearrange("p i (m d) -> p i m d", m=2),
                                            ob.rearrange("p (i m) d -> p i m d", m=2),
                                            rv.rearrange("p (i m) d -> p i m d", m=2), ALU.mult).then_inc(bt_used, 1)
                else:
                    link(nc.vector.tensor_tensor(work[:].rearrange("p (a d) -> p a d", d=DH), ob, rv, ALU.mult))
                    nc.vector.tensor_tensor(yv, yv, work[:].rearrange("p (i d) -> p i d", i=NT), ALU.add).then_inc(bt_used, 1)

            def head_sums(g):
                br, p = PAIRS[g]
                if br == "sel":
                    return
                dve.wait_ge(y_sq_ready, g - 1)
                c = SS_MB if br == "moba" else SS_NSA
                sums = stat[:, c:c + 16].rearrange("p (i h) -> p i h", h=HEADS)[:, :, 2 * p:2 * p + 2]
                nc.vector.tensor_reduce(sums, ysq[:].rearrange("p (i m d) -> p i m d", i=NT, m=2), AX.X, ALU.add
                                        ).then_inc(y_ss, 1)

            def y_low(k):
                c = K_ORDER[k]
                dve.wait_ge(yh_ready, k + 1)
                nc.vector.scalar_tensor_tensor(xT_l[:, c, :], ps[:, YT_BANK[k], :], cols[:, 20 + c:21 + c],
                                               xT_h[:, c, :].bitcast(F32), ALU.mult, ALU.subtract).then_inc(yl_ready, 1)

            for u in range(NU):
                g, i = divmod(u, NT)
                if u + 1 < NU:
                    row_max(2 * u + 3)
                if u + 2 < NU:
                    row_max(2 * u + 4)
                copy_t(u)
                if u in (2, 3):
                    cmp_gated(u - 2)
                if g and i == 3:
                    attn_out(g - 1)
                if g and i == 1:
                    coefficients(g - 1)
                if g >= 2 and i == 1:
                    head_sums(g - 2)
                if u == 3:
                    dve.wait_ge(ml_ss, 16)
                    rsqrt(SS_ML, R_ML, 16, DV).then_inc(ml_rn, 1)
                    dve.wait_ge(ml_rn, 1)
                if g == N_NSA + 1 and i == 2:
                    dve.wait_ge(y_ss, 2)
                    rsqrt(SS_NSA, R_NSA, 16, DH).then_inc(nsa_rn, 1)
                    dve.wait_ge(nsa_rn, 1)
            last_pair = len(PAIRS) - 1
            y_low(0)
            y_low(1)
            coefficients(last_pair)
            head_sums(last_pair - 1)
            y_low(2)
            attn_out(last_pair)
            y_low(3)
            head_sums(last_pair)
            dve.wait_ge(y_ss, 4)
            link(rsqrt(SS_MB, R_MB, 16, DH))
            ym = y[:, :, 0:256].rearrange("p t (h d) -> p t h d", h=HEADS)
            nc.vector.tensor_tensor(ym, ym, stat[:, R_MB:R_MB + 16].rearrange("p (t h o) -> p t h o", h=HEADS, o=1)
                                    .to_broadcast([P, NT, HEADS, DH]), ALU.mult).then_inc(moba_y, 1)
            for k in range(4, 8):
                y_low(k)

            def hm_low(t):
                for b in range(2):
                    dve.wait_ge(hmh_ready, 2 * t + b + 1)
                    nc.vector.tensor_tensor(xT_l[:, 4 * b:4 * b + 4, t * P:(t + 1) * P],
                                            ps[:, WO_BANK[t] + b, :].rearrange("p (c q) -> p c q", c=4),
                                            xT_h[:, 4 * b:4 * b + 4, t * P:(t + 1) * P].bitcast(F32),
                                            ALU.subtract).then_inc(hml_ready, 1)

            def base(ss, n):
                c = BASE + 2 * n
                link(nc.vector.tensor_scalar(stat[:, c:c + 1], stat[:, ss:ss + 1], 1.0 / D, EPS, ALU.mult, ALU.add))
                nc.vector.tensor_scalar(stat[:, c + 1:c + 2], stat[:, c:c + 1], -0.5, None, ALU.mult).then_inc(base_ready, 1)

            for t in range(NT):
                if t == 0:
                    dve.wait_ge(gain1_in, 16)
                    dve.wait_ge(gain2_in, 16)
                if t >= 2:
                    dve.wait_ge(hmt_done, 2 * t - 2)
                for half in range(2):
                    dve.wait_ge(o_sq, 2 * t + half + 1)
                    if half == 0:
                        base(SS_Y + 2 * t, 2 * t)
                    h = slice(512 * half, 512 * half + 512)
                    link(nc.vector.tensor_tensor(ow[:, t % 2, h], ps[:, WO_BANK[t] + half, :], gain_a[:, h], ALU.mult))
                dve.wait_ge(base_ready, 2 * t + 1)
                c = BASE + 4 * t + 1
                link(rsqrt1(SS_Y + 2 * t + 1, R_O + t, ROOT + t, NT + 2 * t + 1, stat[:, c:c + 1]))
                for half in range(2):
                    h = slice(512 * half, 512 * half + 512)
                    nc.vector.scalar_tensor_tensor(xres[:, t, h], ow[:, t % 2, h], stat[:, R_O + t:R_O + t + 1], xres[:, t, h],
                                                   ALU.mult, ALU.add).then_inc(x1_ready, 1)
                if t == NT - 2:
                    chunk_low(C_MLP)
                dve.wait_ge(x1_sq, 2 * t + 1)
                base(SS_O + 2 * t, 2 * t + 1)
                dve.wait_ge(base_ready, 2 * t + 2)
                c = BASE + 4 * t + 3
                link(rsqrt1(SS_O + 2 * t + 1, R_X1 + t, ROOT + NT + t, NT + 2 * t + 2, stat[:, c:c + 1]))
                dve.wait_ge(x1_ready, 2 * t + 2)
                for half in range(2):
                    h = slice(512 * half, 512 * half + 512)
                    nc.vector.scalar_tensor_tensor(ow[:, t % 2, h], xres[:, t, h], stat[:, R_X1 + t:R_X1 + t + 1], gain_b[:, h],
                                                   ALU.mult, ALU.mult).then_inc(hm_ready, 1)
                if t >= 1:
                    hm_low(t - 1)
            hm_low(NT - 1)

            def finish(t):
                dve.wait_ge(acc_ready, 8 * (NB - 1) + 4 + t + 1)
                if t == 0:
                    dve.wait_ge(gain3_in, 16)
                if t >= 2:
                    dve.wait_ge(res_ready, 2 * t - 3)
                nc.vector.tensor_tensor(sq[:, t % 2, :], y[:, t, 512:1024], gain_a[:, 512:1024], ALU.mult).then_inc(yg_ready, 1)
                link(rsqrt1(SS_Y + 2 * t + 1, R_Y + t, ROOT + t, 3 * NT + t + 1, stat[:, SS_X1 + t:SS_X1 + t + 1]))
                dve.wait_ge(yg_ready, NT + t + 1)
                for half in (1, 0):
                    src = sq[:, t % 2, :] if half else yg[:, t, :]
                    xv = xres[:, t, 512 * half:512 * half + 512]
                    nc.vector.scalar_tensor_tensor(xv, src, stat[:, R_Y + t:R_Y + t + 1], xv, ALU.mult, ALU.add
                                                   ).then_inc(res_ready, 1)

            for b in range(NB):
                for f in range(FB):
                    n = FB * b + f
                    dve.wait_ge(relu_ready, n + 1)
                    nc.vector.tensor_tensor(sq[:, n % 2, :], relu[:, n % 2, :], relu[:, n % 2, :], ALU.mult).then_inc(sq_ready, 1)
                    dve.wait_ge(sq_ready, n + 1)
                    dve.wait_ge(hh_ready, n + 1)
                    nc.vector.tensor_tensor(hT_l[:, f, :], sq[:, n % 2, :], hT_h[:, f, :].bitcast(F32),
                                            ALU.subtract).then_inc(hl_ready, 1)
                for half in range(2):
                    banks = SETS[(b + 1 + half) % 2]
                    for t in range(NT):
                        n = 8 * b + 4 * half + t
                        dve.wait_ge(down_done, n + 1)
                        ya = y[:, t, 512 * half:512 * half + 512]
                        if b == 0:
                            nc.vector.tensor_copy(ya, ps[:, banks[t], :]).then_inc(acc_ready, 1)
                        else:
                            dve.wait_ge(acc_ready, n - 7)
                            nc.vector.tensor_tensor(ya, ps[:, banks[t], :], ya, ALU.add).then_inc(acc_ready, 1)
                        if b == NB - 1 and half:
                            finish(t)
                    if b == NB - 1 and half == 0:
                        dve.wait_ge(y_sq, NT)
                        ss0 = stat[:, SS_Y:SS_Y + 2 * NT].rearrange("p (t a) -> p t a", a=2)[:, :, 0]
                        link(nc.vector.tensor_scalar(stat[:, SS_O:SS_O + NT], ss0, 1.0 / D, EPS, ALU.mult, ALU.add))
                        link(nc.vector.tensor_scalar(stat[:, SS_X1:SS_X1 + NT], stat[:, SS_O:SS_O + NT], -0.5, None, ALU.mult))
                        nc.vector.memset(zero1[:], 0.0).then_inc(ss0_ready, 1)

        @block.tensor
        def _(pe):
            def mm3(o, sh, sl, mh, ml, start, stop):
                nc.tensor.matmul(o, sh, mh, start=start, stop=False)
                nc.tensor.matmul(o, sh, ml, start=False, stop=False)
                return nc.tensor.matmul(o, sl, mh, start=False, stop=stop)

            def bank_free(n):
                if n >= 8:
                    pe.wait_ge(*reads(n - 8))

            def chunk(c):
                pe.wait_ge(lo_done, c + 1)
                if c in SHARED:
                    pe.wait_ge(lo_first, SHARED.index(c) + 1)
                r = ring_slot(c)
                return grid(ring_h[r], c), grid(ring_l[r], c)

            def x_transposes(t):
                pe.wait_ge(hn_ready, t + 1)
                for c in range(NC):
                    last = nc.tensor.transpose(ps[:, 2 * t + c // 4, (c % 4) * P:(c % 4) * P + P], y[:, t, c * P:(c + 1) * P], ident[:])
                last.then_inc(xt_done, 1)

            def first_group():
                pe.wait_ge(consts, 2)
                x_transposes(0)
                for t in range(NT):
                    pe.wait_ge(xl_ready, 2 * t + 2)
                    for q in range(2):
                        wh, wl = chunk(C_B + q)
                        for k in range(4):
                            kk = 4 * q + k
                            last = mm3(ps[:, (J_B + t) % 8, 0:BN], xT_h[:, kk, t * P:(t + 1) * P], xT_l[:, kk, t * P:(t + 1) * P],
                                       wh[:, k, :], wl[:, k, :], kk == 0, kk == NC - 1)
                        if q == 1:
                            last.then_inc(job_done, 1)
                        elif t == NT - 1:
                            last.then_inc(part_used, 1)
                        if q == 0 and t < NT - 1:
                            x_transposes(t + 1)

            def token_group(j0, c0, n):
                for q in range(2):
                    wh, wl = chunk(c0 + q)
                    for t in range(NT):
                        if q == 0:
                            bank_free(j0 + t)
                        for k in range(4):
                            kk = 4 * q + k
                            last = mm3(ps[:, (j0 + t) % 8, 0:n], xT_h[:, kk, t * P:(t + 1) * P], xT_l[:, kk, t * P:(t + 1) * P],
                                       wh[:, k, :], wl[:, k, :], kk == 0, kk == NC - 1)
                        if q == 1:
                            last.then_inc(job_done, 1)
                        elif t == NT - 1:
                            last.then_inc(part_used, 1)

            def feature_group(j0, c):
                wh, wl = chunk(c)
                for j in range(2):
                    bank_free(j0 + j)
                    if j0 + j == PARAM_BANK:
                        pe.wait_ge(params_ready, 2)
                    for k in range(NC):
                        last = mm3(ps[:, (j0 + j) % 8, :], wh[:, k, j * P:(j + 1) * P], wl[:, k, j * P:(j + 1) * P],
                                   xT_h[:, k, :], xT_l[:, k, :], k == 0, k == NC - 1)
                    last.then_inc(job_done, 1)

            first_group()
            pe.wait_ge(consts, 13)
            pe.wait_ge(small_in, 16 * 8)
            nc.tensor.transpose(ps[:, PARAM_BANK, 0:28], rows[:], ident[0:28, 0:28])
            nc.tensor.transpose(ps[:, PARAM_BANK, 64:96], pe_rows[:], ident[0:32, 0:32]).then_inc(params_t, 1)
            feature_group(J_CONV, C_LQ)
            feature_group(J_CONV + 2, C_LK)
            token_group(J_LO, C_LO, 512)
            pe.wait_ge(read_v, J_B + NT)
            for job, b0 in ((J_LI, BI), (J_LF, BF)):
                bank_free(job)
                for t in range(NT):
                    last = nc.tensor.transpose(ps[0:HEADS, job % 8, t * P:(t + 1) * P], zB[:, t, b0:b0 + HEADS], ident[:])
                last.then_inc(job_done, 1)
            feature_group(J_KV, C_KVS)
            feature_group(J_NQ, C_NQ)
            bank_free(J_GC)
            pe.wait_ge(read_v, reads(J_LF)[1])
            for k, r in enumerate((1, 0)):
                for t in range(NT):
                    c = 16 * k + HEADS * t
                    last = nc.tensor.transpose(ps[:, J_GC % 8, c:c + HEADS], g_row[:, r, t * P:(t + 1) * P], ident[0:HEADS, 0:HEADS])
            last.then_inc(job_done, 1)
            token_group(J_LV, C_LV, 512)
            feature_group(J_MQ, C_MQ)
            feature_group(J_MK, C_MK)
            for h in range(HEADS):
                bank_free(J_MB + h)
                if h == 0:
                    pe.wait_ge(m_ready, 2)
                nc.tensor.matmul(ps[:, (J_MB + h) % 8, :], sel[:, h, :], m_split[:, 0, :], start=True, stop=False)
                nc.tensor.matmul(ps[:, (J_MB + h) % 8, :], sel[:, h, :], m_split[:, 1, :], start=False, stop=True).then_inc(job_done, 1)
            bank_free(J_H)
            for q in range(4):
                wh, wl = chunk(C_CMP + q)
                for k in range(8):
                    l = 8 * q + k
                    bh, bl = blk_h[:, l].rearrange("p j n -> p (j n)"), blk_l[:, l].rearrange("p j n -> p (j n)")
                    last = mm3(ps[0:2 * NP_, J_H % 8, 0:CMP_HID], bh, bl, wh[:, k, :], wl[:, k, :], l == 0, l == CMP_LEN - 1)
                last.then_inc(job_done if q == 3 else part_used, 1)
            def ml_scores(u):
                p, i = ML_UNITS[u]
                if u >= 2:
                    pe.wait_ge(ml_p, 2 * u - 2)
                for j in range(i + 1):
                    for m in range(2):
                        r = slice(DH * m, DH * m + DH)
                        last = nc.tensor.matmul(ps[:, ML_BANK[u % 2] + m, j * P:(j + 1) * P], qkT[r, 2 + p, j * P:(j + 1) * P],
                                                qkT[r, p, i * P:(i + 1) * P], start=True, stop=True)
                last.then_inc(ml_s, 1)

            def ml_values(u):
                p, i = ML_UNITS[u]
                pe.wait_ge(ml_p, 2 * u + 2)
                if u == 1:
                    pe.wait_ge(*reads(J_MB + HEADS - 1))
                if u >= 2:
                    pe.wait_ge(ml_used, u - 1)
                for m in range(2):
                    for j in range(i + 1):
                        last = nc.tensor.matmul(ps[:, 7 - u % 2, 256 * m:256 * m + DV + 1],
                                                probsT[:, (2 * u + m) % 3, j * P:(j + 1) * P],
                                                lv1[:, j, 2 * p + m, :], start=(j == 0), stop=(j == i))
                last.then_inc(ml_o, 1)

            def score(s):
                u, m = divmod(s, 2)
                g, i = divmod(u, NT)
                br, p = PAIRS[g]
                if s >= 5:
                    pe.wait_ge(p_ready, s - 4)
                w = (i + 1) * P
                n = max(w, 2 * P)
                if br == "moba" and i == 0 and m == 0:
                    pe.wait_ge(mk_in[p], 32)
                    pe.wait_ge(mk_lo_ready, 2 * p + 2)
                    pe.wait_ge(mq_in[p], 32)
                r, bank = half_rows(m), S_BANK[s % 5]
                if br == "moba":
                    q, kh, kl = mq_st[:, 2 * p + m], mk_st[p][:, m], mk_lo[r, p]
                else:
                    b = ("sel", "win").index(br)
                    q, kh, kl = nq_st[:, 2 * p + m], nk_st[:, b], nk_lo[r, b]
                nc.tensor.matmul(ps[:, bank, 0:n], q[:, i * P:(i + 1) * P], kh[:, 0:n], start=True, stop=False)
                nc.tensor.matmul(ps[:, bank, 0:n], q[r, i * P:(i + 1) * P], kl[:, 0:n], start=False, stop=True)
                nc.tensor.matmul(ps[:, bank, w - P:w], identb[:], mask_s[:], start=False,
                                 stop=True, skip_group_check=True).then_inc(s_done, 1)

            pe.wait_ge(silu_done, 4)
            pe.wait_ge(*reads(J_MK + 1))
            pe.wait_ge(*reads(J_MB))
            ml_scores(0)
            pe.wait_ge(*reads(J_MB + 1))
            pe.wait_ge(read_v, reads(J_H)[1])
            for t in range(2):
                last = nc.tensor.transpose(ps[:, HT_BANK, 2 * NP_ * t:2 * NP_ * (t + 1)],
                                           hsb[:, t * P:(t + 1) * P], ident[0:2 * NP_, 0:2 * NP_])
            last.then_inc(job_done, 1)

            for u in range(len(ML_UNITS)):
                if u + 1 < len(ML_UNITS):
                    ml_scores(u + 1)
                if u == 3:
                    pe.wait_ge(gelu_ready, 1)
                    for t in range(2):
                        last = nc.tensor.matmul(ps[:, 4, 0:NP_], w2k[:, t].rearrange("p s d -> p (s d)"), gel[:, t, 0:NP_],
                                                start=(t == 0), stop=(t == 1))
                    last.then_inc(kv_cmp, 1)
                    for t in range(2):
                        last = nc.tensor.matmul(ps[:, 5, 0:DH], gelr[:, t].rearrange("p h n -> p (h n)"), w2v[:, t, :],
                                                start=(t == 0), stop=(t == 1))
                    last.then_inc(kv_cmp, 1)
                ml_values(u)
                if u == 4:
                    pe.wait_ge(kc_ready, 1)
                    pe.wait_ge(vc_ready, 1)
                    for m in range(2):
                        nc.tensor.matmul(ps[:, 4 + m, 0:8 * NP_], identb[:], mask_c[:].rearrange("p i a n -> p (i a n)"),
                                         start=True, stop=True)
                    for i in range(NT):
                        for p in range(2):
                            for m in range(2):
                                r = slice(DH * m, DH * m + DH)
                                c = (2 * i + p) * NP_
                                last = nc.tensor.matmul(ps[:, 4 + m, c:c + NP_], nqT[r, p, i * P:(i + 1) * P], kcT[r, :],
                                                        start=False, stop=True, skip_group_check=True)
                    last.then_inc(cs_done, 1)
                if u == 6:
                    pe.wait_ge(nk_lo_ready, 2)
                    pe.wait_ge(nq_in, 16 * HEADS)
                    pe.wait_ge(ml_p, 14)
                    score(0)
                    score(1)
                if u == 7:
                    score(2)
                    score(3)

            def cmp_transposes():
                pe.wait_ge(cs_ready, 1)
                for i in range(NT):
                    last = nc.tensor.transpose(ps[:, 6, i * P:(i + 1) * P], cexp[:, i].rearrange("p a n -> p (a n)"), ident[:])
                last.then_inc(ct_done, 1)

            def cmp_out(half):
                pe.wait_ge(ct_ready, 1)
                if half:
                    pe.wait_ge(co_used, 1)
                for i in (2 * half, 2 * half + 1):
                    last = nc.tensor.matmul(ps[:, 6, 256 * (i % 2):256 * (i % 2) + 256], cexpT[:, i, :], vbd[:],
                                            start=True, stop=True)
                last.then_inc(co_done, 1)

            def transposes(s):
                u, m = divmod(s, 2)
                pe.wait_ge(p_ready, s + 1)
                if u >= 1:
                    pe.wait_ge(pt_a if m else pt_v, u)
                for j in range(u % NT + 1):
                    last = nc.tensor.transpose(ps[:, 4 + m, j * P:(j + 1) * P], probs[:, s % 3, j * P:(j + 1) * P], ident[:])
                last.then_inc(t_done, 1)

            def values(g, members=(0, 1)):
                br, p = PAIRS[g]
                if g == 0 and 0 in members:
                    pe.wait_ge(co_used, 2)
                if g and 0 in members and O_BANK[g] == O_BANK[g - 1]:
                    pe.wait_ge(bt_used, g)
                for m in members:
                    pe.wait_ge(pt_a if m else pt_v, NT * (g + 1))
                    v0 = {"sel": BS, "win": BW, "moba": BV + DH * (2 * p + m)}[br]
                    for j in range(NT):
                        last = nc.tensor.matmul(ps[DH * m:DH * m + DH, O_BANK[g], j * P:SEQ], zB[:, j, v0:v0 + DH],
                                                block_of(pT[:, g % 2], m, slice(j, NT), j), start=(j == 0), stop=True,
                                                skip_group_check=(j > 0))
                if 1 in members:
                    last.then_inc(o_done, 1)

            def back(g):
                pe.wait_ge(ot_ready, g + 1)
                for i in range(NT):
                    last = nc.tensor.transpose(ps[:, O_BANK[g], i * P:(i + 1) * P], oT[:, i * P:(i + 1) * P], ident[:])
                last.then_inc(bt_done, 1)

            def y_transposes(k):
                c = K_ORDER[k]
                for t in range(NT):
                    last = nc.tensor.transpose(ps[:, YT_BANK[k], t * P:(t + 1) * P], y[:, t, c * P:(c + 1) * P], ident[:])
                last.then_inc(yt_done, 1)

            pe.wait_ge(cs_sub, 1)
            pe.wait_ge(ml_used, len(ML_UNITS))
            for u in range(NU):
                g, i = divmod(u, NT)
                for m in range(2):
                    s = 2 * u + m
                    if s + 4 < 2 * NU:
                        score(s + 4)
                    if m == 0 and g and i == 3:
                        back(g - 1)
                    if m == 0 and g and i in (1, 2):
                        values(g - 1, (i - 1,))
                    transposes(s)
                    if s == CT_S:
                        cmp_transposes()
                    if s in CO_S:
                        cmp_out(CO_S.index(s))
                    if u == NU - 2 and m == 1:
                        pe.wait_ge(ml_y, 2)
                        y_transposes(0)
                        y_transposes(1)
            def project(t, half, k_lo, k_hi):
                for k in range(k_lo, k_hi):
                    kset, kk = divmod(k, 4)
                    wh, wl = grid(ring_h[ring_slot(C_WO + 2 * kset + half)], C_WO), grid(ring_l[ring_slot(C_WO + 2 * kset + half)], C_WO)
                    c = K_ORDER[k]
                    last = mm3(ps[:, WO_BANK[t] + half, :], xT_h[:, c, t * P:(t + 1) * P], xT_l[:, c, t * P:(t + 1) * P],
                               wh[:, kk, :], wl[:, kk, :], k == 0, k == NC - 1)
                    if t == NT - 1 and k == 3:
                        last.then_inc(part_used, 1)
                if k_hi == NC:
                    last.then_inc(wo_done, 1)

            def hm_transposes(t):
                for b in range(2):
                    pe.wait_ge(hm_ready, 2 * t + b + 1)
                    for c in range(4):
                        last = nc.tensor.transpose(ps[:, WO_BANK[t] + b, c * P:c * P + P],
                                                   ow[:, t % 2, (4 * b + c) * P:(4 * b + c + 1) * P], ident[:])
                    last.then_inc(hmt_done, 1)

            def project_all(t, k_lo, k_hi):
                for k in range(k_lo, k_hi):
                    if t == 0:
                        pe.wait_ge(yl_ready, k + 1)
                    project(t, 0, k, k + 1)
                    project(t, 1, k, k + 1)

            last_pair = len(PAIRS) - 1
            y_transposes(2)
            values(last_pair)
            pe.wait_ge(yl_ready, 2)
            y_transposes(3)
            pe.wait_ge(lo_done, C_WO + 4)
            pe.wait_ge(yl_ready, 2)
            project_all(0, 0, 1)
            back(last_pair)
            project_all(0, 1, 4)
            pe.wait_ge(nsa_y, 1)
            y_transposes(4)
            y_transposes(5)
            pe.wait_ge(bt_used, len(PAIRS))
            project_all(1, 0, 4)
            project_all(0, 4, 6)
            project_all(1, 4, 5)
            pe.wait_ge(moba_y, 1)
            y_transposes(6)
            y_transposes(7)
            project_all(1, 5, 6)
            project_all(0, 6, 8)
            project_all(1, 6, 8)
            project(2, 0, 0, NC)
            hm_transposes(0)
            project(2, 1, 0, NC)
            project(3, 0, 0, NC)
            hm_transposes(1)
            project(3, 1, 0, NC)
            hm_transposes(2)
            pe.wait_ge(hml_ready, 2 * EARLY_T)
            for f in range(EARLY_F):
                wh, wl = chunk(C_MLP + f // 2)
                if f == 3:
                    hm_transposes(NT - 1)
                for k in range(NC):
                    last = mm3(ps[:, SETS[0][f], 0:EARLY_T * P], wh[:, k, (f % 2) * P:(f % 2) * P + P], wl[:, k, (f % 2) * P:(f % 2) * P + P],
                               xT_h[:, k, 0:EARLY_T * P], xT_l[:, k, 0:EARLY_T * P], k == 0, k == NC - 1)
            pe.wait_ge(hml_ready, 2 * NT)

            for b in range(NB):
                c0 = C_MLP + PER_BLOCK * b
                for f in range(FB):
                    n = FB * b + f
                    wh, wl = chunk(c0 + f // 2)
                    if f >= 4:
                        pe.wait_ge(relu_ready, n - 3)
                    elif b >= 1:
                        pe.wait_ge(acc_ready, 8 * (b - 1) + f + 1)
                    t0 = EARLY_T * P if n < EARLY_F else 0
                    for k in range(NC):
                        last = mm3(ps[:, SETS[b % 2][f % 4], t0:SEQ], wh[:, k, (f % 2) * P:(f % 2) * P + P], wl[:, k, (f % 2) * P:(f % 2) * P + P],
                                   xT_h[:, k, t0:SEQ], xT_l[:, k, t0:SEQ], k == 0, k == NC - 1)
                    last.then_inc(up_done, 1)
                def down_tile(t, q, half, banks, wh, wl):
                    for k in range(4):
                        f = 4 * q + k
                        last = mm3(ps[:, banks[t], :], hT_h[:, f, t * P:(t + 1) * P], hT_l[:, f, t * P:(t + 1) * P],
                                   wh[:, k, :], wl[:, k, :], f == 0, f == FB - 1)
                    return last

                for half in range(2):
                    banks = SETS[(b + 1 + half) % 2]
                    if b == NB - 1 and half == 1:
                        pe.wait_ge(relu_ready, FB * b + FB)
                        both = [chunk(c0 + FB // 2 + 2 * half + q) for q in range(2)]
                        for t in range(NT):
                            for q in range(2):
                                last = down_tile(t, q, half, banks, *both[q])
                            last.then_inc(down_done, 1)
                        continue
                    for q in range(2):
                        wh, wl = chunk(c0 + FB // 2 + 2 * half + q)
                        for t in range(NT):
                            if q == 0 and half == 0 and b >= 1:
                                pe.wait_ge(acc_ready, 8 * (b - 1) + 4 + t + 1)
                            if q == 0 and half == 1:
                                pe.wait_ge(relu_ready, FB * b + FB)
                            for k in range(4):
                                f = 4 * q + k
                                if t == 0 and half == 0:
                                    pe.wait_ge(hl_ready, FB * b + f + 1)
                                last = mm3(ps[:, banks[t], :], hT_h[:, f, t * P:(t + 1) * P], hT_l[:, f, t * P:(t + 1) * P],
                                           wh[:, k, :], wl[:, k, :], f == 0, f == FB - 1)
                            if q == 1:
                                last.then_inc(down_done, 1)
                            elif t == NT - 1:
                                last.then_inc(part_used, 1)


_INS = ["x", "norm_g", "w_in", "mlstm_conv_w", "mlstm_conv_b", "mlstm_gate_b", "nsa_cmp_pe", "nsa_cmp_w1",
        "nsa_cmp_w2", "head_g", "w_out", "w_mlp1", "w_mlp2"]


def kernel(**inputs):
    import numpy as np
    import concourse.bacc as bacc
    from concourse.bass_utils import run_bass_kernel_spmd

    nc = bacc.Bacc("TRN2", target_bir_lowering=False, num_devices=1)
    arrays, args = {}, []
    for name in _INS:
        a = np.ascontiguousarray(inputs[name])
        arrays[f"in_{name}"] = a
        args.append(nc.dram_tensor(f"in_{name}", a.shape, mybir.dt.from_np(a.dtype), kind="ExternalInput").ap())
    o = nc.dram_tensor("out_0", (1, SEQ, D), F32, kind="ExternalOutput").ap()
    build(nc, *args, o)
    r = run_bass_kernel_spmd(nc, [arrays], core_ids=[0])
    return r.results[0]["out_0"]
```
